# Optimizing a Trainium2 kernel written in Bass

```python
import math
import jax, jax.numpy as jnp
from jax import lax
import numpy as np

D_MODEL = 1024
BATCH = 1
SEQ = 256
DEPTH = 1

ROPE_THETA = 10000.0
NORM_EPS = 1e-6
Q_BLOCK = 128

MLA_HEADS = 8
MLA_NOPE_DIM = 64
MLA_ROPE_DIM = 32
MLA_QK_DIM = MLA_NOPE_DIM + MLA_ROPE_DIM
MLA_V_DIM = 64
MLA_Q_LORA = 768
MLA_KV_LORA = 256
MLA_WIDTH = MLA_HEADS * MLA_V_DIM

DIFF_HEADS = 4
DIFF_HEAD_DIM = 64
DIFF_V_DIM = 2 * DIFF_HEAD_DIM
DIFF_WIDTH = DIFF_HEADS * DIFF_V_DIM

N_BRANCHES = 2
IN_WIDTH = MLA_Q_LORA + MLA_KV_LORA + MLA_ROPE_DIM + 3 * DIFF_WIDTH + N_BRANCHES * D_MODEL

N_EXPERTS = 32
TOP_K = 4
D_EXPERT = D_MODEL
SWIGLU_ALPHA = 1.702
SWIGLU_LIMIT = 7.0

kernel_name = 'hybrid_mla_diffattn_gated_moe'

def rms_norm(x, g):
    xf = x.astype(jnp.float32)
    y = xf * lax.rsqrt(jnp.mean(xf * xf, axis=-1, keepdims=True) + NORM_EPS)
    return (y * g.astype(jnp.float32)).astype(x.dtype)

def rope_tables(seq, dim):
    inv_freq = 1.0 / (ROPE_THETA ** (jnp.arange(0, dim, 2, dtype=jnp.float32) / dim))
    ang = jnp.arange(seq, dtype=jnp.float32)[:, None] * inv_freq[None, :]
    return jnp.cos(ang), jnp.sin(ang)

def apply_rope(x, cos, sin):
    xf = x.astype(jnp.float32)
    x1, x2 = jnp.split(xf, 2, axis=-1)
    c = cos[None, :, None, :]
    s = sin[None, :, None, :]
    return jnp.concatenate([x1 * c - x2 * s, x2 * c + x1 * s], axis=-1).astype(x.dtype)

def causal_block_attention(q, k, v, scale):
    b, s, h, dq = q.shape
    dv = v.shape[-1]
    nb = s // Q_BLOCK
    q_blocks = q.reshape(b, nb, Q_BLOCK, h, dq).transpose(1, 0, 2, 3, 4)
    key_pos = jnp.arange(s)

    def one_block(args):
        q_blk, blk = args
        sc = jnp.einsum('bqhd,bkhd->bhqk', q_blk, k, preferred_element_type=jnp.float32) * scale
        q_pos = blk * Q_BLOCK + jnp.arange(Q_BLOCK)
        mask = key_pos[None, :] <= q_pos[:, None]
        sc = jnp.where(mask[None, None], sc, -jnp.inf)
        p = jax.nn.softmax(sc, axis=-1)
        return jnp.einsum('bhqk,bkhd->bqhd', p.astype(v.dtype), v)

    out = lax.map(one_block, (q_blocks, jnp.arange(nb)))
    return out.transpose(1, 0, 2, 3, 4).reshape(b, s, h, dv)

def mla_branch(q_lat, kv_lat, k_pe, q_lat_norm, kv_lat_norm, w_uq, w_ukv, q_norm, k_norm, cos, sin):
    b, s, _ = q_lat.shape
    q = (rms_norm(q_lat, q_lat_norm) @ w_uq).reshape(b, s, MLA_HEADS, MLA_QK_DIM)
    kv = (rms_norm(kv_lat, kv_lat_norm) @ w_ukv).reshape(b, s, MLA_HEADS, MLA_NOPE_DIM + MLA_V_DIM)
    k_nope, v = kv[..., :MLA_NOPE_DIM], kv[..., MLA_NOPE_DIM:]
    k_pe = jnp.broadcast_to(k_pe[:, :, None, :], (b, s, MLA_HEADS, MLA_ROPE_DIM))
    k = jnp.concatenate([k_nope, k_pe], axis=-1)
    q = rms_norm(q, q_norm)
    k = rms_norm(k, k_norm)
    q = jnp.concatenate([q[..., :MLA_NOPE_DIM], apply_rope(q[..., MLA_NOPE_DIM:], cos, sin)], axis=-1)
    k = jnp.concatenate([k[..., :MLA_NOPE_DIM], apply_rope(k[..., MLA_NOPE_DIM:], cos, sin)], axis=-1)
    o = causal_block_attention(q, k, v, 1.0 / math.sqrt(MLA_QK_DIM))
    return o.reshape(b, s, MLA_WIDTH)

def diff_branch(q, k, v, q_norm, k_norm, lq1, lk1, lq2, lk2, subln, lambda_init, cos, sin):
    b, s, _ = q.shape
    q = rms_norm(q.reshape(b, s, 2 * DIFF_HEADS, DIFF_HEAD_DIM), q_norm)
    k = rms_norm(k.reshape(b, s, 2 * DIFF_HEADS, DIFF_HEAD_DIM), k_norm)
    q = apply_rope(q, cos, sin)
    k = apply_rope(k, cos, sin)
    v = jnp.repeat(v.reshape(b, s, DIFF_HEADS, DIFF_V_DIM), 2, axis=2)
    o = causal_block_attention(q, k, v, 1.0 / math.sqrt(DIFF_HEAD_DIM))
    o = o.reshape(b, s, DIFF_HEADS, 2, DIFF_V_DIM)
    lam = (jnp.exp(jnp.sum(lq1.astype(jnp.float32) * lk1.astype(jnp.float32)))
           - jnp.exp(jnp.sum(lq2.astype(jnp.float32) * lk2.astype(jnp.float32)))
           + lambda_init)
    o = o[..., 0, :] - lam.astype(o.dtype) * o[..., 1, :]
    o = rms_norm(o, subln) * (1.0 - lambda_init)
    return o.reshape(b, s, DIFF_WIDTH)

def moe_ffn(h, w_router, b_router, w1, b1, w2, b2):
    b, s, d = h.shape
    t = h.reshape(b * s, d)
    logits = (t @ w_router).astype(jnp.float32) + b_router.astype(jnp.float32)
    top_val, top_idx = lax.top_k(logits, TOP_K)
    top_w = jax.nn.softmax(top_val, axis=-1)
    gates = jnp.einsum('nk,nke->ne', top_w, jax.nn.one_hot(top_idx, N_EXPERTS, dtype=jnp.float32)).astype(h.dtype)
    out = jnp.zeros_like(t)
    for e in range(N_EXPERTS):
        u = t @ w1[e] + b1[e]
        glu = jnp.minimum(u[:, :D_EXPERT], SWIGLU_LIMIT)
        lin = jnp.clip(u[:, D_EXPERT:], -SWIGLU_LIMIT, SWIGLU_LIMIT)
        a = glu * jax.nn.sigmoid(SWIGLU_ALPHA * glu) * (lin + 1.0)
        out = out + gates[:, e:e + 1] * (a @ w2[e] + b2[e])
    return out.reshape(b, s, d)

def setup_inputs(seed: int = 0) -> dict:
    key = jax.random.key(seed)
    ks = jax.random.split(key, 32)
    f32 = jnp.float32

    def w(k, shape, fan_in):
        return jax.random.normal(k, shape, f32) * (fan_in ** -0.5)

    def gain(k, shape):
        return 1.0 + 0.01 * jax.random.normal(k, shape, f32)

    L = DEPTH
    return {
        'x': jax.random.normal(ks[0], (BATCH, SEQ, D_MODEL), f32),
        'attn_norm': gain(ks[1], (L, D_MODEL)),
        'w_in': w(ks[2], (L, D_MODEL, IN_WIDTH), D_MODEL),
        'mla_q_lat_norm': gain(ks[3], (L, MLA_Q_LORA)),
        'mla_kv_lat_norm': gain(ks[4], (L, MLA_KV_LORA)),
        'mla_w_uq': w(ks[5], (L, MLA_Q_LORA, MLA_HEADS * MLA_QK_DIM), MLA_Q_LORA),
        'mla_w_ukv': w(ks[6], (L, MLA_KV_LORA, MLA_HEADS * (MLA_NOPE_DIM + MLA_V_DIM)), MLA_KV_LORA),
        'mla_q_norm': gain(ks[7], (L, MLA_QK_DIM)),
        'mla_k_norm': gain(ks[8], (L, MLA_QK_DIM)),
        'diff_q_norm': gain(ks[9], (L, DIFF_HEAD_DIM)),
        'diff_k_norm': gain(ks[10], (L, DIFF_HEAD_DIM)),
        'diff_lambda_q1': 0.1 * jax.random.normal(ks[11], (L, DIFF_HEAD_DIM), f32),
        'diff_lambda_k1': 0.1 * jax.random.normal(ks[12], (L, DIFF_HEAD_DIM), f32),
        'diff_lambda_q2': 0.1 * jax.random.normal(ks[13], (L, DIFF_HEAD_DIM), f32),
        'diff_lambda_k2': 0.1 * jax.random.normal(ks[14], (L, DIFF_HEAD_DIM), f32),
        'diff_subln': gain(ks[15], (L, DIFF_V_DIM)),
        'w_branch_mla': w(ks[16], (L, MLA_WIDTH, D_MODEL), MLA_WIDTH),
        'w_branch_diff': w(ks[17], (L, DIFF_WIDTH, D_MODEL), DIFF_WIDTH),
        'w_out': w(ks[18], (L, D_MODEL, D_MODEL), D_MODEL),
        'ffn_norm': gain(ks[19], (L, D_MODEL)),
        'w_router': w(ks[20], (L, D_MODEL, N_EXPERTS), D_MODEL),
        'b_router': 0.01 * jax.random.normal(ks[21], (L, N_EXPERTS), f32),
        'w_mlp1': w(ks[22], (L, N_EXPERTS, D_MODEL, 2 * D_EXPERT), D_MODEL),
        'b_mlp1': 0.01 * jax.random.normal(ks[23], (L, N_EXPERTS, 2 * D_EXPERT), f32),
        'w_mlp2': w(ks[24], (L, N_EXPERTS, D_EXPERT, D_MODEL), D_EXPERT),
        'b_mlp2': 0.01 * jax.random.normal(ks[25], (L, N_EXPERTS, D_MODEL), f32),
    }

def reference(x, attn_norm, w_in, mla_q_lat_norm, mla_kv_lat_norm, mla_w_uq, mla_w_ukv,
              mla_q_norm, mla_k_norm, diff_q_norm, diff_k_norm, diff_lambda_q1, diff_lambda_k1,
              diff_lambda_q2, diff_lambda_k2, diff_subln, w_branch_mla, w_branch_diff, w_out,
              ffn_norm, w_router, b_router, w_mlp1, b_mlp1, w_mlp2, b_mlp2):
    s = x.shape[1]
    cos_mla, sin_mla = rope_tables(s, MLA_ROPE_DIM)
    cos_diff, sin_diff = rope_tables(s, DIFF_HEAD_DIM)
    split_points = list(np.cumsum([MLA_Q_LORA, MLA_KV_LORA, MLA_ROPE_DIM,
                                   DIFF_WIDTH, DIFF_WIDTH, DIFF_WIDTH, D_MODEL]))
    h = x
    for i in range(DEPTH):
        lambda_init = 0.8 - 0.6 * math.exp(-0.3 * i)
        xn = rms_norm(h, attn_norm[i])
        proj = xn @ w_in[i]
        q_lat, kv_lat, k_pe, dq, dk, dv, gate_a, gate_b = jnp.split(proj, split_points, axis=-1)
        o_a = mla_branch(q_lat, kv_lat, k_pe, mla_q_lat_norm[i], mla_kv_lat_norm[i], mla_w_uq[i],
                         mla_w_ukv[i], mla_q_norm[i], mla_k_norm[i], cos_mla, sin_mla)
        o_b = diff_branch(dq, dk, dv, diff_q_norm[i], diff_k_norm[i], diff_lambda_q1[i], diff_lambda_k1[i],
                          diff_lambda_q2[i], diff_lambda_k2[i], diff_subln[i], lambda_init, cos_diff, sin_diff)
        merged = (jax.nn.sigmoid(gate_a) * (o_a @ w_branch_mla[i])
                  + jax.nn.sigmoid(gate_b) * (o_b @ w_branch_diff[i]))
        h = h + merged @ w_out[i]
        h = h + moe_ffn(rms_norm(h, ffn_norm[i]), w_router[i], b_router[i],
                        w_mlp1[i], b_mlp1[i], w_mlp2[i], b_mlp2[i])
    return h


_drawn_inputs = setup_inputs


def setup_inputs(seed=0):
    import zlib

    import numpy as np

    out = dict(_drawn_inputs(seed))
    spreads = {}
    factors = {'mla_q_lat_norm': 8.0,
     'mla_kv_lat_norm': 4.33,
     'mla_q_norm': 8.0,
     'mla_k_norm': 3.612,
     'b_mlp1': 23.136,
     'b_mlp2': 79.861,
     'diff_q_norm': 8.0,
     'diff_k_norm': 8.0,
     'diff_lambda_k1': 3.49,
     'diff_lambda_q2': 3.69,
     'diff_lambda_k2': 5.262,
     'diff_subln': 8.0,
     'ffn_norm': 4.896,
     'b_router': 8.0}
    for name, (base, spread) in spreads.items():
        noise = np.random.default_rng([zlib.crc32(name.encode()), seed]).standard_normal(out[name].shape)
        drawn = base * np.exp(spread * noise) if base else spread * noise
        out[name] = __import__('jax').numpy.asarray(drawn.astype(out[name].dtype))
    for name, factor in factors.items():
        out[name] = (out[name] * factor).astype(out[name].dtype)
    return out
```

```python
import math
from contextlib import ExitStack

import numpy as np

import concourse.bass as bass
from concourse import mybir

F32 = mybir.dt.float32
I32 = mybir.dt.int32
ALU = mybir.AluOpType
ACT = mybir.ActivationFunctionType
AX = mybir.AxisListType

P = 128
SEQ, D = 256, 1024
NM = SEQ // P
KD = D // P
EPS = 1e-6

HA, NOPE, ROPE_A, VA = 8, 64, 32, 64
QK_A = NOPE + ROPE_A
Q_LORA, KV_LORA = 768, 256
KQ, KKV = Q_LORA // P, KV_LORA // P
HD, DD = 4, 64
SUB, DV = 2 * HD, 2 * DD
WA, WD = HA * VA, HD * DV
LAMBDA_INIT = 0.8 - 0.6 * math.exp(-0.3 * 0)

E, TOP_K, F = 32, 4, D
ALPHA, LIMIT = 1.702, 7.0
SLOTS = 64
ROUNDS = SEQ // SLOTS
PAIRS = E // 2
JOBS = ROUNDS * PAIRS
COLS = ROUNDS * E + 2

O_Q, O_KV = 0, Q_LORA
O_DQ = Q_LORA + KV_LORA + ROPE_A
O_DK, O_DV, O_GATE = O_DQ + WD, O_DQ + 2 * WD, O_DQ + 3 * WD
KVW = KV_LORA + ROPE_A
HALF = 512

RING, SLOT = 12, 2048
JOB_CHUNKS = 3 * KD
BIG = 1e30
SENTINEL = 3e38


def head_chunks():
    out = []
    for c0, n in ((O_Q, Q_LORA // 2), (O_Q + Q_LORA // 2, Q_LORA // 2), (O_KV, KVW), (O_DQ, WD), (O_DK, WD)):
        out += [("w_in", k, KD // 2, c0, n) for k in (0, KD // 2)]
    out += [("w_uq", k, 2, 0, HA * QK_A) for k in range(0, KQ, 2)]
    out += [("w_ukv", 0, KKV, 0, HA * (NOPE + VA))]
    out += [("w_in", k, KD // 2, O_DV, WD) for k in (0, KD // 2)]
    for g in range(2 * D // HALF):
        out += [("w_in", k, KD // 2, O_GATE + g * HALF, HALF) for k in (0, KD // 2)]
    out += [("w_bd", 0, WD // P, h * HALF, HALF) for h in range(2)]
    out += [("w_ba", 0, WA // P, h * HALF, HALF) for h in range(2)]
    out += [("w_out", k, KD // 2, h * HALF, HALF) for h in range(2) for k in (0, KD // 2)]
    return out


HEAD = head_chunks()
NHEAD = len(HEAD)


def chunk_index(matrix, k, c0):
    return next(n for n, (w, k0, nk, c, _) in enumerate(HEAD) if (w, c) == (matrix, c0) and k0 <= k < k0 + nk)


def build(nc, x, attn_norm, w_in, q_lat_norm, kv_lat_norm, w_uq, w_ukv, q_norm, k_norm, dq_norm, dk_norm,
          lq1, lk1, lq2, lk2, subln, w_bmla, w_bdiff, w_out, ffn_norm, w_router, b_router,
          w1, b1, w2, b2, rope, out):
    ctx = ExitStack()
    with ctx:
        def sb(name, cols, dt=F32, parts=P):
            return ctx.enter_context(nc.sbuf_tensor(name, [parts, cols], dt))

        sems = {}

        def sem(name):
            if name not in sems:
                sems[name] = ctx.enter_context(nc.semaphore(name))
            return sems[name]

        ring = sb("ring", RING * SLOT)
        acc_r = sb("acc_r", NM * D)
        tok_r = sb("tok_r", NM * D)
        feat_r = sb("feat_r", KD * SEQ)
        gate_r = sb("gate_r", NM * 2 * D)
        qlat_r = sb("qlat_r", NM * Q_LORA)
        kvlat_r = sb("kvlat_r", NM * KVW)
        qkd_r = sb("qkd_r", NM * 2 * WD)
        qka_r = sb("qka_r", NM * 2 * HA * QK_A)
        dv_r = sb("dv_r", NM * WD)
        va_r = sb("va_r", NM * WA)
        latT_r = sb("latT_r", (KQ + KKV) * SEQ)
        qkT_r = sb("qkT_r", 2 * HA * SEQ)
        soft_r = sb("soft_r", 6 * 384)

        v3 = lambda t, a: t.rearrange("p (a b) -> p a b", a=a)
        acc = v3(acc_r[:], NM)
        xn = v3(tok_r[:], NM)
        xnT = v3(feat_r[:], KD)
        gates = v3(gate_r[:], NM)
        g_attn, g_qlat, g_kvlat = gate_r[:, 0:D], gate_r[:, D:D + Q_LORA], gate_r[:, D + Q_LORA:D + Q_LORA + KV_LORA]
        qlat, kvlat = v3(qlat_r[:], NM), v3(kvlat_r[:], NM)
        o_a = qlat_r[:, 0:NM * WA].rearrange("p (m h d) -> p m h d", m=NM, h=HA)
        qkd = qkd_r[:].rearrange("p (m h d) -> p m h d", m=NM, h=2 * SUB)
        qka = qka_r[:].rearrange("p (m h d) -> p m h d", m=NM, h=2 * HA)
        dv, va = v3(dv_r[:], NM), va_r[:].rearrange("p (m h d) -> p m h d", m=NM, h=HA)
        latT = v3(latT_r[:], KQ + KKV)
        o_raw = latT_r[:].rearrange("p (m h d) -> p m h d", m=NM, h=SUB)
        dqkT = v3(tok_r[:], SUB)
        qkaT = v3(qkT_r[:], 2 * HA)
        squares = qkT_r[:, 0:2 * HA * QK_A]
        o_b = qkd_r[:, 0:NM * WD].rearrange("p (m h d) -> p m h d", m=NM, h=HD)
        g_ffn = qkd_r[:, NM * WD:NM * WD + D]
        o_bT, o_aT = v3(qka_r[:, 0:HD * SEQ], HD), v3(qka_r[:, HD * SEQ:2 * HD * SEQ], HD)
        merged, mergedT = xn, xnT
        t_sb, tT = xn, xnT
        soft = v3(soft_r[:], 6)
        scored, probs, probsT = soft[:, 0:2], soft[:, 2:4], soft[:, 4:6]
        b1_sb, b2_sb = qkT_r[0:E, 0:2 * F], qkT_r[0:E, 2 * F:2 * F + D]
        hot_0 = 3 * D
        onehot = qkT_r[:, hot_0:hot_0 + NM * P].rearrange("p (m e s) -> p m e s", m=NM, e=2)
        gated = qkT_r[:, hot_0 + NM * P:hot_0 + 2 * NM * P].rearrange("p (m e s) -> p m e s", m=NM, e=2)
        gatedT = qkT_r[:, hot_0 + 2 * NM * P:hot_0 + 3 * NM * P]
        pick = qkT_r[0:E, hot_0 + 3 * NM * P:hot_0 + 3 * NM * P + P].rearrange("p (e s) -> p e s", e=2)
        xT = v3(feat_r[:, 0:KD * P], KD)
        glu, sig, lin, act_out = (v3(gate_r[:, i * D:(i + 1) * D], 2) for i in range(4))
        aT = [v3(soft_r[:, i * HALF:(i + 1) * HALF], 4) for i in range(2)]
        y_sb = soft_r[:, D:2 * D]

        w_rt = sb("w_rt", KD * E)
        tab = sb("tab", NM * (ROPE_A + DD))
        g_qka, g_qkd = sb("g_qka", 2 * QK_A), sb("g_qkd", 2 * DD)
        g_sub, lam_in = sb("g_sub", DV), sb("lam_in", 4 * DD)
        b_rt = sb("b_rt", E)
        ident, before, ones = sb("ident", P), sb("before", P), sb("ones", P)
        mask = sb("mask", 3 * P)
        iota = sb("iota", SLOTS)
        eye32 = sb("eye32", COLS, parts=E)
        place, weight = sb("place", NM * COLS), sb("weight", NM * COLS)
        place_v, weight_v = v3(place[:], NM), v3(weight[:], NM)
        eps = sb("eps", 1)
        ssq = sb("ssq", 64)
        rstd = sb("rstd", 64)
        nmax, sums, rsum = (sb(n, 2 * (SUB + HA)) for n in ("nmax", "sums", "rsum"))
        lam = sb("lam", 8)
        logit = sb("logit", NM * (E + 8))
        logit_v = v3(logit[:], NM)
        marked = sb("marked", NM * (E + 8))
        marked_v = v3(marked[:], NM)
        top = sb("top", NM * 8)
        chosen, expd = sb("chosen", NM * E), sb("expd", NM * E)
        chosen_v, expd_v = v3(chosen[:], NM), v3(expd[:], NM)
        negtop, gsum, grec = sb("negtop", NM), sb("gsum", NM), sb("grec", NM)
        weightT = sb("weightT", SEQ, parts=E)
        fullest = sb("fullest", 2)
        fullest_i = sb("fullest_i", 1, I32)
        scratch_m = sb("scratch_m", 4 * DD)

        bank = [ctx.enter_context(nc.psum_tensor(f"bank{i}", [P, HALF], F32)) for i in range(8)]

        matrices = {"w_in": w_in, "w_uq": w_uq, "w_ukv": w_ukv, "w_bd": w_bdiff, "w_ba": w_bmla, "w_out": w_out}
        landed = [sem(f"landed{s}") for s in range(RING)]
        ring_used = sem("ring_used")

        def slot(n, cols=SLOT):
            s = n % RING
            return ring[:, s * SLOT:s * SLOT + cols]

        def head_view(n):
            _, _, nk, _, cols = HEAD[n]
            return v3(slot(n, nk * cols), nk)

        def gain(ap, n):
            return ap.rearrange("(a n) -> a n", a=1).broadcast_to([P, n])

        block = ctx.enter_context(nc.Block())

        @block.sync
        def _(sp):
            for m in range(NM):
                sp.dma_start(acc[:, m], x[m * P:(m + 1) * P, :]).then_inc(sem(f"x_landed{m}"), 16)
            for n, (name, k0, nk, c0, cols) in enumerate(HEAD):
                if n >= RING:
                    sp.wait_ge(ring_used, n - RING + 1)
                src = matrices[name].rearrange("(k p) n -> p k n", p=P)
                for a in range(2):
                    ks = slice(a * nk // 2, (a + 1) * nk // 2)
                    sp.dma_start(head_view(n)[:, ks, :], src[:, k0 + ks.start:k0 + ks.stop, c0:c0 + cols])\
                      .then_inc(landed[n % RING], 16)

            w1_v = w1.rearrange("e (k p) (g h n) -> e k p h g n", p=P, g=2, h=2)
            w2_v = w2.rearrange("e (k p) n -> e k p n", p=P)

            def load_pair(j, pair):
                for c in range(JOB_CHUNKS):
                    n = NHEAD + c
                    sp.wait_ge(ring_used, JOB_CHUNKS * j + n - RING + 1)
                    for a in range(2):
                        if c < 2 * KD:
                            src = w1_v[2 * pair + a, c % KD, :, c // KD]
                            dst = slot(n).rearrange("p (e g n) -> p e g n", e=2, g=2)[:, a]
                        else:
                            src = w2_v[2 * pair + a, c - 2 * KD]
                            dst = slot(n).rearrange("p (e n) -> p e n", e=2)[:, a]
                        sp.dma_start(dst, src).then_inc(landed[n % RING], 16)

            with sp.Fori(0, PAIRS) as j:
                load_pair(j, j)
            sp.wait_ge(sem("counted"), 1)
            most = sp.value_load(fullest_i[0:1, 0:1], min_val=0, max_val=SEQ)
            with sp.Fori(1, ROUNDS) as r:
                with sp.If(most > r * SLOTS):
                    with sp.Fori(0, PAIRS) as p_:
                        load_pair(r * PAIRS + p_, p_)
            sp.wait_ge(sem("finished"), 1)
            for m in range(NM):
                sp.dma_start(out[m * P:(m + 1) * P, :], acc[:, m]).then_inc(sem("stored"), 16)
            sp.wait_ge(sem("stored"), 16 * NM)

        @block.gpsimd
        def _(pool):
            pool.memset(ident[:], 0.0).then_inc(sem("const_set"), 1)
            pool.memset(before[:], 1.0).then_inc(sem("const_set"), 1)
            pool.memset(ones[:], 1.0).then_inc(sem("const_set"), 1)
            pool.memset(mask[:], 0.0).then_inc(sem("const_set"), 1)
            pool.memset(eye32[:], 0.0).then_inc(sem("const_set"), 1)
            pool.memset(eps[:], EPS).then_inc(sem("const_set"), 1)
            pool.memset(weight[:], 0.0).then_inc(sem("const_set"), 1)
            pool.wait_ge(sem("const_set"), 7)
            pool.affine_select(out=ident[:], in_=ident[:], compare_op=ALU.not_equal, fill=1.0, base=0,
                               pattern=[[-1, P]], channel_multiplier=1).then_inc(sem("ident_ready"), 1)
            for c in (0, 2 * P):
                pool.affine_select(out=mask[:, c:c + P], in_=mask[:, c:c + P], compare_op=ALU.is_ge, fill=-BIG,
                                   base=0, pattern=[[-1, P]], channel_multiplier=1).then_inc(sem("tables_ready"), 1)
            pool.affine_select(out=before[:], in_=before[:], compare_op=ALU.is_gt, fill=0.0, base=0,
                               pattern=[[1, P]], channel_multiplier=-1).then_inc(sem("tables_ready"), 1)
            pool.affine_select(out=eye32[:, 0:ROUNDS * E], in_=eye32[:, 0:ROUNDS * E], compare_op=ALU.not_equal,
                               fill=1.0, base=0, pattern=[[0, ROUNDS], [-1, E]], channel_multiplier=1)\
                .then_inc(sem("tables_ready"), 1)
            pool.iota(iota[:], pattern=[[1, SLOTS]], base=0, channel_multiplier=0,
                      allow_small_or_imprecise_dtypes=True).then_inc(sem("tables_ready"), 1)

        @block.tensor
        def _(pe):
            def turn(dst, src, rows=P):
                return pe.transpose(dst, src, ident[0:rows, 0:rows])

            used = [0]

            def arrive(n):
                pe.wait_ge(landed[n % RING], 32 * (n // RING + 1))

            def product(banks, left, chunks, cols, kmax):
                for n in chunks:
                    _, k0, nk, _, _ = HEAD[n]
                    arrive(n)
                    w = head_view(n)
                    for m in range(NM):
                        for k in range(k0, k0 + nk):
                            mm = pe.matmul(banks[m][:, 0:cols], left[:, k, m * P:(m + 1) * P], w[:, k - k0, :],
                                           start=(k == 0), stop=(k == kmax - 1), skip_group_check=True)
                    mm.then_inc(ring_used, 1)
                    assert used[0] == n
                    used[0] += 1

            pe.wait_ge(sem("ident_ready"), 1)
            for m in range(NM):
                pe.wait_ge(sem("xn_ready"), m + 1)
                for k in range(KD):
                    mm = turn(bank[2 * m + k // 4][:, (k % 4) * P:(k % 4 + 1) * P], xn[:, m, k * P:(k + 1) * P])
                    if k % 4 == 3:
                        mm.then_inc(sem("xnT_turned"), 1)
            pe.wait_ge(sem("xnT_copied"), 4)

            def unit(u):
                if u >= 4:
                    pe.wait_ge(sem("unit_copied"), 2 * (u - 3))
                return bank[2 * (u % 4)], bank[2 * (u % 4) + 1]

            u = 0
            for c0, n in ((O_Q, Q_LORA // 2), (O_Q + Q_LORA // 2, Q_LORA // 2), (O_KV, KVW), (O_DQ, WD), (O_DK, WD)):
                i = chunk_index("w_in", 0, c0)
                product(unit(u), xnT, (i, i + 1), n, KD)
                u += 1
            for m in range(NM):
                b = unit(u)
                pe.wait_ge(sem("lat_ready"), 2 * (m + 1))
                for k in range(KQ + KKV):
                    src = qlat[:, m, k * P:(k + 1) * P] if k < KQ else kvlat[:, m, (k - KQ) * P:(k - KQ + 1) * P]
                    mm = turn(b[k // 4][:, (k % 4) * P:(k % 4 + 1) * P], src)
                mm.then_inc(sem("lat_turned"), 1)
                u += 1
            b7, b8 = unit(u), unit(u + 1)
            pe.wait_ge(sem("unit_copied"), 2 * u)
            u += 2
            n0 = chunk_index("w_uq", 0, 0)
            HQ = HA * QK_A // 2
            for i in range(KQ // 2):
                arrive(n0 + i)
                w = head_view(n0 + i)
                for h, b in enumerate((b7, b8)):
                    for m in range(NM):
                        for k in (2 * i, 2 * i + 1):
                            mm = pe.matmul(b[m][:, 0:HQ], latT[:, k, m * P:(m + 1) * P], w[:, k - 2 * i, h * HQ:(h + 1) * HQ],
                                           start=(k == 0), stop=(k == KQ - 1), skip_group_check=True)
                mm.then_inc(ring_used, 1)
                used[0] += 1
            n0 = chunk_index("w_ukv", 0, 0)
            arrive(n0)
            w = head_view(n0)
            b9, b10 = unit(u), unit(u + 1)
            u += 2
            for h, b in enumerate((b9, b10)):
                for m in range(NM):
                    for k in range(KKV):
                        mm = pe.matmul(b[m][:], latT[:, KQ + k, m * P:(m + 1) * P], w[:, k, h * HALF:(h + 1) * HALF],
                                       start=(k == 0), stop=(k == KKV - 1), skip_group_check=True)
            mm.then_inc(ring_used, 1)
            used[0] += 1
            i = chunk_index("w_in", 0, O_DV)
            product(unit(u), xnT, (i, i + 1), WD, KD)
            u += 1
            for m in range(NM):
                b = unit(u)
                pe.wait_ge(sem("qkd_ready"), m + 1)
                for i in range(SUB):
                    mm = turn(b[i // 4][:, (i % 4) * P:(i % 4 + 1) * P],
                              qkd[:, m, 2 * i:2 * i + 2, :].rearrange("p a b -> p (a b)"))
                mm.then_inc(sem("qkd_turned"), 1)
                u += 1
            pe.wait_ge(sem("unit_copied"), 2 * u)

            def scores(s):
                if s >= 2:
                    pe.wait_ge(sem("scored"), s - 1)
                b = bank[s % 2]
                for m in range(NM):
                    if s < SUB:
                        lo = DD * (s % 2)
                        q = dqkT[lo:lo + DD, s // 2, m * P:(m + 1) * P]
                        k = dqkT[lo:lo + DD, SUB // 2 + s // 2, 0:(m + 1) * P]
                    else:
                        q = qkaT[0:QK_A, s - SUB, m * P:(m + 1) * P]
                        k = qkaT[0:QK_A, HA + s - SUB, 0:(m + 1) * P]
                    mm = pe.matmul(b[:, m * P:(2 * m + 1) * P], q, k, start=(m == 0), stop=True, skip_group_check=True)
                mm.then_inc(sem("scores"), 1)

            def probs_turn(s):
                pe.wait_ge(sem("exped"), 2 * (s + 1))
                if s >= 2:
                    pe.wait_ge(sem("probsT_copied"), s - 1)
                for i in range(3):
                    mm = turn(bank[2 + s % 2][:, i * P:(i + 1) * P], probs[:, s % 2, i * P:(i + 1) * P])
                mm.then_inc(sem("probs_turned"), 1)

            def values(s):
                pe.wait_ge(sem("probsT_copied"), s + 1)
                if s >= 2:
                    pe.wait_ge(sem("headed"), s - 1)
                n = DV if s < SUB else VA
                b = bank[4 + s % 2]

                def v_of(m):
                    return dv[:, m, (s // 2) * DV:(s // 2 + 1) * DV] if s < SUB else va[:, m, s - SUB, :]

                pT = probsT[:, s % 2]
                pe.matmul(b[:, 0:n], pT[:, 0:P], v_of(0), start=True, stop=True, skip_group_check=True)
                pe.matmul(b[:, n:2 * n], pT[:, P:2 * P], v_of(0), start=True, stop=False, skip_group_check=True)
                pe.matmul(b[:, n:2 * n], pT[:, 2 * P:3 * P], v_of(1), start=False, stop=True, skip_group_check=True)\
                  .then_inc(sem("valued"), 1)

            def gate_part(s):
                g, q = s // 4, s % 4
                n = chunk_index("w_in", 0, O_GATE + g * HALF) + q // 2
                if q == 0 and g >= 1:
                    pe.wait_ge(sem("gates_copied"), 2 * g)
                arrive(n)
                w = head_view(n)
                for m in range(NM):
                    for k in (2 * q, 2 * q + 1):
                        mm = pe.matmul(bank[6 + m][:], xnT[:, k, m * P:(m + 1) * P], w[:, k % 4, :],
                                       start=(k == 0), stop=(k == KD - 1), skip_group_check=True)
                if q % 2:
                    mm.then_inc(ring_used, 1)
                    used[0] += 1

            def step(s, last):
                if s < last:
                    scores(s)
                if s - 1 >= 0 and (s - 1) // SUB == (last - 1) // SUB:
                    probs_turn(s - 1)
                if s < last:
                    gate_part(s)
                if s - 1 >= 0 and (s - 1) // SUB == (last - 1) // SUB:
                    values(s - 1)

            for s in range(SUB + 1):
                step(s, SUB)
            pe.wait_ge(sem("qka_ready"), NM)
            pe.wait_ge(sem("headed"), SUB)
            for i in range(HA):
                if i >= 6:
                    pe.wait_ge(sem("qkaT_copied"), i - 5)
                for a in range(2):
                    for m in range(NM):
                        mm = turn(bank[i % 6][0:QK_A, (2 * a + m) * P:(2 * a + m + 1) * P], qka[:, m, 2 * i + a, :])
                mm.then_inc(sem("qka_turned"), 1)
            pe.wait_ge(sem("qkaT_copied"), HA)
            for s in range(SUB, SUB + HA + 1):
                step(s, SUB + HA)

            pe.wait_ge(sem("headed"), SUB + HA)
            pe.wait_ge(sem("ob_ready"), NM)
            pe.wait_ge(sem("gates_copied"), 8)
            for m in range(NM):
                for i in range(HD):
                    mm = turn(bank[m][:, i * P:(i + 1) * P], o_b[:, m, i, :])
                mm.then_inc(sem("o_turned"), 1)
            for m in range(NM):
                for i in range(HD):
                    mm = turn(bank[2 + m][:, i * P:(i + 1) * P],
                              o_a[:, m, 2 * i:2 * i + 2, :].rearrange("p a b -> p (a b)"))
                mm.then_inc(sem("o_turned"), 1)
            for j, (name, left) in enumerate((("w_bd", o_bT), ("w_ba", o_aT))):
                pe.wait_ge(sem("oT_copied"), 2 if j == 0 else 4)
                base = 4 if j == 0 else 0
                for h in range(2):
                    n = chunk_index(name, 0, h * HALF)
                    product((bank[base + 2 * h], bank[base + 2 * h + 1]), left, (n,), HALF, 4)

            for m in range(NM):
                pe.wait_ge(sem("merged_ready"), m + 1)
                for k in range(KD):
                    mm = turn(bank[4 + 2 * m + k // 4][:, (k % 4) * P:(k % 4 + 1) * P], merged[:, m, k * P:(k + 1) * P])
                    if k % 4 == 3:
                        mm.then_inc(sem("merged_turned"), 1)
            pe.wait_ge(sem("mergedT_copied"), 4)
            for h in range(2):
                n = chunk_index("w_out", 0, h * HALF)
                product((bank[2 * h], bank[2 * h + 1]), mergedT, (n, n + 1), HALF, KD)

            for m in range(NM):
                pe.wait_ge(sem("t_ready"), m + 1)
                for k in range(KD):
                    mm = turn(bank[4 + 2 * m + k // 4][:, (k % 4) * P:(k % 4 + 1) * P], t_sb[:, m, k * P:(k + 1) * P])
                    if k % 4 == 3:
                        mm.then_inc(sem("t_turned"), 1)
            pe.wait_ge(sem("tT_copied"), 4)
            pe.wait_ge(sem("small_landed"), 16 * SMALL)
            wr = v3(w_rt[:], KD)
            for m in range(NM):
                for k in range(KD):
                    mm = pe.matmul(bank[0][:, m * E:(m + 1) * E], tT[:, k, m * P:(m + 1) * P], wr[:, k, :],
                                   start=(k == 0), stop=(k == KD - 1), skip_group_check=True)
            mm.then_inc(sem("logits"), 1)
            pe.wait_ge(sem("chosen"), NM)
            pe.wait_ge(sem("tables_ready"), TABLES)
            pe.matmul(bank[1][:, 0:E], before[:], chosen_v[:, 0], start=True, stop=True, skip_group_check=True)
            pe.matmul(bank[1][:, E:2 * E], ones[:], chosen_v[:, 0], start=True, stop=False, skip_group_check=True)
            pe.matmul(bank[1][:, E:2 * E], before[:], chosen_v[:, 1], start=False, stop=True, skip_group_check=True)
            pe.matmul(bank[1][:, 2 * E:3 * E], ones[:], chosen_v[:, 0], start=True, stop=False, skip_group_check=True)
            pe.matmul(bank[1][:, 2 * E:3 * E], ones[:], chosen_v[:, 1], start=False, stop=True, skip_group_check=True)\
              .then_inc(sem("places"), 1)
            pe.wait_ge(sem("weights_ready"), NM)
            for m in range(NM):
                mm = turn(bank[2][0:E, m * P:(m + 1) * P], weight_v[:, m, 0:E])
            mm.then_inc(sem("weights_turned"), 1)
            pe.wait_ge(sem("weightT_copied"), 1)
            pe.wait_ge(sem("bias_landed"), 32)
            for m in range(NM):
                for h in range(2):
                    pe.matmul(bank[4 + 2 * m + h][:], weightT[:, m * P:(m + 1) * P], b2_sb[:, h * HALF:(h + 1) * HALF],
                              start=True, stop=True, skip_group_check=True).then_inc(sem("b2_done"), 1)

            def gather():
                for k in range(KD):
                    for m in range(NM):
                        mm = pe.matmul(bank[6 + k // 4][:, (k % 4) * P:(k % 4 + 1) * P], t_sb[:, m, k * P:(k + 1) * P],
                                       onehot[:, m].rearrange("p e s -> p (e s)"),
                                       start=(m == 0), stop=(m == 1), skip_group_check=True)
                mm.then_inc(sem("gathered"), 1)

            def pair_arrive(j, c):
                n = NHEAD + c
                pe.wait_ge(landed[n % RING], 32 * (JOB_CHUNKS // RING) * j + 32 * (n // RING + 1))
                return slot(n)

            def turn_act(half):
                for c in range(4):
                    mm = turn(bank[6 + half][:, c * P:(c + 1) * P], act_out[:, half, c * P:(c + 1) * P])
                mm.then_inc(sem(f"act_turned{half}"), 1)

            def pair(j):
                pe.wait_ge(sem("xT_copied"), 2 * j + 2)
                pe.wait_ge(sem("pick_ready"), j + 1)
                for f in range(2):
                    ug, ul = bank[2 * f], bank[2 * f + 1]
                    pe.wait_ge(sem("acc_added"), 4 * j + 2 + 2 * f)
                    for g, b in enumerate((ug, ul)):
                        c0 = g * F + f * HALF
                        pe.matmul(b[:], pick.rearrange("p e s -> p (e s)"), b1_sb[:, c0:c0 + HALF],
                                  start=True, stop=False, skip_group_check=True)
                    for k in range(KD):
                        w = pair_arrive(j, f * KD + k).rearrange("p (e g n) -> p e g n", e=2, g=2)
                        for g, b in enumerate((ug, ul)):
                            for e in range(2):
                                mm = pe.matmul(b[e * SLOTS:(e + 1) * SLOTS, :], xT[:, k, e * SLOTS:(e + 1) * SLOTS],
                                               w[:, e, g, :], start=False, stop=(k == KD - 1), skip_group_check=True)
                        mm.then_inc(ring_used, 1)
                        if f == 1 and k == 5:
                            pe.wait_ge(sem("act_ready0"), j + 1)
                            turn_act(0)
                for k in range(KD):
                    if k % 4 == 0:
                        pe.wait_ge(sem(f"aT_copied{k // 4}"), j + 1)
                    w = pair_arrive(j, 2 * KD + k).rearrange("p (e h n) -> p e h n", e=2, h=2)
                    for h in range(2):
                        for e in range(2):
                            mm = pe.matmul(bank[4 + h][e * SLOTS:(e + 1) * SLOTS, :],
                                           aT[k // 4][:, k % 4, e * SLOTS:(e + 1) * SLOTS], w[:, e, h, :],
                                           start=(k == 0), stop=(k == KD - 1), skip_group_check=True)
                    mm.then_inc(ring_used, 1)
                    if k == 2:
                        pe.wait_ge(sem("act_ready1"), j + 1)
                        turn_act(1)
                        pe.wait_ge(sem("gated_ready"), j + 1)
                        for m in range(NM):
                            mm = turn(bank[2][:, m * P:(m + 1) * P], gated[:, m].rearrange("p e s -> p (e s)"))
                        mm.then_inc(sem("gated_turned"), 1)
                pe.wait_ge(sem("y_copied"), 2 * j + 2)
                pe.wait_ge(sem("gatedT_copied"), j + 1)
                for m in range(NM):
                    for h in range(2):
                        pe.matmul(bank[2 * m + h][:], gatedT[:, m * P:(m + 1) * P], y_sb[:, h * HALF:(h + 1) * HALF],
                                  start=True, stop=True, skip_group_check=True).then_inc(sem("scattered"), 1)
                pe.wait_ge(sem("onehot_ready"), j + 2)
                gather()

            pe.wait_ge(sem("onehot_ready"), 1)
            pe.wait_ge(sem("acc_added"), 4)
            gather()
            for name in ("gated_turned", "act_turned0", "act_turned1"):
                pe.sem_inc(sem(name), 1)
            pe.sem_inc(sem("scattered"), 4)
            with pe.Fori(0, PAIRS) as j:
                pair(j)
            pe.wait_ge(sem("counted"), 1)
            most = pe.value_load(fullest_i[0:1, 0:1], min_val=0, max_val=SEQ)
            with pe.Fori(1, ROUNDS) as r:
                with pe.If(most > r * SLOTS):
                    with pe.Fori(0, PAIRS) as p_:
                        pair(r * PAIRS + p_)

        @block.scalar
        def _(act):
            act.dma_start(g_attn, gain(attn_norm, D)).then_inc(sem("gain_landed"), 16)
            act.dma_start(g_qlat, gain(q_lat_norm, Q_LORA)).then_inc(sem("lat_gain_landed"), 16)
            act.dma_start(g_kvlat, gain(kv_lat_norm, KV_LORA)).then_inc(sem("lat_gain_landed"), 16)
            small = [(tab[:], rope), (g_qkd[:, 0:DD], gain(dq_norm, DD)), (g_qkd[:, DD:2 * DD], gain(dk_norm, DD)),
                     (g_qka[:, 0:QK_A], gain(q_norm, QK_A)), (g_qka[:, QK_A:2 * QK_A], gain(k_norm, QK_A)),
                     (lam_in[:, 0:DD], gain(lq1, DD)), (lam_in[:, DD:2 * DD], gain(lq2, DD)),
                     (lam_in[:, 2 * DD:3 * DD], gain(lk1, DD)), (lam_in[:, 3 * DD:4 * DD], gain(lk2, DD)),
                     (g_sub[:], gain(subln, DV)), (b_rt[:], gain(b_router, E)),
                     (v3(w_rt[:], KD), w_router.rearrange("(k p) n -> p k n", p=P))]
            assert len(small) == SMALL
            for dst, src in small:
                act.dma_start(dst, src).then_inc(sem("small_landed"), 16)
            act.wait_ge(sem("const_set"), 7)

            for m in range(NM):
                act.wait_ge(sem(f"x_landed{m}"), 16)
                act.activation(xn[:, m], acc[:, m], ACT.Square, accum_out=ssq[:, m:m + 1]).then_inc(sem("x_squared"), 1)
                act.wait_ge(sem("x_squared"), m + 1)
                act.activation(ssq[:, m:m + 1], ssq[:, m:m + 1], ACT.Sqrt, bias=eps[:], scale=1.0 / D)\
                   .then_inc(sem("x_rooted"), 1)
            for i in range(4):
                m, half = i // 2, i % 2
                act.wait_ge(sem("xnT_turned"), i + 1)
                act.copy(xnT[:, 4 * half:4 * half + 4, m * P:(m + 1) * P], v3(bank[i][:], 4))\
                   .then_inc(sem("xnT_copied"), 1)

            def unit_copy(u, m, dst, src_cols, done=None):
                b = bank[2 * (u % 4) + m]
                return act.copy(dst, b[:, 0:src_cols])

            UQ = chunk_index("w_in", 4, O_Q), chunk_index("w_in", 4, O_Q + Q_LORA // 2), chunk_index("w_in", 4, O_KV)
            for u in range(3):
                act.wait_ge(ring_used, UQ[u] + 1)
                for m in range(NM):
                    if u < 2:
                        dst, n = qlat[:, m, u * Q_LORA // 2:(u + 1) * Q_LORA // 2], Q_LORA // 2
                    else:
                        dst, n = kvlat[:, m, :], KVW
                    unit_copy(u, m, dst, n).then_inc(sem("unit_copied"), 1)
            act.wait_ge(sem("unit_copied"), 6)
            act.wait_ge(sem("xn_ready"), NM)
            act.wait_ge(sem("xnT_turned"), 4)
            for m in range(NM):
                act.activation(xn[:, m, 0:Q_LORA], qlat[:, m], ACT.Square, accum_out=ssq[:, 4 + m:5 + m])\
                   .then_inc(sem("lat_squared"), 1)
                act.activation(xn[:, m, Q_LORA:], kvlat[:, m, 0:KV_LORA], ACT.Square, accum_out=ssq[:, 6 + m:7 + m])\
                   .then_inc(sem("lat_squared"), 1)
            act.wait_ge(sem("lat_squared"), 4)
            act.activation(ssq[:, 4:6], ssq[:, 4:6], ACT.Sqrt, bias=eps[:], scale=1.0 / Q_LORA).then_inc(sem("lat_rooted"), 1)
            act.activation(ssq[:, 6:8], ssq[:, 6:8], ACT.Sqrt, bias=eps[:], scale=1.0 / KV_LORA).then_inc(sem("lat_rooted"), 1)

            for i, c0 in enumerate((O_DQ, O_DK)):
                act.wait_ge(ring_used, chunk_index("w_in", 4, c0) + 1)
                for m in range(NM):
                    unit_copy(3 + i, m, qkd[:, m, i * SUB:(i + 1) * SUB, :].rearrange("p a b -> p (a b)"), WD)\
                        .then_inc(sem("unit_copied"), 1)
            act.wait_ge(sem("unit_copied"), 10)
            for m in range(NM):
                act.activation(tok_r[:, m * D:(m + 1) * D], qkd[:, m].rearrange("p a b -> p (a b)"), ACT.Square)\
                   .then_inc(sem("qkd_squared"), 1)
            for m in range(NM):
                act.wait_ge(sem("lat_turned"), m + 1)
                for i in range(2):
                    act.copy(latT[:, 4 * i:4 * i + 4, m * P:(m + 1) * P], v3(bank[2 * ((5 + m) % 4) + i][:], 4))\
                       .then_inc(sem("unit_copied"), 1)
            for m in range(NM):
                act.wait_ge(sem("qkd_summed"), m + 1)
                r = slice(8 + 16 * m, 24 + 16 * m)
                act.activation(ssq[:, r], ssq[:, r], ACT.Sqrt, bias=eps[:], scale=1.0 / DD).then_inc(sem("qkd_rooted"), 1)
            act.wait_ge(ring_used, chunk_index("w_uq", 4, 0) + 1)
            for i in range(2):
                for m in range(NM):
                    unit_copy(7 + i, m, qka[:, m, 4 * i:4 * i + 4, :].rearrange("p a b -> p (a b)"), 4 * QK_A)\
                        .then_inc(sem("unit_copied"), 1)
            act.wait_ge(ring_used, chunk_index("w_ukv", 0, 0) + 1)
            for i in range(2):
                for m in range(NM):
                    b = bank[2 * ((9 + i) % 4) + m][:].rearrange("p (h d) -> p h d", h=4)
                    act.copy(qka[:, m, HA + 4 * i:HA + 4 * i + 4, 0:NOPE], b[:, :, 0:NOPE]).then_inc(sem("k_copied"), 1)
                    act.copy(va[:, m, 4 * i:4 * i + 4, :], b[:, :, NOPE:]).then_inc(sem("unit_copied"), 1)
            for m in range(NM):
                act.copy(qka[:, m, HA:, NOPE:], kvlat[:, m, KV_LORA:].unsqueeze(1).broadcast_to([P, HA, ROPE_A]))\
                   .then_inc(sem("k_copied"), 1)
            act.wait_ge(sem("k_copied"), 6)
            act.wait_ge(sem("unit_copied"), 22)
            for m in range(NM):
                if m:
                    act.wait_ge(sem("qka_summed"), m)
                act.activation(squares, qka[:, m].rearrange("p a b -> p (a b)"), ACT.Square).then_inc(sem("qka_squared"), 1)
            act.wait_ge(ring_used, chunk_index("w_in", 4, O_DV) + 1)
            for m in range(NM):
                unit_copy(11, m, dv[:, m], WD).then_inc(sem("unit_copied"), 1)
            act.wait_ge(sem("qka_summed"), NM)
            r = slice(8, 40)
            act.wait_ge(sem("qkd_inverted"), NM)
            for m in range(NM):
                act.activation(rstd[:, 16 * m + 8:16 * m + 24], ssq[:, 16 * m + 8:16 * m + 24], ACT.Sqrt, bias=eps[:],
                               scale=1.0 / QK_A).then_inc(sem("qka_rooted"), 1)
            for m in range(NM):
                act.wait_ge(sem("qkd_turned"), m + 1)
                for i in range(2):
                    act.copy(dqkT[:, 4 * i:4 * i + 4, m * P:(m + 1) * P], v3(bank[2 * ((12 + m) % 4) + i][:], 4))\
                       .then_inc(sem("unit_copied"), 1)
            act.wait_ge(sem("lambda_summed"), 1)
            act.activation(lam[:, 2:4], lam[:, 0:2], ACT.Exp).then_inc(sem("lambda_exped"), 1)

            def exps(s):
                act.wait_ge(sem("maxed"), 2 * (s + 1))
                if s >= 2:
                    act.wait_ge(sem("probs_turned"), s - 1)
                for m in range(NM):
                    c = slice(0, P) if m == 0 else slice(P, 3 * P)
                    act.activation(probs[:, s % 2, c], scored[:, s % 2, c], ACT.Exp, bias=nmax[:, 2 * s + m:2 * s + m + 1],
                                   accum_out=sums[:, 2 * s + m:2 * s + m + 1]).then_inc(sem("exped"), 1)

            def probsT_copy(s):
                act.wait_ge(sem("probs_turned"), s + 1)
                if s >= 2:
                    act.wait_ge(sem("valued"), s - 1)
                act.copy(probsT[:, s % 2], bank[2 + s % 2][:, 0:3 * P]).then_inc(sem("probsT_copied"), 1)

            def gates_copy(s):
                if s % 4 == 3:
                    g = s // 4
                    act.wait_ge(ring_used, chunk_index("w_in", 4, O_GATE + g * HALF) + 1)
                    for m in range(NM):
                        act.copy(gates[:, m, g * HALF:(g + 1) * HALF], bank[6 + m][:]).then_inc(sem("gates_copied"), 1)

            act.wait_ge(sem("lat_ready"), 4)
            for lo, hi in ((0, SUB), (SUB, SUB + HA)):
                if lo:
                    for i in range(HA):
                        act.wait_ge(sem("qka_turned"), i + 1)
                        act.copy(qkaT[0:QK_A, 2 * i:2 * i + 2, :], v3(bank[i % 6][0:QK_A, :], 2)).then_inc(sem("qkaT_copied"), 1)
                for s in range(lo, hi + 1):
                    if s < hi:
                        exps(s)
                    if s - 1 >= lo:
                        probsT_copy(s - 1)
                    if s < hi:
                        gates_copy(s)
            act.wait_ge(sem("scores"), SUB + HA)
            act.dma_start(b1_sb, b1).then_inc(sem("bias_landed"), 16)
            act.dma_start(b2_sb, b2).then_inc(sem("bias_landed"), 16)
            act.wait_ge(sem("qkd_turned"), NM)
            act.dma_start(g_ffn, gain(ffn_norm, D)).then_inc(sem("ffn_gain_landed"), 16)
            for m in range(NM):
                act.wait_ge(sem("ob_diffed"), m + 1)
                act.activation(scored_sq(soft, m), o_b[:, m].rearrange("p a b -> p (a b)"), ACT.Square).then_inc(sem("ob_squared"), 1)
            act.wait_ge(sem("ob_summed"), NM)
            act.activation(ssq[:, 40:40 + 2 * HD], ssq[:, 40:40 + 2 * HD], ACT.Sqrt, bias=eps[:], scale=1.0 / DV)\
               .then_inc(sem("ob_rooted"), 1)
            act.wait_ge(sem("gates_copied"), 8)
            for m in range(NM):
                act.activation(gates[:, m], gates[:, m], ACT.Sigmoid).then_inc(sem("gates_ready"), 1)
            for i in range(4):
                act.wait_ge(sem("o_turned"), i + 1)
                dst = o_bT if i < 2 else o_aT
                act.copy(dst[:, :, (i % 2) * P:(i % 2 + 1) * P], v3(bank[i][:], 4)).then_inc(sem("oT_copied"), 1)
            for i in range(4):
                m, half = i // 2, i % 2
                act.wait_ge(sem("merged_turned"), i + 1)
                act.copy(mergedT[:, 4 * half:4 * half + 4, m * P:(m + 1) * P], v3(bank[4 + i][:], 4))\
                   .then_inc(sem("mergedT_copied"), 1)
            for m in range(NM):
                act.wait_ge(sem("h_ready"), 2 * NM)
                act.wait_ge(sem("merged_turned"), 4)
                act.activation(t_sb[:, m], acc[:, m], ACT.Square, accum_out=ssq[:, 50 + m:51 + m]).then_inc(sem("h_squared"), 1)
            act.wait_ge(sem("h_squared"), NM)
            act.activation(ssq[:, 50:52], ssq[:, 50:52], ACT.Sqrt, bias=eps[:], scale=1.0 / D).then_inc(sem("h_rooted"), 1)
            for i in range(4):
                m, half = i // 2, i % 2
                act.wait_ge(sem("t_turned"), i + 1)
                act.copy(tT[:, 4 * half:4 * half + 4, m * P:(m + 1) * P], v3(bank[4 + i][:], 4)).then_inc(sem("tT_copied"), 1)
            for m in range(NM):
                act.wait_ge(sem("top_negated"), m + 1)
                act.activation(expd_v[:, m], logit_v[:, m, 0:E], ACT.Exp, bias=negtop[:, m:m + 1]).then_inc(sem("router_exped"), 1)
            act.wait_ge(sem("weights_turned"), 1)
            act.copy(weightT[:], bank[2][0:E, 0:SEQ]).then_inc(sem("weightT_copied"), 1)

            def xT_copy():
                for i in range(2):
                    act.copy(xT[:, 4 * i:4 * i + 4, :], v3(bank[6 + i][:], 4)).then_inc(sem("xT_copied"), 1)

            def pair(j):
                for f in range(2):
                    act.wait_ge(sem(f"glu_ready{f}"), j + 1)
                    act.activation(sig[:, f], glu[:, f], ACT.Sigmoid, scale=ALPHA).then_inc(sem(f"sig_ready{f}"), 1)
                    act.wait_ge(sem(f"act_turned{f}"), j + 2)
                    act.wait_ge(ring_used, JOB_CHUNKS * j + NHEAD)
                    act.copy(aT[f], v3(bank[6 + f][:], 4)).then_inc(sem(f"aT_copied{f}"), 1)
                act.wait_ge(sem("gated_turned"), j + 2)
                act.wait_ge(sem("scattered"), 4 * j + 4)
                act.copy(gatedT, bank[2][:, 0:SEQ]).then_inc(sem("gatedT_copied"), 1)
                act.wait_ge(ring_used, JOB_CHUNKS * j + NHEAD + JOB_CHUNKS)
                for h in range(2):
                    act.copy(y_sb[:, h * HALF:(h + 1) * HALF], bank[4 + h][:]).then_inc(sem("y_copied"), 1)
                act.wait_ge(sem("gathered"), j + 2)
                xT_copy()

            act.wait_ge(sem("gathered"), 1)
            xT_copy()
            with act.Fori(0, PAIRS) as j:
                pair(j)
            act.wait_ge(sem("counted"), 1)
            most = act.value_load(fullest_i[0:1, 0:1], min_val=0, max_val=SEQ)
            with act.Fori(1, ROUNDS) as r:
                with act.If(most > r * SLOTS):
                    with act.Fori(0, PAIRS) as p_:
                        pair(r * PAIRS + p_)

        @block.vector
        def _(dve):
            chain = [0]

            def link(ins):
                chain[0] += 1
                ins.then_inc(sem("dve_chain"), 1)
                dve.wait_ge(sem("dve_chain"), chain[0])

            tt, ts, stt = dve.tensor_tensor, dve.tensor_scalar, dve.scalar_tensor_tensor

            dve.memset(logit_v[:, :, E:], -SENTINEL).then_inc(sem("sentinels"), 1)
            dve.wait_ge(sem("gain_landed"), 16)
            for m in range(NM):
                dve.wait_ge(sem("x_rooted"), m + 1)
                link(dve.reciprocal(rstd[:, m:m + 1], ssq[:, m:m + 1]))
                stt(xn[:, m], acc[:, m], rstd[:, m:m + 1], g_attn, ALU.mult, ALU.mult).then_inc(sem("xn_ready"), 1)
            dve.wait_ge(sem("small_landed"), 16 * SMALL)
            link(tt(scratch_m[:, 0:2 * DD], lam_in[:, 0:2 * DD], lam_in[:, 2 * DD:], ALU.mult))
            dve.tensor_reduce(lam[:, 0:2], v3(scratch_m[:, 0:2 * DD], 2), AX.X, ALU.add).then_inc(sem("lambda_summed"), 1)
            dve.wait_ge(sem("lat_rooted"), 2)
            dve.wait_ge(sem("lat_gain_landed"), 32)
            link(dve.reciprocal(rstd[:, 4:8], ssq[:, 4:8]))
            for m in range(NM):
                stt(qlat[:, m], qlat[:, m], rstd[:, 4 + m:5 + m], g_qlat, ALU.mult, ALU.mult).then_inc(sem("lat_ready"), 1)
                stt(kvlat[:, m, 0:KV_LORA], kvlat[:, m, 0:KV_LORA], rstd[:, 6 + m:7 + m], g_kvlat, ALU.mult, ALU.mult)\
                    .then_inc(sem("lat_ready"), 1)

            tab_v = tab[:].rearrange("p (m c) -> p m c", m=NM)

            def norm_rope(qk, m, n, width, rot, tab0, gains, r, tmp, done):
                t4 = qk[:, m]
                link(tt(t4, t4, r.unsqueeze(2).broadcast_to([P, 2 * n, width]), ALU.mult))
                for i in range(2):
                    g = gains[:, i * width:(i + 1) * width].unsqueeze(1).broadcast_to([P, n, width])
                    ins = tt(t4[:, i * n:(i + 1) * n], t4[:, i * n:(i + 1) * n], g, ALU.mult)
                    if i:
                        link(ins)
                    else:
                        ins.then_inc(sem("gain_half"), 1)
                half = rot // 2
                x1, x2 = t4[:, :, width - rot:width - half], t4[:, :, width - half:width]
                cos = tab_v[:, m, tab0:tab0 + half].unsqueeze(1).broadcast_to([P, 2 * n, half])
                sin = tab_v[:, m, tab0 + half:tab0 + rot].unsqueeze(1).broadcast_to([P, 2 * n, half])
                nt = 2 * n * half
                a, b, c, d = (v3(tmp[:, i * nt:(i + 1) * nt], 2 * n) for i in range(4))
                gained[0] += 1
                dve.wait_ge(sem("gain_half"), gained[0])
                tt(a, x1, cos, ALU.mult).then_inc(sem("rotated"), 1)
                tt(b, x2, sin, ALU.mult).then_inc(sem("rotated"), 1)
                tt(c, x2, cos, ALU.mult).then_inc(sem("rotated"), 1)
                tt(d, x1, sin, ALU.mult).then_inc(sem("rotated"), 1)
                rotated[0] += 4
                dve.wait_ge(sem("rotated"), rotated[0])
                link(tt(x1, a, b, ALU.subtract))
                tt(x2, c, d, ALU.add).then_inc(done, 1)

            gained, rotated = [0], [0]
            for m in range(NM):
                dve.wait_ge(sem("qkd_squared"), m + 1)
                dve.tensor_reduce(ssq[:, 8 + 16 * m:24 + 16 * m], v3(tok_r[:, m * D:(m + 1) * D], 2 * SUB), AX.X, ALU.add)\
                   .then_inc(sem("qkd_summed"), 1)
            for m in range(NM):
                dve.wait_ge(sem("qkd_rooted"), m + 1)
                dve.wait_ge(sem("qkd_summed"), NM)
                r = rstd[:, 8 + 16 * m:24 + 16 * m]
                link(dve.reciprocal(r, ssq[:, 8 + 16 * m:24 + 16 * m]))
                dve.sem_inc(sem("qkd_inverted"), 1)
                norm_rope(qkd, m, SUB, DD, DD, ROPE_A, g_qkd, r, tok_r, sem("qkd_ready"))
            dve.wait_ge(sem("qkd_ready"), NM)
            for m in range(NM):
                dve.wait_ge(sem("qka_squared"), m + 1)
                dve.tensor_reduce(ssq[:, 8 + 16 * m:24 + 16 * m], v3(squares, 2 * HA), AX.X, ALU.add)\
                   .then_inc(sem("qka_summed"), 1)

            def scale_mask(s):
                dve.wait_ge(sem("scores"), s + 1)
                if s >= 2:
                    dve.wait_ge(sem("exped"), 2 * (s - 1))
                scale = DD ** -0.5 if s < SUB else QK_A ** -0.5
                stt(scored[:, s % 2], bank[s % 2][:, 0:3 * P], scale, mask[:], ALU.mult, ALU.add).then_inc(sem("scored"), 1)
                dve.wait_ge(sem("scored"), s + 1)
                for m in range(NM):
                    c = slice(0, P) if m == 0 else slice(P, 3 * P)
                    dve.tensor_reduce(nmax[:, 2 * s + m:2 * s + m + 1], scored[:, s % 2, c], AX.X, ALU.max, negate=True)\
                       .then_inc(sem("maxed"), 1)

            def head_out(s):
                dve.wait_ge(sem("exped"), 2 * (s + 1))
                link(dve.reciprocal(rsum[:, 2 * s:2 * s + 2], sums[:, 2 * s:2 * s + 2]))
                dve.wait_ge(sem("valued"), s + 1)
                n = DV if s < SUB else VA
                dst = o_raw[:, :, s, :] if s < SUB else o_a[:, :, s - SUB, :]
                tt(dst, v3(bank[4 + s % 2][:, 0:2 * n], 2), rsum[:, 2 * s:2 * s + 2].unsqueeze(2).broadcast_to([P, NM, n]),
                   ALU.mult).then_inc(sem("headed"), 1)

            dve.wait_ge(sem("tables_ready"), TABLES)
            for s in range(SUB + 1):
                if s < SUB:
                    scale_mask(s)
                if s >= 1:
                    head_out(s - 1)
                if s in (1, 3):
                    m = s // 2
                    dve.wait_ge(sem("qka_rooted"), m + 1)
                    r = rstd[:, 8 + 16 * m:24 + 16 * m]
                    link(dve.reciprocal(r, r))
                    norm_rope(qka, m, HA, QK_A, ROPE_A, 0, g_qka, r, qkT_r, sem("qka_ready"))
            for s in range(SUB, SUB + HA + 1):
                if s < SUB + HA:
                    scale_mask(s)
                if s >= SUB + 1:
                    head_out(s - 1)
            dve.wait_ge(sem("headed"), SUB + HA)
            dve.wait_ge(sem("lambda_exped"), 1)
            link(tt(lam[:, 4:5], lam[:, 3:4], lam[:, 2:3], ALU.subtract))
            link(ts(lam[:, 5:6], lam[:, 4:5], -LAMBDA_INIT, None, ALU.add))
            pairs = o_raw.rearrange("p m (h a) d -> p m h a d", a=2)
            for m in range(NM):
                stt(o_b[:, m], pairs[:, m, :, 1], lam[:, 5:6], pairs[:, m, :, 0], ALU.mult, ALU.add)\
                    .then_inc(sem("ob_diffed"), 1)
            for m in range(NM):
                dve.wait_ge(sem("ob_squared"), m + 1)
                dve.tensor_reduce(ssq[:, 40 + HD * m:40 + HD * (m + 1)], v3(scored_sq(soft, m), HD), AX.X, ALU.add)\
                   .then_inc(sem("ob_summed"), 1)
            link(ts(g_sub[:], g_sub[:], 1.0 - LAMBDA_INIT, None, ALU.mult))
            dve.wait_ge(sem("ob_rooted"), 1)
            link(dve.reciprocal(rstd[:, 40:48], ssq[:, 40:48]))
            for m in range(NM):
                r = rstd[:, 40 + HD * m:40 + HD * (m + 1)].unsqueeze(2).broadcast_to([P, HD, DV])
                link(tt(o_b[:, m], o_b[:, m], r, ALU.mult))
                tt(o_b[:, m], o_b[:, m], g_sub[:].unsqueeze(1).broadcast_to([P, HD, DV]), ALU.mult)\
                    .then_inc(sem("ob_ready"), 1)
            for j, (name, base) in enumerate((("w_bd", 4), ("w_ba", 0))):
                for h in range(2):
                    dve.wait_ge(ring_used, chunk_index(name, 0, h * HALF) + 1)
                    for m in range(NM):
                        if j == 0 and h == 0:
                            dve.wait_ge(sem("gates_ready"), m + 1)
                        g = gates[:, m, (1 - j) * D + h * HALF:(1 - j) * D + (h + 1) * HALF]
                        tt(g, bank[base + 2 * h + m][:], g, ALU.mult).then_inc(sem("branch_gated"), 1)
            dve.wait_ge(sem("branch_gated"), 8)
            dve.wait_ge(sem("scores"), SUB)
            for m in range(NM):
                tt(merged[:, m], gates[:, m, 0:D], gates[:, m, D:], ALU.add).then_inc(sem("merged_ready"), 1)
            for h in range(2):
                dve.wait_ge(ring_used, chunk_index("w_out", 4, h * HALF) + 1)
                for m in range(NM):
                    a = acc[:, m, h * HALF:(h + 1) * HALF]
                    tt(a, bank[2 * h + m][:], a, ALU.add).then_inc(sem("h_ready"), 1)
            dve.wait_ge(sem("h_rooted"), 1)
            link(dve.reciprocal(rstd[:, 50:52], ssq[:, 50:52]))
            dve.wait_ge(sem("ffn_gain_landed"), 16)
            for m in range(NM):
                stt(t_sb[:, m], acc[:, m], rstd[:, 50 + m:51 + m], g_ffn, ALU.mult, ALU.mult).then_inc(sem("t_ready"), 1)
            dve.wait_ge(sem("logits"), 1)
            dve.wait_ge(sem("sentinels"), 1)
            for m in range(NM):
                link(tt(logit_v[:, m, 0:E], bank[0][:, m * E:(m + 1) * E], b_rt[:], ALU.add))
                t8 = top[:, 8 * m:8 * m + 8]
                link(dve.max(t8, logit_v[:, m]))
                ts(negtop[:, m:m + 1], t8[:, 0:1], -1.0, None, ALU.mult).then_inc(sem("top_negated"), 1)
                dve.wait_ge(sem("top_negated"), m + 1)
                link(dve.memset(t8[:, TOP_K:8], -SENTINEL))
                link(dve.match_replace(marked_v[:, m], t8, logit_v[:, m], SENTINEL))
                ts(chosen_v[:, m], marked_v[:, m, 0:E], SENTINEL, None, ALU.is_ge).then_inc(sem("chosen"), 1)
            for m in range(NM):
                dve.wait_ge(sem("router_exped"), m + 1)
                dve.wait_ge(sem("chosen"), m + 1)
                link(tt(expd_v[:, m], expd_v[:, m], chosen_v[:, m], ALU.mult))
                link(dve.tensor_reduce(gsum[:, m:m + 1], expd_v[:, m], AX.X, ALU.add))
                link(dve.reciprocal(grec[:, m:m + 1], gsum[:, m:m + 1]))
                ts(weight_v[:, m, 0:E], expd_v[:, m], grec[:, m:m + 1], None, ALU.mult).then_inc(sem("weights_ready"), 1)
            dve.wait_ge(sem("places"), 1)
            FAR = 1024.0
            dve.memset(place_v[:, :, ROUNDS * E:], -FAR).then_inc(sem("place_pad"), 1)
            dve.wait_ge(sem("weights_ready"), NM)
            for m in range(NM):
                link(stt(marked_v[:, m, 0:E], bank[1][:, m * E:(m + 1) * E], FAR, chosen_v[:, m], ALU.add, ALU.mult))
                for r in range(ROUNDS):
                    ts(place_v[:, m, r * E:(r + 1) * E], marked_v[:, m, 0:E], -FAR - SLOTS * r, None, ALU.add)\
                        .then_inc(sem("placed"), 1)
                for r in range(1, ROUNDS):
                    dve.tensor_copy(weight_v[:, m, r * E:(r + 1) * E], weight_v[:, m, 0:E]).then_inc(sem("placed"), 1)
            link(dve.tensor_reduce(fullest[:, 0:1], bank[1][:, 2 * E:3 * E], AX.X, ALU.max))
            dve.tensor_copy(fullest_i[:], fullest[:, 0:1]).then_inc(sem("counted"), 1)
            dve.wait_ge(sem("placed"), NM * (2 * ROUNDS - 1))
            dve.wait_ge(sem("place_pad"), 1)

            def columns(j):
                return slice(2 * j, 2 * j + 2)

            def spread(ap, parts=P):
                return ap.unsqueeze(2).broadcast_to([parts, 2, SLOTS])

            iota_b = iota[:].unsqueeze(1).broadcast_to([P, 2, SLOTS])

            def onehots(j):
                for m in range(NM):
                    ins = tt(onehot[:, m], iota_b, spread(place_v[:, m, bass.ds(2 * j, 2)]), ALU.is_equal)
                return ins

            def picks(j):
                return dve.tensor_copy(pick, spread(eye32[:, bass.ds(2 * j, 2)], E))

            dve.wait_ge(sem("scores"), SUB + HA)
            for m in range(NM):
                ins = tt(onehot[:, m], iota_b, spread(place_v[:, m, 0:2]), ALU.is_equal)
            ins.then_inc(sem("onehot_ready"), 1)
            dve.tensor_copy(pick, spread(eye32[:, 0:2], E)).then_inc(sem("pick_ready"), 1)
            for i in range(2 * NM):
                m, h = i // 2, i % 2
                dve.wait_ge(sem("b2_done"), i + 1)
                a = acc[:, m, h * HALF:(h + 1) * HALF]
                tt(a, bank[4 + i][:], a, ALU.add).then_inc(sem("acc_added"), 1)

            def pair(j):
                dve.wait_ge(sem("onehot_ready"), j + 1)
                dve.wait_ge(sem("gated_turned"), j + 1)
                for m in range(NM):
                    ins = tt(gated[:, m], onehot[:, m], spread(weight_v[:, m, bass.ds(2 * j, 2)]), ALU.mult)
                ins.then_inc(sem("gated_ready"), 1)
                dve.wait_ge(sem("gathered"), j + 1)
                dve.wait_ge(sem("gated_ready"), j + 1)
                onehots(j + 1).then_inc(sem("onehot_ready"), 1)
                for f in range(2):
                    dve.wait_ge(ring_used, JOB_CHUNKS * j + NHEAD + KD * (f + 1))
                    dve.wait_ge(sem(f"act_turned{f}"), j + 1)
                    ts(glu[:, f], bank[2 * f][:], LIMIT, None, ALU.min).then_inc(sem(f"glu_ready{f}"), 1)
                    ts(lin[:, f], bank[2 * f + 1][:], LIMIT, -LIMIT, ALU.min, ALU.max).then_inc(sem(f"lin_ready{f}"), 1)
                    dve.wait_ge(sem(f"glu_ready{f}"), j + 1)
                    dve.wait_ge(sem(f"lin_ready{f}"), 2 * j + 1)
                    stt(lin[:, f], lin[:, f], 1.0, glu[:, f], ALU.add, ALU.mult).then_inc(sem(f"lin_ready{f}"), 1)
                    dve.wait_ge(sem(f"lin_ready{f}"), 2 * j + 2)
                    dve.wait_ge(sem(f"sig_ready{f}"), j + 1)
                    tt(act_out[:, f], lin[:, f], sig[:, f], ALU.mult).then_inc(sem(f"act_ready{f}"), 1)
                picks(j + 1).then_inc(sem("pick_ready"), 1)
                for i in range(2 * NM):
                    m, h = i // 2, i % 2
                    dve.wait_ge(sem("scattered"), 4 * j + i + 5)
                    a = acc[:, m, h * HALF:(h + 1) * HALF]
                    tt(a, bank[i][:], a, ALU.add).then_inc(sem("acc_added"), 1)

            with dve.Fori(0, PAIRS) as j:
                pair(j)
            dve.wait_ge(sem("acc_added"), 4 + 4 * PAIRS)
            most = dve.value_load(fullest_i[0:1, 0:1], min_val=0, max_val=SEQ)
            with dve.Fori(1, ROUNDS) as r:
                with dve.If(most > r * SLOTS):
                    with dve.Fori(0, PAIRS) as p_:
                        pair(r * PAIRS + p_)
                    dve.wait_ge(sem("acc_added"), 4 * PAIRS * (r + 1) + 4)
                    dve.sem_inc(sem("rounds_added"), 1)
            dve.sem_inc(sem("finished"), 1)


TABLES = 5
SMALL = 12


def scored_sq(soft, m):
    return soft.rearrange("p a b -> p (a b)")[:, m * HALF:(m + 1) * HALF]


def rope_tables():
    cols = []
    for dim in (ROPE_A, DD):
        inv = (1.0 / (np.float32(10000.0) ** (np.arange(0, dim, 2, dtype=np.float32) / np.float32(dim)))).astype(np.float32)
        ang = np.arange(SEQ, dtype=np.float32)[:, None] * inv[None, :]
        cols += [np.cos(ang).astype(np.float32), np.sin(ang).astype(np.float32)]
    tabs = np.concatenate(cols, axis=1)
    return np.ascontiguousarray(tabs.reshape(NM, P, -1).transpose(1, 0, 2).reshape(P, -1))


_INS = ['x', 'attn_norm', 'w_in', 'mla_q_lat_norm', 'mla_kv_lat_norm', 'mla_w_uq', 'mla_w_ukv', 'mla_q_norm',
        'mla_k_norm', 'diff_q_norm', 'diff_k_norm', 'diff_lambda_q1', 'diff_lambda_k1', 'diff_lambda_q2',
        'diff_lambda_k2', 'diff_subln', 'w_branch_mla', 'w_branch_diff', 'w_out', 'ffn_norm', 'w_router',
        'b_router', 'w_mlp1', 'b_mlp1', 'w_mlp2', 'b_mlp2']


def kernel(**inputs):
    import concourse.bacc as _bacc
    from concourse.bass_utils import run_bass_kernel_spmd as _run

    nc = _bacc.Bacc("TRN2", target_bir_lowering=False, num_devices=1, dynamic_dma_scratch_size=1024)
    arrays, args = {}, []
    for name in _INS + ["rope"]:
        a = rope_tables() if name == "rope" else np.ascontiguousarray(inputs[name])[0]
        arrays[f"in_{name}"] = a
        args.append(nc.dram_tensor(f"in_{name}", a.shape, F32, kind="ExternalInput").ap())
    out = nc.dram_tensor("out_h", [SEQ, D], F32, kind="ExternalOutput").ap()
    build(nc, *args, out)
    r = _run(nc, [arrays], core_ids=[0])
    return r.results[0]["out_h"].reshape(1, SEQ, D)
```

```python
import math
from contextlib import ExitStack

import numpy as np

import concourse.bass as bass
from concourse import mybir

F32 = mybir.dt.float32
F32R = mybir.dt.float32r
I32 = mybir.dt.int32
ALU = mybir.AluOpType
ACT = mybir.ActivationFunctionType
AX = mybir.AxisListType

P = 128
SEQ, D = 256, 1024
NM = SEQ // P
KD = D // P
EPS = 1e-6

HA, NOPE, ROPE_A, VA = 8, 64, 32, 64
QK_A = NOPE + ROPE_A
Q_LORA, KV_LORA = 768, 256
KQ, KKV = Q_LORA // P, KV_LORA // P
HD, DD = 4, 64
SUB, DV = 2 * HD, 2 * DD
WA, WD = HA * VA, HD * DV
LAMBDA_INIT = 0.8 - 0.6 * math.exp(-0.3 * 0)

E, TOP_K, F = 32, 4, D
ALPHA, LIMIT = 1.702, 7.0
SLOTS = 64
ROUNDS = SEQ // SLOTS
PAIRS = E // 2
JOBS = ROUNDS * PAIRS
COLS = ROUNDS * E + 2

O_Q, O_KV = 0, Q_LORA
O_DQ = Q_LORA + KV_LORA + ROPE_A
O_DK, O_DV, O_GATE = O_DQ + WD, O_DQ + 2 * WD, O_DQ + 3 * WD
KVW = KV_LORA + ROPE_A
HALF = 512

RING, SLOT = 12, 2048
HEAD_RING = 8
BUFFERS = RING - 1 - HEAD_RING
EXTRA = 4
WIDE = RING + EXTRA
JOB_CHUNKS = 3 * KD
CYCLE = 2 * JOB_CHUNKS
assert CYCLE % WIDE == 0
BIG = 1e30
SENTINEL = 3e38


def head_chunks():
    out = []
    for c0, n in ((O_Q, Q_LORA // 2), (O_Q + Q_LORA // 2, Q_LORA // 2), (O_KV, KVW), (O_DQ, WD), (O_DK, WD)):
        out += [("w_in", k, KD // 2, c0, n) for k in (0, KD // 2)]
    out += [("w_uq", k, 2, 0, HA * QK_A) for k in range(0, KQ, 2)]
    out += [("w_ukv", 0, KKV, 0, HA * (NOPE + VA))]
    out += [("w_in", k, KD // 2, O_DV, WD) for k in (0, KD // 2)]
    for g in range(2 * D // HALF):
        out += [("w_in", k, KD // 2, O_GATE + g * HALF, HALF) for k in (0, KD // 2)]
    out += [("w_bd", 0, WD // P, h * HALF, HALF) for h in range(2)]
    out += [("w_ba", 0, WA // P, h * HALF, HALF) for h in range(2)]
    out += [("w_out", k, KD // 2, h * HALF, HALF) for h in range(2) for k in (0, KD // 2)]
    return out


HEAD = head_chunks()
NHEAD = len(HEAD)
SPLIT = [n for n, c in enumerate(HEAD) if c[0] in ("w_in", "w_out")]


def slot_of(n):
    if n < NHEAD:
        return n % HEAD_RING
    s = (n - NHEAD) % WIDE
    if s < EXTRA:
        return RING + s
    return (NHEAD + s - EXTRA) % HEAD_RING if s < EXTRA + HEAD_RING else s - EXTRA


def lap_of(n):
    s = slot_of(n)
    return sum(slot_of(i) == s for i in range(min(n + 1, NHEAD))) + (0 if n < NHEAD else (n - NHEAD) // WIDE + 1)


def chunk_index(matrix, k, c0):
    return next(n for n, (w, k0, nk, c, _) in enumerate(HEAD) if (w, c) == (matrix, c0) and k0 <= k < k0 + nk)


def build(nc, x, attn_norm, w_in, q_lat_norm, kv_lat_norm, w_uq, w_ukv, q_norm, k_norm, dq_norm, dk_norm,
          lq1, lk1, lq2, lk2, subln, w_bmla, w_bdiff, w_out, ffn_norm, w_router, b_router,
          w1, b1, w2, b2, rope, out):
    ctx = ExitStack()
    with ctx:
        def sb(name, cols, dt=F32, parts=P):
            return ctx.enter_context(nc.sbuf_tensor(name, [parts, cols], dt))

        sems = {}

        def sem(name):
            if name not in sems:
                sems[name] = ctx.enter_context(nc.semaphore(name))
            return sems[name]

        with nc.sbuf_tensor("ring_s", [P, RING * SLOT], F32R) as ring_s, \
             nc.sbuf_tensor("feat_s", [P, KD * SEQ], F32R) as feat_s:
            pass
        ring = sb("ring", RING * SLOT)
        feat_r = sb("feat_r", KD * SEQ)
        acc_r = sb("acc_r", NM * D)
        tok_r = sb("tok_r", NM * D)
        gate_r = sb("gate_r", NM * 2 * D)
        lat_r = sb("lat_r", NM * (Q_LORA + KVW))
        qkd_r = sb("qkd_r", NM * 2 * WD)
        qka_r = sb("qka_r", NM * 2 * HA * QK_A)
        v_r = sb("v_r", NM * (WD + WA))
        latT_r = sb("latT_r", (KQ + KKV) * SEQ)
        qkT_r = sb("qkT_r", 2 * HA * SEQ)
        soft_r = sb("soft_r", 6 * 384)

        v3 = lambda t, a: t.rearrange("p (a b) -> p a b", a=a)
        acc = v3(acc_r[:], NM)
        xn = v3(tok_r[:], NM)
        featT = v3(feat_s[:], KD), v3(ring_s[:, (RING - 1) * SLOT:RING * SLOT], KD)
        gates = v3(gate_r[:], NM)
        g_attn, g_qlat, g_kvlat = gate_r[:, 0:D], gate_r[:, D:D + Q_LORA], gate_r[:, D + Q_LORA:D + Q_LORA + KV_LORA]
        qlat, kvlat = v3(lat_r[:, 0:NM * Q_LORA], NM), v3(lat_r[:, NM * Q_LORA:], NM)
        o_a = lat_r[:, 0:NM * WA].rearrange("p (m h d) -> p m h d", m=NM, h=HA)
        qkd = qkd_r[:].rearrange("p (m h d) -> p m h d", m=NM, h=2 * SUB)
        qka = qka_r[:].rearrange("p (m h d) -> p m h d", m=NM, h=2 * HA)
        dv, va = v3(v_r[:, 0:NM * WD], NM), v_r[:, NM * WD:].rearrange("p (m h d) -> p m h d", m=NM, h=HA)
        latT = v3(latT_r[:], KQ + KKV)
        o_raw = latT_r[:].rearrange("p (m h d) -> p m h d", m=NM, h=SUB)
        dqkT = v3(tok_r[:], SUB)
        qkaT = v3(qkT_r[:], 2 * HA)
        squares = qkT_r[:, 0:2 * HA * QK_A]
        o_b = qkd_r[:, 0:NM * WD].rearrange("p (m h d) -> p m h d", m=NM, h=HD)
        g_ffn = qkd_r[:, NM * WD:NM * WD + D]
        o_bT, o_aT = v3(qka_r[:, 0:HD * SEQ], HD), v3(qka_r[:, HD * SEQ:2 * HD * SEQ], HD)
        merged, t_sb, tT = xn, xn, v3(feat_r[:], KD)
        soft = v3(soft_r[:], 6)
        scored, probs, probsT = soft[:, 0:2], soft[:, 2:4], soft[:, 4:6]
        b1_sb, b2_sb = qkT_r[0:E, 0:2 * F], qkT_r[0:E, 2 * F:2 * F + D]
        hot_0 = 3 * D
        onehot = qkT_r[:, hot_0:hot_0 + NM * P].rearrange("p (m e s) -> p m e s", m=NM, e=2)
        gated = qkT_r[:, hot_0 + NM * P:hot_0 + 2 * NM * P].rearrange("p (m e s) -> p m e s", m=NM, e=2)
        gatedT = qkT_r[:, hot_0 + 2 * NM * P:hot_0 + 3 * NM * P]
        pick = qkT_r[0:E, hot_0 + 3 * NM * P:hot_0 + 3 * NM * P + P].rearrange("p (e s) -> p e s", e=2)
        xT = v3(feat_r[:, 0:KD * P], KD)
        glu, sig, lin, act_out = (v3(gate_r[:, i * D:(i + 1) * D], 2) for i in range(4))
        aT = [v3(soft_r[:, i * HALF:(i + 1) * HALF], 4) for i in range(2)]
        y_sb = soft_r[:, D:2 * D]

        fold = sb("fold", E)
        partial = sb("partial", SEQ)
        w_rt = sb("w_rt", KD * E)
        tab = sb("tab", NM * (ROPE_A + DD))
        g_qka, g_qkd = sb("g_qka", 2 * QK_A), sb("g_qkd", 2 * DD)
        g_sub, lam_in = sb("g_sub", DV), sb("lam_in", 4 * DD)
        b_rt = sb("b_rt", E)
        ident, before, ones = sb("ident", P), sb("before", P), sb("ones", P)
        mask = sb("mask", 3 * P)
        iota = sb("iota", SLOTS)
        eye32 = sb("eye32", COLS, parts=E)
        place, weight = sb("place", NM * COLS), sb("weight", NM * COLS)
        place_v, weight_v = v3(place[:], NM), v3(weight[:], NM)
        eps = sb("eps", 1)
        ssq = sb("ssq", 64)
        rstd = sb("rstd", 64)
        nmax, sums, rsum = (sb(n, 2 * (SUB + HA)) for n in ("nmax", "sums", "rsum"))
        lam = sb("lam", 8)
        logit = sb("logit", NM * (E + 8))
        logit_v = v3(logit[:], NM)
        marked = sb("marked", NM * (E + 8))
        marked_v = v3(marked[:], NM)
        top = sb("top", NM * 8)
        chosen, expd = sb("chosen", NM * E), sb("expd", NM * E)
        chosen_v, expd_v = v3(chosen[:], NM), v3(expd[:], NM)
        negtop, gsum, grec = sb("negtop", NM), sb("gsum", NM), sb("grec", NM)
        weightT = sb("weightT", SEQ, parts=E)
        fullest = sb("fullest", 2)
        fullest_i = sb("fullest_i", 1, I32)
        scratch_m = sb("scratch_m", 4 * DD)

        bank = [ctx.enter_context(nc.psum_tensor(f"bank{i}", [P, HALF], F32)) for i in range(8)]

        matrices = {"w_in": w_in, "w_uq": w_uq, "w_ukv": w_ukv, "w_bd": w_bdiff, "w_ba": w_bmla, "w_out": w_out}
        landed = [sem(f"landed{s}") for s in range(WIDE)]
        ring_used = sem("ring_used")

        extra = [latT_r[:], v_r[:], lat_r[:, 0:SLOT], qka_r[:, 0:SLOT]]

        def slot(n, cols=SLOT):
            s = slot_of(n)
            return ring[:, s * SLOT:s * SLOT + cols] if s < RING else extra[s - RING]

        def head_view(n):
            _, _, nk, _, cols = HEAD[n]
            return v3(slot(n, nk * cols), nk)

        def split_views(i):
            n = SPLIT[i]
            _, _, nk, _, cols = HEAD[n]
            hi = (HEAD_RING + i % BUFFERS) * SLOT
            lo = slot_of(n) * SLOT
            return ring_s[:, hi:hi + nk * cols], ring_s[:, lo:lo + nk * cols]

        def gain(ap, n):
            return ap.rearrange("(a n) -> a n", a=1).broadcast_to([P, n])

        tab_v = tab[:].rearrange("p (m c) -> p m c", m=NM)

        def norm_rotate(eng, name, qk, m, n, width, r, gains, rot, tab0, tmp):
            t4 = qk[:, m]
            half = rot // 2
            x1, x2 = t4[:, :, width - rot:width - half], t4[:, :, width - half:width]
            cos = tab_v[:, m, tab0:tab0 + half].unsqueeze(1).broadcast_to([P, 2 * n, half])
            sin = tab_v[:, m, tab0 + half:tab0 + rot].unsqueeze(1).broadcast_to([P, 2 * n, half])
            nt = 2 * n * half
            a, b, c, d = (v3(tmp[:, i * nt:(i + 1) * nt], 2 * n) for i in range(4))
            tt = eng.tensor_tensor
            tt(t4, t4, r.unsqueeze(2).broadcast_to([P, 2 * n, width]), ALU.mult).then_inc(sem(f"{name}_normed"), 1)
            eng.wait_ge(sem(f"{name}_normed"), m + 1)
            for i in range(2):
                g = gains[:, i * width:(i + 1) * width].unsqueeze(1).broadcast_to([P, n, width])
                tt(t4[:, i * n:(i + 1) * n], t4[:, i * n:(i + 1) * n], g, ALU.mult).then_inc(sem(f"{name}_scaled"), 1)
            eng.wait_ge(sem(f"{name}_scaled"), 2 * m + 2)
            for dst, x_, by in ((a, x1, cos), (b, x2, sin), (c, x2, cos), (d, x1, sin)):
                tt(dst, x_, by, ALU.mult).then_inc(sem(f"{name}_rotated"), 1)
            eng.wait_ge(sem(f"{name}_rotated"), 4 * m + 4)
            tt(x1, a, b, ALU.subtract).then_inc(sem(f"{name}_ready"), 1)
            tt(x2, c, d, ALU.add).then_inc(sem(f"{name}_ready"), 1)

        block = ctx.enter_context(nc.Block())

        @block.sync
        def _(sp):
            sp.dma_start(acc[:, 0], x[0:P, :]).then_inc(sem("x_landed0"), 16)
            sp.dma_start(acc[:, 1], x[P:2 * P, :]).then_inc(sem("x_landed1"), 16)
            small = [(tab[:], rope), (g_qkd[:, 0:DD], gain(dq_norm, DD)), (g_qkd[:, DD:2 * DD], gain(dk_norm, DD)),
                     (g_qka[:, 0:QK_A], gain(q_norm, QK_A)), (g_qka[:, QK_A:2 * QK_A], gain(k_norm, QK_A)),
                     (lam_in[:, 0:DD], gain(lq1, DD)), (lam_in[:, DD:2 * DD], gain(lq2, DD)),
                     (lam_in[:, 2 * DD:3 * DD], gain(lk1, DD)), (lam_in[:, 3 * DD:4 * DD], gain(lk2, DD)),
                     (g_sub[:], gain(subln, DV)), (b_rt[:], gain(b_router, E)),
                     (v3(w_rt[:], KD), w_router.rearrange("(k p) n -> p k n", p=P))]
            assert len(small) == SMALL
            for n, (name, k0, nk, c0, cols) in enumerate(HEAD):
                if n == 4:
                    sp.dma_start(g_qlat, gain(q_lat_norm, Q_LORA)).then_inc(sem("lat_gain_landed"), 16)
                    sp.dma_start(g_kvlat, gain(kv_lat_norm, KV_LORA)).then_inc(sem("lat_gain_landed"), 16)
                if 6 <= n < 6 + SMALL // 2:
                    for dst, src in small[2 * (n - 6):2 * (n - 6) + 2]:
                        sp.dma_start(dst, src).then_inc(sem("small_landed"), 16)
                if n >= HEAD_RING:
                    sp.wait_ge(ring_used, n - HEAD_RING + 1)
                src = matrices[name].rearrange("(k p) n -> p k n", p=P)
                for a in range(2):
                    ks = slice(a * nk // 2, (a + 1) * nk // 2)
                    sp.dma_start(head_view(n)[:, ks, :], src[:, k0 + ks.start:k0 + ks.stop, c0:c0 + cols])\
                      .then_inc(landed[slot_of(n)], 16)

            w1_v = w1.rearrange("e (k p) (g h n) -> e k p h g n", p=P, g=2, h=2)
            w2_v = w2.rearrange("e (k p) n -> e k p n", p=P)

            def load_pair(i, pair, cycle):
                for c in range(JOB_CHUNKS):
                    n = NHEAD + i * JOB_CHUNKS + c
                    if n - NHEAD >= WIDE or not isinstance(cycle, int):
                        sp.wait_ge(ring_used, CYCLE * cycle + n - WIDE + 1)
                    elif n - NHEAD >= EXTRA:
                        sp.wait_ge(ring_used, min(n - EXTRA - HEAD_RING + 1, NHEAD))
                    elif c == 0:
                        sp.wait_ge(sem("ob_diffed"), NM)
                    elif c == 1:
                        sp.wait_ge(sem("valued"), SUB + HA)
                    elif c == 2:
                        sp.wait_ge(sem("o_turned"), 4)
                    else:
                        sp.wait_ge(ring_used, chunk_index("w_ba", 0, HALF) + 1)
                    for a in range(2):
                        if c < 2 * KD:
                            src = w1_v[2 * pair + a, c % KD, :, c // KD]
                            dst = slot(n).rearrange("p (e g n) -> p e g n", e=2, g=2)[:, a]
                        else:
                            src = w2_v[2 * pair + a, c - 2 * KD]
                            dst = slot(n).rearrange("p (e n) -> p e n", e=2)[:, a]
                        sp.dma_start(dst, src).then_inc(landed[slot_of(n)], 16)

            for i in range(2):
                load_pair(i, i, 0)
            with sp.Fori(1, PAIRS // 2) as j:
                for i in range(2):
                    load_pair(i, 2 * j + i, j)
            sp.wait_ge(sem("counted"), 1)
            most = sp.value_load(fullest_i[0:1, 0:1], min_val=0, max_val=SEQ)
            with sp.Fori(1, ROUNDS) as r:
                with sp.If(most > r * SLOTS):
                    with sp.Fori(0, PAIRS // 2) as j:
                        for i in range(2):
                            load_pair(i, 2 * j + i, r * (PAIRS // 2) + j)
            sp.wait_ge(sem("finished"), 1)
            for m in range(NM):
                sp.dma_start(out[m * P:(m + 1) * P, :], acc[:, m]).then_inc(sem("stored"), 16)
            sp.wait_ge(sem("stored"), 16 * NM)

        @block.gpsimd
        def _(pool):
            pool.memset(ident[:], 0.0).then_inc(sem("const_set"), 1)
            pool.memset(before[:], 1.0).then_inc(sem("const_set"), 1)
            pool.memset(ones[:], 1.0).then_inc(sem("const_set"), 1)
            pool.memset(mask[:], 0.0).then_inc(sem("const_set"), 1)
            pool.memset(eye32[:], 0.0).then_inc(sem("const_set"), 1)
            pool.memset(eps[:], EPS).then_inc(sem("const_set"), 1)
            pool.memset(weight[:], 0.0).then_inc(sem("const_set"), 1)
            pool.memset(fold[:], 0.0).then_inc(sem("const_set"), 1)
            pool.wait_ge(sem("const_set"), 8)
            pool.affine_select(out=ident[:], in_=ident[:], compare_op=ALU.not_equal, fill=1.0, base=0,
                               pattern=[[-1, P]], channel_multiplier=1).then_inc(sem("ident_ready"), 1)
            for c in (0, 2 * P):
                pool.affine_select(out=mask[:, c:c + P], in_=mask[:, c:c + P], compare_op=ALU.is_ge, fill=-BIG,
                                   base=0, pattern=[[-1, P]], channel_multiplier=1).then_inc(sem("tables_ready"), 1)
            pool.affine_select(out=before[:], in_=before[:], compare_op=ALU.is_gt, fill=0.0, base=0,
                               pattern=[[1, P]], channel_multiplier=-1).then_inc(sem("tables_ready"), 1)
            pool.affine_select(out=eye32[:, 0:ROUNDS * E], in_=eye32[:, 0:ROUNDS * E], compare_op=ALU.not_equal,
                               fill=1.0, base=0, pattern=[[0, ROUNDS], [-1, E]], channel_multiplier=1)\
                .then_inc(sem("tables_ready"), 1)
            for q in range(4):
                pool.affine_select(out=fold[:], in_=fold[:], compare_op=ALU.not_equal, fill=1.0, base=-E * q,
                                   pattern=[[-1, E]], channel_multiplier=1).then_inc(sem("folded"), 1)
                pool.wait_ge(sem("folded"), q + 1)
            pool.iota(iota[:], pattern=[[1, SLOTS]], base=0, channel_multiplier=0,
                      allow_small_or_imprecise_dtypes=True).then_inc(sem("tables_ready"), 1)
            for m in range(NM):
                pool.wait_ge(sem("qka_inverted"), m + 1)
                norm_rotate(pool, "qka", qka, m, HA, QK_A, rstd[:, 8 + 16 * m:24 + 16 * m], g_qka, ROPE_A, 0, qkT_r)

        @block.tensor
        def _(pe):
            def turn(dst, src, rows=P):
                return pe.transpose(dst, src, ident[0:rows, 0:rows])

            def arrive(n):
                pe.wait_ge(landed[slot_of(n)], 32 * lap_of(n))

            def product(banks, left, chunks, cols, kmax):
                for n in chunks:
                    _, k0, nk, _, _ = HEAD[n]
                    arrive(n)
                    w = head_view(n)
                    for m in range(NM):
                        for k in range(k0, k0 + nk):
                            mm = pe.matmul(banks[m][:, 0:cols], left[:, k, m * P:(m + 1) * P], w[:, k - k0, :],
                                           start=(k == 0), stop=(k == kmax - 1), skip_group_check=True)
                    mm.then_inc(ring_used, 1)

            def split_part(banks, n, ks, ms=range(NM)):
                _, k0, nk, _, cols = HEAD[n]
                i = SPLIT.index(n)
                pe.wait_ge(sem("lo_ready"), 2 * i + (2 if ks[-1] == k0 + nk - 1 else 1))
                hi, lo = (v3(v, nk) for v in split_views(i))
                for m in ms:
                    for k in ks:
                        for left, right in ((0, hi), (0, lo), (1, hi)):
                            mm = pe.matmul(banks[m][:, 0:cols], featT[left][:, k, m * P:(m + 1) * P], right[:, k - k0, :],
                                           start=(k == 0 and left == 0 and right is hi),
                                           stop=(k == KD - 1 and left == 1), skip_group_check=True)
                if ks[-1] == k0 + nk - 1 and ms[-1] == NM - 1:
                    mm.then_inc(ring_used, 1)

            def split_product(banks, chunks):
                for n in chunks:
                    split_part(banks, n, range(HEAD[n][1], HEAD[n][1] + HEAD[n][2]))

            pe.wait_ge(sem("ident_ready"), 1)
            for m in range(NM):
                pe.wait_ge(sem("xg_ready"), m + 1)
                for k in range(KD):
                    mm = turn(bank[2 * m + k // 4][:, (k % 4) * P:(k % 4 + 1) * P], xn[:, m, k * P:(k + 1) * P])
                    if k % 4 == 3:
                        mm.then_inc(sem("xgT_turned"), 1)
            pe.wait_ge(sem("featT_ready"), 4)

            def unit(u):
                if u >= 4:
                    pe.wait_ge(sem("unit_copied"), 2 * (u - 3))
                return bank[2 * (u % 4)], bank[2 * (u % 4) + 1]

            def project(u, c0):
                i = chunk_index("w_in", 0, c0)
                split_product(unit(u), (i, i + 1))

            project(0, O_Q)
            project(1, O_Q + Q_LORA // 2)
            project(2, O_KV)
            project(3, O_DQ)
            for m in range(NM):
                b = unit(4 + m)
                pe.wait_ge(sem("lat_ready"), 2 * (m + 1))
                for k in range(KQ + KKV):
                    src = qlat[:, m, k * P:(k + 1) * P] if k < KQ else kvlat[:, m, (k - KQ) * P:(k - KQ + 1) * P]
                    mm = turn(b[k // 4][:, (k % 4) * P:(k % 4 + 1) * P], src)
                mm.then_inc(sem("lat_turned"), 1)
            project(6, O_DK)
            bq = unit(7), unit(8)
            pe.wait_ge(sem("unit_copied"), 2 * 6)
            n0 = chunk_index("w_uq", 0, 0)
            HQ = HA * QK_A // 2
            for i in range(KQ // 2):
                arrive(n0 + i)
                w = head_view(n0 + i)
                for h, b in enumerate(bq):
                    for m in range(NM):
                        for k in (2 * i, 2 * i + 1):
                            mm = pe.matmul(b[m][:, 0:HQ], latT[:, k, m * P:(m + 1) * P], w[:, k - 2 * i, h * HQ:(h + 1) * HQ],
                                           start=(k == 0), stop=(k == KQ - 1), skip_group_check=True)
                mm.then_inc(ring_used, 1)
            n0 = chunk_index("w_ukv", 0, 0)
            arrive(n0)
            w = head_view(n0)
            for h in range(2):
                b = unit(9 + h)
                for m in range(NM):
                    for k in range(KKV):
                        mm = pe.matmul(b[m][:], latT[:, KQ + k, m * P:(m + 1) * P], w[:, k, h * HALF:(h + 1) * HALF],
                                       start=(k == 0), stop=(k == KKV - 1), skip_group_check=True)
            mm.then_inc(ring_used, 1)
            for m in range(NM):
                b = unit(11 + m)
                pe.wait_ge(sem("qkd_ready"), 2 * (m + 1))
                for i in range(SUB):
                    mm = turn(b[i // 4][:, (i % 4) * P:(i % 4 + 1) * P],
                              qkd[:, m, 2 * i:2 * i + 2, :].rearrange("p a b -> p (a b)"))
                mm.then_inc(sem("qkd_turned"), 1)
            project(13, O_DV)
            pe.wait_ge(sem("unit_copied"), 2 * 13)

            def scores(s):
                if s >= 2:
                    pe.wait_ge(sem("scored"), s - 1)
                b = bank[s % 2]
                for m in range(NM):
                    if s < SUB:
                        lo = DD * (s % 2)
                        q = dqkT[lo:lo + DD, s // 2, m * P:(m + 1) * P]
                        k = dqkT[lo:lo + DD, SUB // 2 + s // 2, 0:(m + 1) * P]
                    else:
                        q = qkaT[0:QK_A, s - SUB, m * P:(m + 1) * P]
                        k = qkaT[0:QK_A, HA + s - SUB, 0:(m + 1) * P]
                    mm = pe.matmul(b[:, m * P:(2 * m + 1) * P], q, k, start=(m == 0), stop=True, skip_group_check=True)
                mm.then_inc(sem("scores"), 1)

            def probs_turn(s):
                pe.wait_ge(sem("exped"), 2 * (s + 1))
                if s >= 2:
                    pe.wait_ge(sem("probsT_copied"), s - 1)
                for i in range(3):
                    mm = turn(bank[2 + s % 2][:, i * P:(i + 1) * P], probs[:, s % 2, i * P:(i + 1) * P])
                mm.then_inc(sem("probs_turned"), 1)

            def values(s):
                pe.wait_ge(sem("probsT_copied"), s + 1)
                if s >= 2:
                    pe.wait_ge(sem("headed"), s - 1)
                if s == 0:
                    pe.wait_ge(sem("unit_copied"), 2 * 14)
                n = DV if s < SUB else VA
                b = bank[4 + s % 2]

                def v_of(m):
                    return dv[:, m, (s // 2) * DV:(s // 2 + 1) * DV] if s < SUB else va[:, m, s - SUB, :]

                pT = probsT[:, s % 2]
                pe.matmul(b[:, 0:n], pT[:, 0:P], v_of(0), start=True, stop=True, skip_group_check=True)
                pe.matmul(b[:, n:2 * n], pT[:, P:2 * P], v_of(0), start=True, stop=False, skip_group_check=True)
                pe.matmul(b[:, n:2 * n], pT[:, 2 * P:3 * P], v_of(1), start=False, stop=True, skip_group_check=True)\
                  .then_inc(sem("valued"), 1)

            def gate_part(s, m):
                g, q = s // 4, s % 4
                n = chunk_index("w_in", 0, O_GATE + g * HALF) + q // 2
                if q == 0 and m == 0 and g >= 1:
                    pe.wait_ge(sem("gates_copied"), 2 * g)
                split_part((bank[6], bank[7]), n, (2 * q, 2 * q + 1), (m,))

            def step(s, first, last):
                if s < last:
                    scores(s)
                    gate_part(s, 0)
                if s > first:
                    probs_turn(s - 1)
                if s < last:
                    gate_part(s, 1)
                if s > first:
                    values(s - 1)

            for s in range(SUB + 1):
                step(s, 0, SUB)
            pe.wait_ge(sem("qka_ready"), 2 * NM)
            pe.wait_ge(sem("headed"), SUB)
            for i in range(HA):
                if i >= 6:
                    pe.wait_ge(sem("qkaT_copied"), i - 5)
                for a in range(2):
                    for m in range(NM):
                        mm = turn(bank[i % 6][0:QK_A, (2 * a + m) * P:(2 * a + m + 1) * P], qka[:, m, 2 * i + a, :])
                mm.then_inc(sem("qka_turned"), 1)
            pe.wait_ge(sem("qkaT_copied"), HA)
            HEADS = SUB + HA
            for s in range(SUB, HEADS):
                step(s, SUB, HEADS)

            def o_b_turn(m):
                pe.wait_ge(sem("ob_ready"), m + 1)
                pe.wait_ge(sem("scored"), HEADS - 1 + m)
                for i in range(HD):
                    mm = turn(bank[m][:, i * P:(i + 1) * P], o_b[:, m, i, :])
                mm.then_inc(sem("o_turned"), 1)

            o_b_turn(0)
            probs_turn(HEADS - 1)
            o_b_turn(1)
            values(HEADS - 1)
            pe.wait_ge(sem("gates_copied"), 8)
            pe.wait_ge(sem("oT_copied"), 2)
            product((bank[6], bank[7]), o_bT, (chunk_index("w_bd", 0, 0),), HALF, 4)
            pe.wait_ge(sem("headed"), HEADS)
            for m in range(NM):
                for i in range(HD):
                    mm = turn(bank[2 + m][:, i * P:(i + 1) * P],
                              o_a[:, m, 2 * i:2 * i + 2, :].rearrange("p a b -> p (a b)"))
                mm.then_inc(sem("o_turned"), 1)
            product((bank[4], bank[5]), o_bT, (chunk_index("w_bd", 0, HALF),), HALF, 4)
            pe.wait_ge(sem("oT_copied"), 4)
            for h in range(2):
                product((bank[2 * h], bank[2 * h + 1]), o_aT, (chunk_index("w_ba", 0, h * HALF),), HALF, 4)

            def turn_half(src, h, done, ready):
                for m in range(NM):
                    pe.wait_ge(ready, 2 * h + m + 1)
                    for i in range(4):
                        k = 4 * h + i
                        mm = turn(bank[4 + 2 * h + m][:, i * P:(i + 1) * P], src[:, m, k * P:(k + 1) * P])
                    mm.then_inc(done, 1)

            turn_half(merged, 0, sem("merged_turned"), sem("merged_ready"))
            turn_half(merged, 1, sem("merged_turned"), sem("merged_ready"))
            for h in range(2):
                n = chunk_index("w_out", 0, h * HALF)
                for i in range(2):
                    if h == 0:
                        pe.wait_ge(sem("featT_ready"), 4 + 2 * (i + 1))
                    split_product((bank[2 * h], bank[2 * h + 1]), (n + i,))

            for h in range(2):
                turn_half(t_sb, h, sem("t_turned"), sem("hg_ready"))
            pe.wait_ge(sem("small_landed"), 16 * SMALL)
            wr = v3(w_rt[:], KD)
            for i in range(2):
                pe.wait_ge(sem("tT_copied"), 2 * (i + 1))
                for q in range(4):
                    k = 4 * i + q
                    mm = pe.matmul(bank[0][q * E:(q + 1) * E, 0:SEQ], wr[:, k, :], tT[:, k, :],
                                   start=(i == 0), stop=(i == 1), skip_group_check=True)
            mm.then_inc(sem("partials"), 1)
            pe.wait_ge(sem("partial_copied"), 1)
            pe.wait_ge(sem("tables_ready"), TABLES)
            for m in range(NM):
                mm = pe.matmul(bank[1][:, m * E:(m + 1) * E], partial[:, m * P:(m + 1) * P], fold[:],
                               start=True, stop=True, skip_group_check=True)
            mm.then_inc(sem("logits"), 1)
            pe.wait_ge(sem("chosen"), NM)
            pe.matmul(bank[2][:, 0:E], before[:], chosen_v[:, 0], start=True, stop=True, skip_group_check=True)
            pe.matmul(bank[2][:, E:2 * E], ones[:], chosen_v[:, 0], start=True, stop=False, skip_group_check=True)
            pe.matmul(bank[2][:, E:2 * E], before[:], chosen_v[:, 1], start=False, stop=True, skip_group_check=True)\
              .then_inc(sem("places"), 1)

            def weights_turn():
                for m in range(NM):
                    mm = pe.matmul(bank[3][:, 0:E], ones[:], chosen_v[:, m], start=(m == 0), stop=(m == 1),
                                   skip_group_check=True)
                mm.then_inc(sem("counts"), 1)
                for m in range(NM):
                    mm = turn(bank[2][0:E, SEQ + m * P:SEQ + (m + 1) * P], weight_v[:, m, 0:E])
                mm.then_inc(sem("weights_turned"), 1)

            def gather():
                for k in range(KD):
                    for m in range(NM):
                        mm = pe.matmul(bank[6 + k // 4][:, (k % 4) * P:(k % 4 + 1) * P], t_sb[:, m, k * P:(k + 1) * P],
                                       onehot[:, m].rearrange("p e s -> p (e s)"),
                                       start=(m == 0), stop=(m == 1), skip_group_check=True)
                mm.then_inc(sem("gathered"), 1)

            def pair_arrive(i, cycle, c):
                n = NHEAD + i * JOB_CHUNKS + c
                pe.wait_ge(landed[slot_of(n)], 32 * (CYCLE // WIDE) * cycle + 32 * lap_of(n))
                return slot(n)

            def turn_act(half):
                for c in range(4):
                    mm = turn(bank[6 + half][:, c * P:(c + 1) * P], act_out[:, half, c * P:(c + 1) * P])
                mm.then_inc(sem(f"act_turned{half}"), 1)

            def pair(i, cycle, first=False):
                j = 2 * cycle + i
                pe.wait_ge(sem("xT_copied"), 2 * j + 2)
                pe.wait_ge(sem("pick_ready"), j + 1)
                for f in range(2):
                    ug, ul = bank[2 * f], bank[2 * f + 1]
                    if not first:
                        pe.wait_ge(sem("acc_added"), 4 * j - 2 + 2 * f)
                    else:
                        pe.wait_ge(sem("bias_landed"), 32)
                    for g, b in enumerate((ug, ul)):
                        c0 = g * F + f * HALF
                        pe.matmul(b[:], pick.rearrange("p e s -> p (e s)"), b1_sb[:, c0:c0 + HALF],
                                  start=True, stop=False, skip_group_check=True)
                    for k in range(KD):
                        w = pair_arrive(i, cycle, f * KD + k).rearrange("p (e g n) -> p e g n", e=2, g=2)
                        for g, b in enumerate((ug, ul)):
                            for e in range(2):
                                mm = pe.matmul(b[e * SLOTS:(e + 1) * SLOTS, :], xT[:, k, e * SLOTS:(e + 1) * SLOTS],
                                               w[:, e, g, :], start=False, stop=(k == KD - 1), skip_group_check=True)
                        mm.then_inc(ring_used, 1)
                        if f == 1 and k == 5:
                            pe.wait_ge(sem("act_ready0"), j + 1)
                            turn_act(0)
                for k in range(KD):
                    if k % 4 == 0:
                        pe.wait_ge(sem(f"aT_copied{k // 4}"), j + 1)
                    w = pair_arrive(i, cycle, 2 * KD + k).rearrange("p (e h n) -> p e h n", e=2, h=2)
                    for h in range(2):
                        for e in range(2):
                            mm = pe.matmul(bank[4 + h][e * SLOTS:(e + 1) * SLOTS, :],
                                           aT[k // 4][:, k % 4, e * SLOTS:(e + 1) * SLOTS], w[:, e, h, :],
                                           start=(k == 0), stop=(k == KD - 1), skip_group_check=True)
                    mm.then_inc(ring_used, 1)
                    if k == 2:
                        pe.wait_ge(sem("act_ready1"), j + 1)
                        turn_act(1)
                        pe.wait_ge(sem("gated_ready"), j + 1)
                        for m in range(NM):
                            mm = turn(bank[2][:, m * P:(m + 1) * P], gated[:, m].rearrange("p e s -> p (e s)"))
                        mm.then_inc(sem("gated_turned"), 1)
                        if first:
                            weights_turn()
                pe.wait_ge(sem("y_copied"), 2 * j + 2)
                pe.wait_ge(sem("gatedT_copied"), j + 1)
                if first:
                    pe.wait_ge(sem("weightT_copied"), 1)
                    pe.wait_ge(sem("counted"), 1)
                for m in range(NM):
                    for h in range(2):
                        if first:
                            pe.matmul(bank[2 * m + h][:], weightT[:, m * P:(m + 1) * P], b2_sb[:, h * HALF:(h + 1) * HALF],
                                      start=True, stop=False, skip_group_check=True)
                        pe.matmul(bank[2 * m + h][:], gatedT[:, m * P:(m + 1) * P], y_sb[:, h * HALF:(h + 1) * HALF],
                                  start=not first, stop=True, skip_group_check=True).then_inc(sem("scattered"), 1)
                pe.wait_ge(sem("onehot_ready"), j + 2)
                gather()

            pe.wait_ge(sem("onehot_ready"), 1)
            pe.wait_ge(sem("t_scaled"), 2)
            gather()
            pair(0, 0, first=True)
            pair(1, 0)
            with pe.Fori(1, PAIRS // 2) as j:
                pair(0, j)
                pair(1, j)
            most = pe.value_load(fullest_i[0:1, 0:1], min_val=0, max_val=SEQ)
            with pe.Fori(1, ROUNDS) as r:
                with pe.If(most > r * SLOTS):
                    with pe.Fori(0, PAIRS // 2) as j:
                        pair(0, r * (PAIRS // 2) + j)
                        pair(1, r * (PAIRS // 2) + j)

        @block.scalar
        def _(act):
            act.dma_start(g_attn, gain(attn_norm, D)).then_inc(sem("gain_landed"), 16)
            act.wait_ge(sem("const_set"), 8)

            for m in range(NM):
                act.wait_ge(sem(f"x_landed{m}"), 16)
                act.activation(qkd_r[:, m * D:(m + 1) * D], acc[:, m], ACT.Square, accum_out=ssq[:, m:m + 1])\
                   .then_inc(sem("x_squared"), 1)
            act.wait_ge(sem("x_squared"), NM)
            act.activation(ssq[:, 0:NM], ssq[:, 0:NM], ACT.Sqrt, bias=eps[:], scale=1.0 / D).then_inc(sem("x_rooted"), 1)
            def split_hi(i):
                n = SPLIT[i]
                act.wait_ge(landed[slot_of(n)], 32 * lap_of(n))
                if i >= BUFFERS:
                    act.wait_ge(ring_used, SPLIT[i - BUFFERS] + 1)
                _, _, nk, _, cols = HEAD[n]
                act.copy(split_views(i)[0], slot(n, nk * cols)).then_inc(sem("hi_ready"), 1)

            for i in range(4):
                act.wait_ge(sem("xgT_turned"), i + 1)
                act.copy(featT[0][:, 4 * (i % 2):4 * (i % 2) + 4, (i // 2) * P:(i // 2 + 1) * P], v3(bank[i][:], 4))\
                   .then_inc(sem("featT_hi"), 1)
            for i in range(BUFFERS):
                split_hi(i)
            act.wait_ge(sem("x_inverted"), 1)

            def project_copy(u, m, dst, n):
                act.activation(dst, bank[2 * (u % 4) + m][:, 0:n], ACT.Copy, scale=rstd[:, m:m + 1])\
                   .then_inc(sem("unit_copied"), 1)

            act.wait_ge(sem("xgT_turned"), 4)
            for u, c0 in enumerate((O_Q, O_Q + Q_LORA // 2, O_KV)):
                split_hi(2 * u + 3)
                act.wait_ge(ring_used, chunk_index("w_in", 4, c0) + 1)
                for m in range(NM):
                    if u < 2:
                        project_copy(u, m, qlat[:, m, u * Q_LORA // 2:(u + 1) * Q_LORA // 2], Q_LORA // 2)
                    else:
                        project_copy(u, m, kvlat[:, m, :], KVW)
                split_hi(2 * u + 4)
            act.wait_ge(sem("unit_copied"), 6)
            for m in range(NM):
                act.activation(xn[:, m, 0:Q_LORA], qlat[:, m], ACT.Square, accum_out=ssq[:, 4 + m:5 + m])\
                   .then_inc(sem("lat_squared"), 1)
                act.activation(xn[:, m, Q_LORA:], kvlat[:, m, 0:KV_LORA], ACT.Square, accum_out=ssq[:, 6 + m:7 + m])\
                   .then_inc(sem("lat_squared"), 1)
            act.wait_ge(sem("lat_squared"), 4)
            act.activation(ssq[:, 4:6], ssq[:, 4:6], ACT.Sqrt, bias=eps[:], scale=1.0 / Q_LORA).then_inc(sem("lat_rooted"), 1)
            act.activation(ssq[:, 6:8], ssq[:, 6:8], ACT.Sqrt, bias=eps[:], scale=1.0 / KV_LORA).then_inc(sem("lat_rooted"), 1)
            split_hi(9)
            act.wait_ge(ring_used, chunk_index("w_in", 4, O_DQ) + 1)
            for m in range(NM):
                project_copy(3, m, qkd[:, m, 0:SUB, :].rearrange("p a b -> p (a b)"), WD)
            for m in range(NM):
                act.wait_ge(sem("lat_turned"), m + 1)
                for i in range(2):
                    act.copy(latT[:, 4 * i:4 * i + 4, m * P:(m + 1) * P], v3(bank[2 * ((4 + m) % 4) + i][:], 4))\
                       .then_inc(sem("unit_copied"), 1)
            split_hi(10)
            split_hi(11)
            act.wait_ge(ring_used, chunk_index("w_in", 4, O_DK) + 1)
            for m in range(NM):
                project_copy(6, m, qkd[:, m, SUB:, :].rearrange("p a b -> p (a b)"), WD)
            act.wait_ge(sem("unit_copied"), 14)
            for m in range(NM):
                act.activation(tok_r[:, m * D:(m + 1) * D], qkd[:, m].rearrange("p a b -> p (a b)"), ACT.Square)\
                   .then_inc(sem("qkd_squared"), 1)
            split_hi(12)
            for m in range(NM):
                act.wait_ge(sem("qkd_summed"), m + 1)
                r = slice(8 + 16 * m, 24 + 16 * m)
                act.activation(ssq[:, r], ssq[:, r], ACT.Sqrt, bias=eps[:], scale=1.0 / DD).then_inc(sem("qkd_rooted"), 1)
            act.wait_ge(ring_used, chunk_index("w_uq", 4, 0) + 1)
            for i in range(2):
                for m in range(NM):
                    act.copy(qka[:, m, 4 * i:4 * i + 4, :].rearrange("p a b -> p (a b)"),
                             bank[2 * ((7 + i) % 4) + m][:, 0:4 * QK_A]).then_inc(sem("unit_copied"), 1)
            act.wait_ge(ring_used, chunk_index("w_ukv", 0, 0) + 1)
            for i in range(2):
                for m in range(NM):
                    b = bank[2 * ((9 + i) % 4) + m][:].rearrange("p (h d) -> p h d", h=4)
                    act.copy(qka[:, m, HA + 4 * i:HA + 4 * i + 4, 0:NOPE], b[:, :, 0:NOPE]).then_inc(sem("k_copied"), 1)
                    act.copy(va[:, m, 4 * i:4 * i + 4, :], b[:, :, NOPE:]).then_inc(sem("unit_copied"), 1)
            for m in range(NM):
                act.copy(qka[:, m, HA:, NOPE:], kvlat[:, m, KV_LORA:].unsqueeze(1).broadcast_to([P, HA, ROPE_A]))\
                   .then_inc(sem("k_copied"), 1)
            for m in range(NM):
                act.wait_ge(sem("qkd_turned"), m + 1)
                for i in range(2):
                    act.copy(dqkT[:, 4 * i:4 * i + 4, m * P:(m + 1) * P], v3(bank[2 * ((11 + m) % 4) + i][:], 4))\
                       .then_inc(sem("unit_copied"), 1)
            act.wait_ge(sem("k_copied"), 6)
            act.wait_ge(sem("unit_copied"), 22)
            for m in range(NM):
                if m:
                    act.wait_ge(sem("qka_summed"), m)
                act.activation(squares, qka[:, m].rearrange("p a b -> p (a b)"), ACT.Square).then_inc(sem("qka_squared"), 1)
            act.wait_ge(sem("qka_summed"), NM)
            for m in range(NM):
                act.activation(rstd[:, 16 * m + 8:16 * m + 24], ssq[:, 16 * m + 8:16 * m + 24], ACT.Sqrt, bias=eps[:],
                               scale=1.0 / QK_A).then_inc(sem("qka_rooted"), 1)
            act.wait_ge(sem("lambda_summed"), 1)
            act.activation(lam[:, 2:4], lam[:, 0:2], ACT.Exp).then_inc(sem("lambda_exped"), 1)
            split_hi(13)
            act.wait_ge(ring_used, chunk_index("w_in", 4, O_DV) + 1)
            for m in range(NM):
                project_copy(13, m, dv[:, m], WD)

            def exps(s):
                act.wait_ge(sem("maxed"), 2 * (s + 1))
                if s >= 2:
                    act.wait_ge(sem("probs_turned"), s - 1)
                for m in range(NM):
                    c = slice(0, P) if m == 0 else slice(P, 3 * P)
                    act.activation(probs[:, s % 2, c], scored[:, s % 2, c], ACT.Exp, bias=nmax[:, 2 * s + m:2 * s + m + 1],
                                   accum_out=sums[:, 2 * s + m:2 * s + m + 1]).then_inc(sem("exped"), 1)

            def probsT_copy(s):
                act.wait_ge(sem("probs_turned"), s + 1)
                if s >= 2:
                    act.wait_ge(sem("valued"), s - 1)
                act.copy(probsT[:, s % 2], bank[2 + s % 2][:, 0:3 * P]).then_inc(sem("probsT_copied"), 1)

            def gates_copy(s):
                if s % 4 == 3:
                    g = s // 4
                    act.wait_ge(ring_used, chunk_index("w_in", 4, O_GATE + g * HALF) + 1)
                    for m in range(NM):
                        act.activation(gates[:, m, g * HALF:(g + 1) * HALF], bank[6 + m][:], ACT.Copy,
                                       scale=rstd[:, m:m + 1]).then_inc(sem("gates_copied"), 1)

            act.wait_ge(sem("lat_ready"), 4)
            for lo, hi in ((0, SUB), (SUB, SUB + HA)):
                if lo:
                    for i in range(HA):
                        act.wait_ge(sem("qka_turned"), i + 1)
                        act.copy(qkaT[0:QK_A, 2 * i:2 * i + 2, :], v3(bank[i % 6][0:QK_A, :], 2)).then_inc(sem("qkaT_copied"), 1)
                for s in range(lo, hi + 1):
                    if s < hi:
                        exps(s)
                    if s - 1 >= lo:
                        probsT_copy(s - 1)
                    if s < hi:
                        gates_copy(s)
                        if s % 2 == 0:
                            split_hi(14 + s // 2)
                    if s == SUB + 1:
                        for m in range(NM):
                            act.wait_ge(sem("ob_diffed"), m + 1)
                            act.activation(tok_r[:, m * WD:(m + 1) * WD], o_b[:, m].rearrange("p a b -> p (a b)"),
                                           ACT.Square).then_inc(sem("ob_squared"), 1)
                    if s == SUB + 3:
                        act.wait_ge(sem("ob_summed"), NM)
                        act.activation(ssq[:, 40:40 + 2 * HD], ssq[:, 40:40 + 2 * HD], ACT.Sqrt, bias=eps[:],
                                       scale=1.0 / DV).then_inc(sem("ob_rooted"), 1)
            act.wait_ge(sem("scores"), SUB + HA)
            act.dma_start(b1_sb, b1).then_inc(sem("bias_landed"), 16)
            act.dma_start(b2_sb, b2).then_inc(sem("bias_landed"), 16)
            act.wait_ge(sem("qkd_turned"), NM)
            act.dma_start(g_ffn, gain(ffn_norm, D)).then_inc(sem("ffn_gain_landed"), 16)
            def oT_copy(i):
                act.wait_ge(sem("o_turned"), i + 1)
                dst = o_bT if i < 2 else o_aT
                act.copy(dst[:, :, (i % 2) * P:(i % 2 + 1) * P], v3(bank[i][:], 4)).then_inc(sem("oT_copied"), 1)

            oT_copy(0)
            oT_copy(1)
            act.wait_ge(sem("gates_copied"), 8)
            for m in range(NM):
                act.activation(gates[:, m], gates[:, m], ACT.Sigmoid).then_inc(sem("gates_ready"), 1)
            oT_copy(2)
            oT_copy(3)
            split_hi(22)
            for i in range(4):
                h, m = i // 2, i % 2
                act.wait_ge(sem("merged_turned"), i + 1)
                act.copy(featT[0][:, 4 * h:4 * h + 4, m * P:(m + 1) * P], v3(bank[4 + i][:], 4))\
                   .then_inc(sem("featT_hi"), 1)
            split_hi(23)
            for h in range(2):
                for m in range(NM):
                    act.wait_ge(sem("h_ready"), 2 * h + m + 1)
                    act.activation(gate_r[:, (2 * h + m) * HALF:(2 * h + m + 1) * HALF], acc[:, m, h * HALF:(h + 1) * HALF],
                                   ACT.Square, accum_out=ssq[:, 50 + 2 * h + m:51 + 2 * h + m]).then_inc(sem("h_squared"), 1)
            for i in range(4):
                h, m = i // 2, i % 2
                act.wait_ge(sem("t_turned"), i + 1)
                act.copy(tT[:, 4 * h:4 * h + 4, m * P:(m + 1) * P], v3(bank[4 + i][:], 4)).then_inc(sem("tT_copied"), 1)
            act.wait_ge(sem("h_summed"), 1)
            act.activation(ssq[:, 54:56], ssq[:, 54:56], ACT.Sqrt, bias=eps[:], scale=1.0 / D).then_inc(sem("h_rooted"), 1)
            act.wait_ge(sem("partials"), 1)
            act.copy(partial[:], bank[0][:, 0:SEQ]).then_inc(sem("partial_copied"), 1)
            def xT_copy():
                for i in range(2):
                    act.copy(xT[:, 4 * i:4 * i + 4, :], v3(bank[6 + i][:], 4)).then_inc(sem("xT_copied"), 1)

            act.wait_ge(sem("gathered"), 1)
            xT_copy()
            for m in range(NM):
                act.wait_ge(sem("top_negated"), m + 1)
                act.activation(expd_v[:, m], logit_v[:, m, 0:E], ACT.Exp, bias=negtop[:, m:m + 1]).then_inc(sem("router_exped"), 1)

            def pair(j, first=False):
                for f in range(2):
                    act.wait_ge(sem(f"glu_ready{f}"), j + 1)
                    act.activation(sig[:, f], glu[:, f], ACT.Sigmoid, scale=ALPHA).then_inc(sem(f"sig_ready{f}"), 1)
                    act.wait_ge(sem(f"act_turned{f}"), j + 1)
                    act.wait_ge(ring_used, JOB_CHUNKS * j + NHEAD)
                    act.copy(aT[f], v3(bank[6 + f][:], 4)).then_inc(sem(f"aT_copied{f}"), 1)
                act.wait_ge(sem("gated_turned"), j + 1)
                if not first:
                    act.wait_ge(sem("scattered"), 4 * j)
                else:
                    act.wait_ge(sem("weights_turned"), 1)
                act.copy(gatedT, bank[2][:, 0:SEQ]).then_inc(sem("gatedT_copied"), 1)
                if first:
                    act.copy(weightT[:], bank[2][0:E, SEQ:]).then_inc(sem("weightT_copied"), 1)
                act.wait_ge(ring_used, JOB_CHUNKS * j + NHEAD + JOB_CHUNKS)
                for h in range(2):
                    act.copy(y_sb[:, h * HALF:(h + 1) * HALF], bank[4 + h][:]).then_inc(sem("y_copied"), 1)
                act.wait_ge(sem("gathered"), j + 2)
                xT_copy()

            pair(0, first=True)
            with act.Fori(1, PAIRS) as j:
                pair(j)
            act.wait_ge(sem("counted"), 1)
            most = act.value_load(fullest_i[0:1, 0:1], min_val=0, max_val=SEQ)
            with act.Fori(1, ROUNDS) as r:
                with act.If(most > r * SLOTS):
                    with act.Fori(0, PAIRS) as p_:
                        pair(r * PAIRS + p_)

        @block.vector
        def _(dve):
            chain = [0]

            def link(ins):
                chain[0] += 1
                ins.then_inc(sem("dve_chain"), 1)
                dve.wait_ge(sem("dve_chain"), chain[0])

            tt, ts, stt = dve.tensor_tensor, dve.tensor_scalar, dve.scalar_tensor_tensor

            dve.memset(logit_v[:, :, E:], -SENTINEL).then_inc(sem("sentinels"), 1)
            dve.wait_ge(sem("gain_landed"), 16)
            for m in range(NM):
                dve.wait_ge(sem(f"x_landed{m}"), 16)
                tt(xn[:, m], acc[:, m], g_attn, ALU.mult).then_inc(sem("xg_ready"), 1)
            def split_lo(i, halves=(0, 1)):
                n = SPLIT[i]
                _, _, nk, _, cols = HEAD[n]
                hi, lo = split_views(i)
                dve.wait_ge(sem("hi_ready"), i + 1)
                for a in halves:
                    c = slice(a * nk * cols // 2, (a + 1) * nk * cols // 2)
                    tt(lo[:, c], slot(n, nk * cols)[:, c], hi[:, c], ALU.subtract).then_inc(sem("lo_ready"), 1)

            def turned_lo(i, k, m, b, before):
                dve.wait_ge(sem("featT_hi"), before + i + 1)
                c = slice(m * P, (m + 1) * P)
                tt(featT[1][:, k:k + 4, c], v3(bank[b][:], 4), featT[0][:, k:k + 4, c], ALU.subtract)\
                    .then_inc(sem("featT_ready"), 1)

            for i in range(4):
                turned_lo(i, 4 * (i % 2), i // 2, i, 0)
            split_lo(0)
            dve.wait_ge(sem("x_rooted"), 1)
            dve.reciprocal(rstd[:, 0:NM], ssq[:, 0:NM]).then_inc(sem("x_inverted"), 1)
            for i in range(1, 9):
                split_lo(i)
            dve.wait_ge(sem("small_landed"), 16 * SMALL)
            link(tt(scratch_m[:, 0:2 * DD], lam_in[:, 0:2 * DD], lam_in[:, 2 * DD:], ALU.mult))
            dve.tensor_reduce(lam[:, 0:2], v3(scratch_m[:, 0:2 * DD], 2), AX.X, ALU.add).then_inc(sem("lambda_summed"), 1)
            dve.wait_ge(sem("lat_rooted"), 2)
            dve.wait_ge(sem("lat_gain_landed"), 32)
            link(dve.reciprocal(rstd[:, 4:8], ssq[:, 4:8]))
            for m in range(NM):
                stt(qlat[:, m], qlat[:, m], rstd[:, 4 + m:5 + m], g_qlat, ALU.mult, ALU.mult).then_inc(sem("lat_ready"), 1)
                stt(kvlat[:, m, 0:KV_LORA], kvlat[:, m, 0:KV_LORA], rstd[:, 6 + m:7 + m], g_kvlat, ALU.mult, ALU.mult)\
                    .then_inc(sem("lat_ready"), 1)

            for i in range(9, 12):
                split_lo(i)
            for m in range(NM):
                dve.wait_ge(sem("qkd_squared"), m + 1)
                dve.tensor_reduce(ssq[:, 8 + 16 * m:24 + 16 * m], v3(tok_r[:, m * D:(m + 1) * D], 2 * SUB), AX.X, ALU.add)\
                   .then_inc(sem("qkd_summed"), 1)
            for m in range(NM):
                dve.wait_ge(sem("qkd_rooted"), m + 1)
                dve.wait_ge(sem("qkd_summed"), NM)
                r = rstd[:, 8 + 16 * m:24 + 16 * m]
                link(dve.reciprocal(r, ssq[:, 8 + 16 * m:24 + 16 * m]))
                norm_rotate(dve, "qkd", qkd, m, SUB, DD, r, g_qkd, DD, ROPE_A, gate_r)
            split_lo(12)
            for m in range(NM):
                dve.wait_ge(sem("qka_squared"), m + 1)
                dve.tensor_reduce(ssq[:, 8 + 16 * m:24 + 16 * m], v3(squares, 2 * HA), AX.X, ALU.add)\
                   .then_inc(sem("qka_summed"), 1)

            def scale_mask(s):
                dve.wait_ge(sem("scores"), s + 1)
                if s >= 2:
                    dve.wait_ge(sem("exped"), 2 * (s - 1))
                scale = DD ** -0.5 if s < SUB else QK_A ** -0.5
                stt(scored[:, s % 2], bank[s % 2][:, 0:3 * P], scale, mask[:], ALU.mult, ALU.add).then_inc(sem("scored"), 1)
                dve.wait_ge(sem("scored"), s + 1)
                for m in range(NM):
                    c = slice(0, P) if m == 0 else slice(P, 3 * P)
                    dve.tensor_reduce(nmax[:, 2 * s + m:2 * s + m + 1], scored[:, s % 2, c], AX.X, ALU.max, negate=True)\
                       .then_inc(sem("maxed"), 1)

            def head_out(s):
                dve.wait_ge(sem("exped"), 2 * (s + 1))
                link(dve.reciprocal(rsum[:, 2 * s:2 * s + 2], sums[:, 2 * s:2 * s + 2]))
                dve.wait_ge(sem("valued"), s + 1)
                n = DV if s < SUB else VA
                dst = o_raw[:, :, s, :] if s < SUB else o_a[:, :, s - SUB, :]
                tt(dst, v3(bank[4 + s % 2][:, 0:2 * n], 2), rsum[:, 2 * s:2 * s + 2].unsqueeze(2).broadcast_to([P, NM, n]),
                   ALU.mult).then_inc(sem("headed"), 1)

            split_lo(13)
            dve.wait_ge(sem("tables_ready"), TABLES)
            for s in range(SUB + 1):
                if s < SUB:
                    scale_mask(s)
                if s >= 1:
                    split_lo(14 + (s - 1) // 2, ((s - 1) % 2,))
                if s >= 1:
                    head_out(s - 1)
                if s < NM:
                    dve.wait_ge(sem("qka_rooted"), s + 1)
                    r = rstd[:, 8 + 16 * s:24 + 16 * s]
                    dve.reciprocal(r, r).then_inc(sem("qka_inverted"), 1)
            dve.wait_ge(sem("lambda_exped"), 1)
            link(tt(lam[:, 4:5], lam[:, 3:4], lam[:, 2:3], ALU.subtract))
            link(ts(lam[:, 5:6], lam[:, 4:5], -LAMBDA_INIT, None, ALU.add))
            link(ts(g_sub[:], g_sub[:], 1.0 - LAMBDA_INIT, None, ALU.mult))
            pairs = o_raw.rearrange("p m (h a) d -> p m h a d", a=2)

            def diff_piece(s):
                if s == SUB:
                    dve.wait_ge(sem("headed"), SUB)
                    dve.wait_ge(sem("qkd_turned"), NM)
                    for m in range(NM):
                        stt(o_b[:, m], pairs[:, m, :, 1], lam[:, 5:6], pairs[:, m, :, 0], ALU.mult, ALU.add)\
                            .then_inc(sem("ob_diffed"), 1)
                elif s == SUB + 2:
                    for m in range(NM):
                        dve.wait_ge(sem("ob_squared"), m + 1)
                        dve.tensor_reduce(ssq[:, 40 + HD * m:40 + HD * (m + 1)], v3(tok_r[:, m * WD:(m + 1) * WD], HD),
                                          AX.X, ALU.add).then_inc(sem("ob_summed"), 1)
                elif s in (SUB + 4, SUB + 5):
                    m = s - SUB - 4
                    if m == 0:
                        dve.wait_ge(sem("ob_rooted"), 1)
                        link(dve.reciprocal(rstd[:, 40:48], ssq[:, 40:48]))
                    r = rstd[:, 40 + HD * m:40 + HD * (m + 1)].unsqueeze(2).broadcast_to([P, HD, DV])
                    link(tt(o_b[:, m], o_b[:, m], r, ALU.mult))
                    tt(o_b[:, m], o_b[:, m], g_sub[:].unsqueeze(1).broadcast_to([P, HD, DV]), ALU.mult)\
                        .then_inc(sem("ob_ready"), 1)

            for s in range(SUB, SUB + HA + 1):
                if s < SUB + HA:
                    scale_mask(s)
                if s >= SUB + 1:
                    split_lo(14 + (s - 1) // 2, ((s - 1) % 2,))
                    head_out(s - 1)
                diff_piece(s)
            def gate(name, h, g0, b0):
                dve.wait_ge(ring_used, chunk_index(name, 0, h * HALF) + 1)
                for m in range(NM):
                    g = gates[:, m, g0 + h * HALF:g0 + (h + 1) * HALF]
                    tt(g, bank[b0 + m][:], g, ALU.mult).then_inc(sem("branch_gated"), 1)

            dve.wait_ge(sem("gates_ready"), NM)
            gate("w_bd", 0, D, 6)
            gate("w_bd", 1, D, 4)
            for h in range(2):
                gate("w_ba", h, 0, 2 * h)
                dve.wait_ge(sem("branch_gated"), 6 + 2 * h)
                for m in range(NM):
                    c = slice(h * HALF, (h + 1) * HALF)
                    tt(merged[:, m, c], gates[:, m, c], gates[:, m, D + c.start:D + c.stop], ALU.add)\
                        .then_inc(sem("merged_ready"), 1)
            split_lo(22)
            for i in range(4):
                turned_lo(i, 4 * (i // 2), i % 2, 4 + i, 4)
            split_lo(23)
            dve.wait_ge(sem("ffn_gain_landed"), 16)
            dve.wait_ge(sem("merged_turned"), 4)
            for h in range(2):
                dve.wait_ge(ring_used, chunk_index("w_out", 4, h * HALF) + 1)
                c = slice(h * HALF, (h + 1) * HALF)
                for m in range(NM):
                    tt(acc[:, m, c], bank[2 * h + m][:], acc[:, m, c], ALU.add).then_inc(sem("h_ready"), 1)
                for m in range(NM):
                    dve.wait_ge(sem("h_ready"), 2 * h + m + 1)
                    tt(t_sb[:, m, c], acc[:, m, c], g_ffn[:, c], ALU.mult).then_inc(sem("hg_ready"), 1)
            dve.wait_ge(sem("h_squared"), 4)
            tt(ssq[:, 54:56], ssq[:, 50:52], ssq[:, 52:54], ALU.add).then_inc(sem("h_summed"), 1)
            dve.wait_ge(sem("h_rooted"), 1)
            link(dve.reciprocal(rstd[:, 54:56], ssq[:, 54:56]))
            dve.wait_ge(sem("t_turned"), 4)
            for m in range(NM):
                ts(t_sb[:, m], t_sb[:, m], rstd[:, 54 + m:55 + m], None, ALU.mult).then_inc(sem("t_scaled"), 1)
            dve.wait_ge(sem("scores"), SUB + HA)
            dve.tensor_copy(pick, eye32[:, 0:2].unsqueeze(2).broadcast_to([E, 2, SLOTS])).then_inc(sem("pick_ready"), 1)
            dve.wait_ge(sem("logits"), 1)
            dve.wait_ge(sem("sentinels"), 1)
            for m in range(NM):
                link(stt(logit_v[:, m, 0:E], bank[1][:, m * E:(m + 1) * E], rstd[:, 54 + m:55 + m], b_rt[:],
                         ALU.mult, ALU.add))
                t8 = top[:, 8 * m:8 * m + 8]
                link(dve.max(t8, logit_v[:, m]))
                ts(negtop[:, m:m + 1], t8[:, 0:1], -1.0, None, ALU.mult).then_inc(sem("top_negated"), 1)
                dve.wait_ge(sem("top_negated"), m + 1)
                link(dve.memset(t8[:, TOP_K:8], -SENTINEL))
                link(dve.match_replace(marked_v[:, m], t8, logit_v[:, m], SENTINEL))
                ts(chosen_v[:, m], marked_v[:, m, 0:E], SENTINEL, None, ALU.is_ge).then_inc(sem("chosen"), 1)
            FAR = 1024.0
            iota_b = iota[:].unsqueeze(1).broadcast_to([P, 2, SLOTS])

            def spread(ap, parts=P):
                return ap.unsqueeze(2).broadcast_to([parts, 2, SLOTS])

            dve.wait_ge(sem("places"), 1)
            for m in range(NM):
                stt(marked_v[:, m, 0:E], bank[2][:, m * E:(m + 1) * E], FAR, chosen_v[:, m], ALU.add, ALU.mult)\
                    .then_inc(sem("placing"), 1)
            for m in range(NM):
                dve.wait_ge(sem("placing"), m + 1)
                ts(place_v[:, m, 0:E], marked_v[:, m, 0:E], -FAR, None, ALU.add).then_inc(sem("placed"), 1)
            for m in range(NM):
                dve.wait_ge(sem("placed"), m + 1)
                ins = tt(onehot[:, m], iota_b, spread(place_v[:, m, 0:2]), ALU.is_equal)
            ins.then_inc(sem("onehot_ready"), 1)
            for m in range(NM):
                dve.wait_ge(sem("router_exped"), m + 1)
                link(tt(expd_v[:, m], expd_v[:, m], chosen_v[:, m], ALU.mult))
                link(dve.tensor_reduce(gsum[:, m:m + 1], expd_v[:, m], AX.X, ALU.add))
                link(dve.reciprocal(grec[:, m:m + 1], gsum[:, m:m + 1]))
                ts(weight_v[:, m, 0:E], expd_v[:, m], grec[:, m:m + 1], None, ALU.mult).then_inc(sem("weights_ready"), 1)

            def onehots(j):
                for m in range(NM):
                    ins = tt(onehot[:, m], iota_b, spread(place_v[:, m, bass.ds(2 * j, 2)]), ALU.is_equal)
                return ins

            def picks(j):
                return dve.tensor_copy(pick, spread(eye32[:, bass.ds(2 * j, 2)], E))

            def pair(j, first=False):
                dve.wait_ge(sem("onehot_ready"), j + 1)
                if first:
                    dve.wait_ge(sem("weights_ready"), NM)
                else:
                    dve.wait_ge(sem("gated_turned"), j)
                for m in range(NM):
                    ins = tt(gated[:, m], onehot[:, m], spread(weight_v[:, m, bass.ds(2 * j, 2)]), ALU.mult)
                ins.then_inc(sem("gated_ready"), 1)
                dve.wait_ge(sem("gathered"), j + 1)
                dve.wait_ge(sem("gated_ready"), j + 1)
                onehots(j + 1).then_inc(sem("onehot_ready"), 1)
                for f in range(2):
                    dve.wait_ge(ring_used, JOB_CHUNKS * j + NHEAD + KD * (f + 1))
                    if not first:
                        dve.wait_ge(sem(f"act_turned{f}"), j)
                    ts(glu[:, f], bank[2 * f][:], LIMIT, None, ALU.min).then_inc(sem(f"glu_ready{f}"), 1)
                    ts(lin[:, f], bank[2 * f + 1][:], LIMIT, -LIMIT, ALU.min, ALU.max).then_inc(sem(f"lin_ready{f}"), 1)
                    dve.wait_ge(sem(f"glu_ready{f}"), j + 1)
                    dve.wait_ge(sem(f"lin_ready{f}"), 2 * j + 1)
                    stt(lin[:, f], lin[:, f], 1.0, glu[:, f], ALU.add, ALU.mult).then_inc(sem(f"lin_ready{f}"), 1)
                    dve.wait_ge(sem(f"lin_ready{f}"), 2 * j + 2)
                    dve.wait_ge(sem(f"sig_ready{f}"), j + 1)
                    tt(act_out[:, f], lin[:, f], sig[:, f], ALU.mult).then_inc(sem(f"act_ready{f}"), 1)
                picks(j + 1).then_inc(sem("pick_ready"), 1)
                if first:
                    dve.wait_ge(sem("counts"), 1)
                    link(dve.tensor_reduce(fullest[:, 0:1], bank[3][:, 0:E], AX.X, ALU.max))
                    dve.tensor_copy(fullest_i[:], fullest[:, 0:1]).then_inc(sem("counted"), 1)
                for i in range(2 * NM):
                    m, h = i // 2, i % 2
                    dve.wait_ge(sem("scattered"), 4 * j + i + 1)
                    a = acc[:, m, h * HALF:(h + 1) * HALF]
                    tt(a, bank[i][:], a, ALU.add).then_inc(sem("acc_added"), 1)

            pair(0, first=True)
            dve.memset(place_v[:, :, ROUNDS * E:], -FAR).then_inc(sem("place_pad"), 1)
            for m in range(NM):
                for r in range(1, ROUNDS):
                    ts(place_v[:, m, r * E:(r + 1) * E], marked_v[:, m, 0:E], -FAR - SLOTS * r, None, ALU.add)\
                        .then_inc(sem("placed"), 1)
                    dve.tensor_copy(weight_v[:, m, r * E:(r + 1) * E], weight_v[:, m, 0:E]).then_inc(sem("placed"), 1)
            dve.wait_ge(sem("placed"), NM + 2 * NM * (ROUNDS - 1))
            dve.wait_ge(sem("place_pad"), 1)
            with dve.Fori(1, PAIRS) as j:
                pair(j)
            dve.wait_ge(sem("acc_added"), 4 * PAIRS)
            most = dve.value_load(fullest_i[0:1, 0:1], min_val=0, max_val=SEQ)
            with dve.Fori(1, ROUNDS) as r:
                with dve.If(most > r * SLOTS):
                    with dve.Fori(0, PAIRS) as p_:
                        pair(r * PAIRS + p_)
                    dve.wait_ge(sem("acc_added"), 4 * PAIRS * (r + 1))
                    dve.sem_inc(sem("rounds_added"), 1)
            dve.sem_inc(sem("finished"), 1)


TABLES = 5
SMALL = 12


def rope_tables():
    cols = []
    for dim in (ROPE_A, DD):
        inv = (1.0 / (np.float32(10000.0) ** (np.arange(0, dim, 2, dtype=np.float32) / np.float32(dim)))).astype(np.float32)
        ang = np.arange(SEQ, dtype=np.float32)[:, None] * inv[None, :]
        cols += [np.cos(ang).astype(np.float32), np.sin(ang).astype(np.float32)]
    tabs = np.concatenate(cols, axis=1)
    return np.ascontiguousarray(tabs.reshape(NM, P, -1).transpose(1, 0, 2).reshape(P, -1))


_INS = ['x', 'attn_norm', 'w_in', 'mla_q_lat_norm', 'mla_kv_lat_norm', 'mla_w_uq', 'mla_w_ukv', 'mla_q_norm',
        'mla_k_norm', 'diff_q_norm', 'diff_k_norm', 'diff_lambda_q1', 'diff_lambda_k1', 'diff_lambda_q2',
        'diff_lambda_k2', 'diff_subln', 'w_branch_mla', 'w_branch_diff', 'w_out', 'ffn_norm', 'w_router',
        'b_router', 'w_mlp1', 'b_mlp1', 'w_mlp2', 'b_mlp2']


def kernel(**inputs):
    import concourse.bacc as _bacc
    from concourse.bass_utils import run_bass_kernel_spmd as _run

    nc = _bacc.Bacc("TRN2", target_bir_lowering=False, num_devices=1, dynamic_dma_scratch_size=1024)
    arrays, args = {}, []
    for name in _INS + ["rope"]:
        a = rope_tables() if name == "rope" else np.ascontiguousarray(inputs[name])[0]
        arrays[f"in_{name}"] = a
        args.append(nc.dram_tensor(f"in_{name}", a.shape, F32, kind="ExternalInput").ap())
    out = nc.dram_tensor("out_h", [SEQ, D], F32, kind="ExternalOutput").ap()
    build(nc, *args, out)
    r = _run(nc, [arrays], core_ids=[0])
    return r.results[0]["out_h"].reshape(1, SEQ, D)
```

```python
import math
from contextlib import ExitStack

import numpy as np

import concourse.bass as bass
from concourse import mybir

F32 = mybir.dt.float32
F32R = mybir.dt.float32r
I32 = mybir.dt.int32
ALU = mybir.AluOpType
ACT = mybir.ActivationFunctionType
AX = mybir.AxisListType

P = 128
SEQ, D = 256, 1024
NM = SEQ // P
KD = D // P
EPS = 1e-6

HA, NOPE, ROPE_A, VA = 8, 64, 32, 64
QK_A = NOPE + ROPE_A
Q_LORA, KV_LORA = 768, 256
KQ, KKV = Q_LORA // P, KV_LORA // P
HD, DD = 4, 64
SUB, DV = 2 * HD, 2 * DD
WA, WD = HA * VA, HD * DV
LAMBDA_INIT = 0.8 - 0.6 * math.exp(-0.3 * 0)

E, TOP_K, F = 32, 4, D
ALPHA, LIMIT = 1.702, 7.0
SLOTS = 64
ROUNDS = SEQ // SLOTS
PAIRS = E // 2
JOBS = ROUNDS * PAIRS
COLS = ROUNDS * E + 2

O_Q, O_KV = 0, Q_LORA
O_DQ = Q_LORA + KV_LORA + ROPE_A
O_DK, O_DV, O_GATE = O_DQ + WD, O_DQ + 2 * WD, O_DQ + 3 * WD
KVW = KV_LORA + ROPE_A
HALF = 512

RING, SLOT = 12, 2048
HEAD_RING = 8
BUFFERS = RING - 1 - HEAD_RING
EXTRA = 4
WIDE = RING + EXTRA
ONCE = (12, 2, 4, 7)
JOB_CHUNKS = 3 * KD
CYCLE = 2 * JOB_CHUNKS
assert CYCLE % WIDE == 0
BIG = 1e30
QKA_ORDER = (0, 4, 1, 5, 2, 6, 3, 7)
SENTINEL = 3e38
FAR = 1024.0


def head_chunks():
    out = []
    for c0, n in ((O_Q, Q_LORA // 2), (O_Q + Q_LORA // 2, Q_LORA // 2), (O_KV, KVW), (O_DQ, WD), (O_DK, WD)):
        out += [("w_in", k, KD // 2, c0, n) for k in (0, KD // 2)]
    out += [("w_uq", k, 2, 0, HA * QK_A) for k in range(0, KQ, 2)]
    out += [("w_ukv", 0, KKV, 0, HA * (NOPE + VA))]
    out += [("w_in", k, KD // 2, O_DV, WD) for k in (0, KD // 2)]
    for g in range(2 * D // HALF):
        out += [("w_in", k, KD // 2, O_GATE + g * HALF, HALF) for k in (0, KD // 2)]
    out += [("w_bd", 0, WD // P, h * HALF, HALF) for h in range(2)]
    out += [("w_ba", 0, WA // P, h * HALF, HALF) for h in range(2)]
    out += [("w_out", k, KD // 2, h * HALF, HALF) for h in range(2) for k in (0, KD // 2)]
    return out


HEAD = head_chunks()
NHEAD = len(HEAD)
SPLIT = [n for n, c in enumerate(HEAD) if c[0] not in ("w_uq", "w_ukv")]


def ring_place(n):
    return n - NHEAD - sum(c < n - NHEAD for c in ONCE)


def slot_of(n):
    if n < NHEAD:
        return n % HEAD_RING
    if n - NHEAD in ONCE:
        return WIDE + ONCE.index(n - NHEAD)
    s = ring_place(n) % WIDE
    if s < EXTRA:
        return RING + s
    return (NHEAD + s - EXTRA) % HEAD_RING if s < EXTRA + HEAD_RING else s - EXTRA


def lap_of(n):
    s = slot_of(n)
    if s >= WIDE:
        return 1
    return sum(slot_of(i) == s for i in range(min(n + 1, NHEAD))) + (0 if n < NHEAD else ring_place(n) // WIDE + 1)


def chunk_index(matrix, k, c0):
    return next(n for n, (w, k0, nk, c, _) in enumerate(HEAD) if (w, c) == (matrix, c0) and k0 <= k < k0 + nk)


def build(nc, x, attn_norm, w_in, q_lat_norm, kv_lat_norm, w_uq, w_ukv, q_norm, k_norm, dq_norm, dk_norm,
          lq1, lk1, lq2, lk2, subln, w_bmla, w_bdiff, w_out, ffn_norm, w_router, b_router,
          w1, b1, w2, b2, rope, out):
    ctx = ExitStack()
    with ctx:
        def sb(name, cols, dt=F32, parts=P):
            return ctx.enter_context(nc.sbuf_tensor(name, [parts, cols], dt))

        sems = {}

        def sem(name):
            if name not in sems:
                sems[name] = ctx.enter_context(nc.semaphore(name))
            return sems[name]

        with nc.sbuf_tensor("ring_s", [P, RING * SLOT], F32R) as ring_s, \
             nc.sbuf_tensor("feat_s", [P, KD * SEQ], F32R) as feat_s:
            pass
        ring = sb("ring", RING * SLOT)
        feat_r = sb("feat_r", KD * SEQ)
        acc_r = sb("acc_r", NM * D)
        tok_r = sb("tok_r", NM * D)
        gate_r = sb("gate_r", NM * 2 * D)
        lat_r = sb("lat_r", NM * (Q_LORA + KVW))
        qkd_r = sb("qkd_r", NM * 2 * WD)
        qka_r = sb("qka_r", NM * 2 * HA * QK_A)
        v_r = sb("v_r", NM * (WD + WA))
        latT_r = sb("latT_r", (KQ + KKV) * SEQ)
        qkT_r = sb("qkT_r", 2 * HA * SEQ)
        soft_r = sb("soft_r", 6 * 384)

        v3 = lambda t, a: t.rearrange("p (a b) -> p a b", a=a)
        acc = v3(acc_r[:], NM)
        xn = v3(tok_r[:], NM)
        featT = v3(feat_s[:], KD), v3(ring_s[:, (RING - 1) * SLOT:RING * SLOT], KD)
        gates = v3(gate_r[:], NM)
        g_attn, g_qlat, g_kvlat = gate_r[:, 0:D], gate_r[:, D:D + Q_LORA], gate_r[:, D + Q_LORA:D + Q_LORA + KV_LORA]
        qlat, kvlat = v3(lat_r[:, 0:NM * Q_LORA], NM), v3(lat_r[:, NM * Q_LORA:], NM)
        o_a = lat_r[:, 0:NM * WA].rearrange("p (m h d) -> p m h d", m=NM, h=HA)
        qkd = qkd_r[:].rearrange("p (m h d) -> p m h d", m=NM, h=2 * SUB)
        qka = qka_r[:].rearrange("p (m h d) -> p m h d", m=NM, h=2 * HA)
        dv, va = v3(v_r[:, 0:NM * WD], NM), v_r[:, NM * WD:].rearrange("p (m h d) -> p m h d", m=NM, h=HA)
        latT = v3(latT_r[:], KQ + KKV)
        o_raw = latT_r[:].rearrange("p (m h d) -> p m h d", m=NM, h=SUB)
        dqkT = v3(tok_r[:], SUB)
        qkaT = v3(qkT_r[:], 2 * HA)
        squares = qkT_r[:, 0:2 * HA * QK_A]
        o_b = qkd_r[:, 0:NM * WD].rearrange("p (m h d) -> p m h d", m=NM, h=HD)
        g_ffn = soft_r[:, 0:D]
        merged, t_sb, tT = xn, xn, v3(feat_r[:], KD)
        soft = v3(soft_r[:], 6)
        scored, probs, probsT = soft[:, 0:2], soft[:, 2:4], soft[:, 4:6]
        b1_sb, b2_sb = qkT_r[0:E, 0:2 * F], qkT_r[0:E, 2 * F:2 * F + D]
        hot_0 = 3 * D
        onehot = qkT_r[:, hot_0:hot_0 + NM * P].rearrange("p (m e s) -> p m e s", m=NM, e=2)
        gated = qkT_r[:, hot_0 + NM * P:hot_0 + 2 * NM * P].rearrange("p (m e s) -> p m e s", m=NM, e=2)
        gatedT = qkT_r[:, hot_0 + 2 * NM * P:hot_0 + 3 * NM * P]
        pick = qkT_r[0:E, hot_0 + 3 * NM * P:hot_0 + 3 * NM * P + P].rearrange("p (e s) -> p e s", e=2)
        xT = v3(feat_r[:, 0:KD * P], KD)
        glu, sig, lin, act_out = (v3(gate_r[:, i * D:(i + 1) * D], 2) for i in range(4))
        aT = [v3(soft_r[:, i * HALF:(i + 1) * HALF], 4) for i in range(2)]
        y_sb = soft_r[:, D:2 * D]

        fold = sb("fold", E)
        partial = sb("partial", SEQ)
        w_rt = sb("w_rt", KD * E)
        tab = sb("tab", NM * (ROPE_A + DD))
        g_qka, g_qkd = sb("g_qka", 2 * QK_A), sb("g_qkd", 2 * DD)
        g_sub, lam_in = sb("g_sub", DV), sb("lam_in", 4 * DD)
        b_rt = sb("b_rt", E)
        ident, before, ones = sb("ident", P), sb("before", P), sb("ones", P)
        mask = sb("mask", 3 * P)
        iota = sb("iota", SLOTS)
        eye32 = sb("eye32", COLS, parts=E)
        place, weight = sb("place", NM * COLS), sb("weight", NM * COLS)
        place_v, weight_v = v3(place[:], NM), v3(weight[:], NM)
        eps = sb("eps", 1)
        ssq = sb("ssq", 64)
        rstd = sb("rstd", 64)
        nmax, sums, rsum = (sb(n, 2 * (SUB + HA)) for n in ("nmax", "sums", "rsum"))
        lam = sb("lam", 8)
        logit = sb("logit", NM * (E + 8))
        logit_v = v3(logit[:], NM)
        marked = sb("marked", NM * (E + 8))
        marked_v = v3(marked[:], NM)
        top = sb("top", NM * 8)
        chosen, expd = sb("chosen", NM * E), sb("expd", NM * E)
        chosen_v, expd_v = v3(chosen[:], NM), v3(expd[:], NM)
        negtop, gsum, grec = sb("negtop", NM), sb("gsum", NM), sb("grec", NM)
        weightT = sb("weightT", SEQ, parts=E)
        fullest = sb("fullest", 2)
        fullest_i = sb("fullest_i", 1, I32)
        scratch_m = sb("scratch_m", 4 * DD)

        bank = [ctx.enter_context(nc.psum_tensor(f"bank{i}", [P, HALF], F32)) for i in range(8)]

        matrices = {"w_in": w_in, "w_uq": w_uq, "w_ukv": w_ukv, "w_bd": w_bdiff, "w_ba": w_bmla, "w_out": w_out}
        landed = [sem(f"landed{s}") for s in range(WIDE + len(ONCE))]
        ring_used = sem("ring_used")

        extra = [latT_r[:], qka_r[:, 0:SLOT], v_r[:], lat_r[:, 0:SLOT]]
        extra += [qkd_r[:], soft_r[:, 0:SLOT], gate_r[:, 0:SLOT], gate_r[:, SLOT:]]

        def slot(n, cols=SLOT):
            s = slot_of(n)
            return ring[:, s * SLOT:s * SLOT + cols] if s < RING else extra[s - RING]

        def head_view(n):
            _, _, nk, _, cols = HEAD[n]
            return v3(slot(n, nk * cols), nk)

        def split_views(i):
            n = SPLIT[i]
            _, _, nk, _, cols = HEAD[n]
            hi = (HEAD_RING + i % BUFFERS) * SLOT
            lo = slot_of(n) * SLOT
            return ring_s[:, hi:hi + nk * cols], ring_s[:, lo:lo + nk * cols]

        w1_v = w1.rearrange("e (k p) (g h n) -> e k p h g n", p=P, g=2, h=2)
        w2_v = w2.rearrange("e (k p) n -> e k p n", p=P)

        def load_expert_chunk(eng, n, c, pair):
            for a in range(2):
                if c < 2 * KD:
                    src = w1_v[2 * pair + a, c % KD, :, c // KD]
                    dst = slot(n).rearrange("p (e g n) -> p e g n", e=2, g=2)[:, a]
                else:
                    src = w2_v[2 * pair + a, c - 2 * KD]
                    dst = slot(n).rearrange("p (e n) -> p e n", e=2)[:, a]
                eng.dma_start(dst, src).then_inc(landed[slot_of(n)], 16)

        def gain(ap, n):
            return ap.rearrange("(a n) -> a n", a=1).broadcast_to([P, n])

        tab_v = tab[:].rearrange("p (m c) -> p m c", m=NM)

        def norm_rotate(eng, name, qk, m, n, width, r, gains, rot, tab0, tmp):
            t4 = qk[:, m]
            half = rot // 2
            x1, x2 = t4[:, :, width - rot:width - half], t4[:, :, width - half:width]
            cos = tab_v[:, m, tab0:tab0 + half].unsqueeze(1).broadcast_to([P, 2 * n, half])
            sin = tab_v[:, m, tab0 + half:tab0 + rot].unsqueeze(1).broadcast_to([P, 2 * n, half])
            nt = 2 * n * half
            a, b, c, d = (v3(tmp[:, i * nt:(i + 1) * nt], 2 * n) for i in range(4))
            tt = eng.tensor_tensor
            tt(t4, t4, r.unsqueeze(2).broadcast_to([P, 2 * n, width]), ALU.mult).then_inc(sem(f"{name}_normed"), 1)
            eng.wait_ge(sem(f"{name}_normed"), m + 1)
            for i in range(2):
                g = gains[:, i * width:(i + 1) * width].unsqueeze(1).broadcast_to([P, n, width])
                tt(t4[:, i * n:(i + 1) * n], t4[:, i * n:(i + 1) * n], g, ALU.mult).then_inc(sem(f"{name}_scaled"), 1)
            eng.wait_ge(sem(f"{name}_scaled"), 2 * m + 2)
            for dst, x_, by in ((a, x1, cos), (b, x2, sin), (c, x2, cos), (d, x1, sin)):
                tt(dst, x_, by, ALU.mult).then_inc(sem(f"{name}_rotated"), 1)
            eng.wait_ge(sem(f"{name}_rotated"), 4 * m + 4)
            tt(x1, a, b, ALU.subtract).then_inc(sem(f"{name}_ready"), 1)
            tt(x2, c, d, ALU.add).then_inc(sem(f"{name}_ready"), 1)

        block = ctx.enter_context(nc.Block())

        @block.sync
        def _(sp):
            sp.dma_start(acc[:, 0], x[0:P, :]).then_inc(sem("x_landed0"), 16)
            sp.dma_start(acc[:, 1], x[P:2 * P, :]).then_inc(sem("x_landed1"), 16)
            small = [(tab[:], rope), (g_qkd[:, 0:DD], gain(dq_norm, DD)), (g_qkd[:, DD:2 * DD], gain(dk_norm, DD)),
                     (g_qka[:, 0:QK_A], gain(q_norm, QK_A)), (g_qka[:, QK_A:2 * QK_A], gain(k_norm, QK_A)),
                     (lam_in[:, 0:DD], gain(lq1, DD)), (lam_in[:, DD:2 * DD], gain(lq2, DD)),
                     (lam_in[:, 2 * DD:3 * DD], gain(lk1, DD)), (lam_in[:, 3 * DD:4 * DD], gain(lk2, DD)),
                     (g_sub[:], gain(subln, DV)), (b_rt[:], gain(b_router, E)),
                     (v3(w_rt[:], KD), w_router.rearrange("(k p) n -> p k n", p=P))]
            assert len(small) == SMALL
            for n, (name, k0, nk, c0, cols) in enumerate(HEAD):
                if n == 4:
                    sp.dma_start(g_qlat, gain(q_lat_norm, Q_LORA)).then_inc(sem("lat_gain_landed"), 16)
                    sp.dma_start(g_kvlat, gain(kv_lat_norm, KV_LORA)).then_inc(sem("lat_gain_landed"), 16)
                if 6 <= n < 6 + SMALL // 2:
                    for dst, src in small[2 * (n - 6):2 * (n - 6) + 2]:
                        sp.dma_start(dst, src).then_inc(sem("small_landed"), 16)
                if n >= HEAD_RING:
                    sp.wait_ge(ring_used, n - HEAD_RING + 1)
                src = matrices[name].rearrange("(k p) n -> p k n", p=P)
                for a in range(2):
                    ks = slice(a * nk // 2, (a + 1) * nk // 2)
                    sp.dma_start(head_view(n)[:, ks, :], src[:, k0 + ks.start:k0 + ks.stop, c0:c0 + cols])\
                      .then_inc(landed[slot_of(n)], 16)

            def load_pair(i, pair, cycle):
                for c in range(JOB_CHUNKS):
                    n = NHEAD + i * JOB_CHUNKS + c
                    if n - NHEAD in ONCE[1:] and isinstance(cycle, int):
                        continue
                    place = ring_place(n)
                    if not isinstance(cycle, int):
                        sp.wait_ge(ring_used, CYCLE * cycle + n - WIDE + 1)
                        n += CYCLE
                    elif place >= WIDE:
                        last = next(i for i in range(NHEAD, n)
                                    if i - NHEAD not in ONCE and ring_place(i) == place - WIDE)
                        sp.wait_ge(ring_used, last + 1)
                    elif n - NHEAD == ONCE[0]:
                        sp.wait_ge(sem("o_turned"), NM)
                    elif place >= EXTRA:
                        sp.wait_ge(ring_used, min(NHEAD + place - EXTRA - HEAD_RING + 1, NHEAD))
                    elif place == 0:
                        sp.wait_ge(sem("ob_diffed"), NM)
                    elif place == 1:
                        sp.wait_ge(sem("qka_turned"), HA)
                    elif place == 2:
                        sp.wait_ge(sem("valued"), SUB + HA)
                    else:
                        sp.wait_ge(sem("o_turned"), 4)
                    load_expert_chunk(sp, n, c, pair)

            for i in range(2):
                load_pair(i, i, 0)
            with sp.Fori(1, PAIRS // 2) as j:
                for i in range(2):
                    load_pair(i, 2 * j + i, j)
            for i in range(2 * NM):
                m, c = i % 2, slice((i // 2) * HALF, (i // 2 + 1) * HALF)
                sp.wait_ge(sem("acc_added"), 4 * (PAIRS - 1) + i + 1)
                sp.dma_start(out[m * P:(m + 1) * P, c], acc[:, m, c]).then_inc(sem("stored"), 16)
            sp.wait_ge(sem("stored"), 16 * 2 * NM)
            sp.wait_ge(sem("counted"), 1)
            most = sp.value_load(fullest_i[0:1, 0:1], min_val=0, max_val=SEQ)
            with sp.Fori(1, ROUNDS) as r:
                with sp.If(most > r * SLOTS):
                    with sp.Fori(0, PAIRS // 2) as j:
                        for i in range(2):
                            load_pair(i, 2 * j + i, r * (PAIRS // 2) + j)
                    sp.wait_ge(sem("rounds_added"), r)
                    for m in range(NM):
                        sp.dma_start(out[m * P:(m + 1) * P, :], acc[:, m]).then_inc(sem("stored"), 16)
                    sp.wait_ge(sem("stored"), 16 * 2 * NM + 16 * NM * r)
                    sp.sem_inc(sem("rounds_stored"), 1)

        @block.gpsimd
        def _(pool):
            pool.memset(ident[:], 0.0).then_inc(sem("const_set"), 1)
            pool.memset(before[:], 1.0).then_inc(sem("const_set"), 1)
            pool.memset(ones[:], 1.0).then_inc(sem("const_set"), 1)
            pool.memset(mask[:], 0.0).then_inc(sem("const_set"), 1)
            pool.memset(eye32[:], 0.0).then_inc(sem("const_set"), 1)
            pool.memset(eps[:], EPS).then_inc(sem("const_set"), 1)
            pool.memset(weight[:], 0.0).then_inc(sem("const_set"), 1)
            pool.memset(fold[:], 0.0).then_inc(sem("const_set"), 1)
            pool.wait_ge(sem("const_set"), 8)
            pool.affine_select(out=ident[:], in_=ident[:], compare_op=ALU.not_equal, fill=1.0, base=0,
                               pattern=[[-1, P]], channel_multiplier=1).then_inc(sem("ident_ready"), 1)
            for c in (0, 2 * P):
                pool.affine_select(out=mask[:, c:c + P], in_=mask[:, c:c + P], compare_op=ALU.is_ge, fill=-BIG,
                                   base=0, pattern=[[-1, P]], channel_multiplier=1).then_inc(sem("tables_ready"), 1)
            pool.affine_select(out=before[:], in_=before[:], compare_op=ALU.is_gt, fill=0.0, base=0,
                               pattern=[[1, P]], channel_multiplier=-1).then_inc(sem("tables_ready"), 1)
            pool.affine_select(out=eye32[:, 0:ROUNDS * E], in_=eye32[:, 0:ROUNDS * E], compare_op=ALU.not_equal,
                               fill=1.0, base=0, pattern=[[0, ROUNDS], [-1, E]], channel_multiplier=1)\
                .then_inc(sem("tables_ready"), 1)
            for q in range(4):
                pool.affine_select(out=fold[:], in_=fold[:], compare_op=ALU.not_equal, fill=1.0, base=-E * q,
                                   pattern=[[-1, E]], channel_multiplier=1).then_inc(sem("folded"), 1)
                pool.wait_ge(sem("folded"), q + 1)
            pool.iota(iota[:], pattern=[[1, SLOTS]], base=int(FAR), channel_multiplier=0,
                      allow_small_or_imprecise_dtypes=True).then_inc(sem("tables_ready"), 1)
            for m in range(NM):
                pool.wait_ge(sem("qka_inverted"), m + 1)
                norm_rotate(pool, "qka", qka, m, HA, QK_A, rstd[:, 8 + 16 * m:24 + 16 * m], g_qka, ROPE_A, 0, qkT_r)
            pool.wait_ge(sem("ob_inverted"), 1)
            for m in range(NM):
                r = rstd[:, 40 + HD * m:40 + HD * (m + 1)].unsqueeze(2).broadcast_to([P, HD, DV])
                pool.tensor_tensor(o_b[:, m], o_b[:, m], r, ALU.mult).then_inc(sem("ob_normed"), 1)
            pool.wait_ge(sem("sub_gain_scaled"), 1)
            for m in range(NM):
                pool.wait_ge(sem("ob_normed"), m + 1)
                pool.tensor_tensor(o_b[:, m], o_b[:, m], g_sub[:].unsqueeze(1).broadcast_to([P, HD, DV]), ALU.mult)\
                    .then_inc(sem("ob_ready"), 1)

        @block.tensor
        def _(pe):
            def turn(dst, src, rows=P):
                return pe.transpose(dst, src, ident[0:rows, 0:rows])

            def arrive(n):
                pe.wait_ge(landed[slot_of(n)], 32 * lap_of(n))

            def split_part(banks, n, ks, ms=range(NM)):
                name, k0, nk, _, cols = HEAD[n]
                i = SPLIT.index(n)
                first = 4 if name == "w_ba" else 0
                kmax = KD if name in ("w_in", "w_out") else 4
                pe.wait_ge(sem("lo_ready"), 2 * i + (2 if ks[-1] == k0 + nk - 1 else 1))
                hi, lo = (v3(v, nk) for v in split_views(i))
                for m in ms:
                    for k in ks:
                        for left, right in ((0, hi), (0, lo), (1, hi)):
                            mm = pe.matmul(banks[m][:, 0:cols], featT[left][:, first + k, m * P:(m + 1) * P], right[:, k - k0, :],
                                           start=(k == 0 and left == 0 and right is hi),
                                           stop=(k == kmax - 1 and left == 1), skip_group_check=True)
                if ks[-1] == k0 + nk - 1 and ms[-1] == NM - 1:
                    mm.then_inc(ring_used, 1)

            def split_product(banks, chunks):
                for n in chunks:
                    split_part(banks, n, range(HEAD[n][1], HEAD[n][1] + HEAD[n][2]))

            pe.wait_ge(sem("ident_ready"), 1)
            for m in range(NM):
                pe.wait_ge(sem("xg_ready"), m + 1)
                for k in range(KD):
                    mm = turn(bank[2 * m + k // 4][:, (k % 4) * P:(k % 4 + 1) * P], xn[:, m, k * P:(k + 1) * P])
                    if k % 4 == 3:
                        mm.then_inc(sem("xgT_turned"), 1)

            def unit(u):
                if u >= 4:
                    pe.wait_ge(sem("unit_copied"), 2 * (u - 3))
                return bank[2 * (u % 4)], bank[2 * (u % 4) + 1]

            def project(u, c0):
                i = chunk_index("w_in", 0, c0)
                split_product(unit(u), (i, i + 1))

            for m in range(NM):
                pe.wait_ge(sem("featT_ready"), 2 * (m + 1))
                split_part(unit(0), 0, range(KD // 2), (m,))
            split_part(unit(0), 1, range(KD // 2, KD))
            project(1, O_Q + Q_LORA // 2)
            project(2, O_KV)
            project(3, O_DQ)
            for m in range(NM):
                b = unit(4 + m)
                pe.wait_ge(sem("lat_ready"), 2 * (m + 1))
                for k in range(KQ + KKV):
                    src = qlat[:, m, k * P:(k + 1) * P] if k < KQ else kvlat[:, m, (k - KQ) * P:(k - KQ + 1) * P]
                    mm = turn(b[k // 4][:, (k % 4) * P:(k % 4 + 1) * P], src)
                mm.then_inc(sem("lat_turned"), 1)
            project(6, O_DK)
            bq = unit(7), unit(8)
            pe.wait_ge(sem("unit_copied"), 2 * 6)
            n0 = chunk_index("w_uq", 0, 0)
            HQ = HA * QK_A // 2
            for i in range(KQ // 2):
                arrive(n0 + i)
                w = head_view(n0 + i)
                for h, b in enumerate(bq):
                    for m in range(NM):
                        for k in (2 * i, 2 * i + 1):
                            mm = pe.matmul(b[m][:, 0:HQ], latT[:, k, m * P:(m + 1) * P], w[:, k - 2 * i, h * HQ:(h + 1) * HQ],
                                           start=(k == 0), stop=(k == KQ - 1), skip_group_check=True)
                mm.then_inc(ring_used, 1)
            n0 = chunk_index("w_ukv", 0, 0)
            arrive(n0)
            w = head_view(n0)
            for h in range(2):
                b = unit(9 + h)
                for m in range(NM):
                    for k in range(KKV):
                        mm = pe.matmul(b[m][:], latT[:, KQ + k, m * P:(m + 1) * P], w[:, k, h * HALF:(h + 1) * HALF],
                                       start=(k == 0), stop=(k == KKV - 1), skip_group_check=True)
            mm.then_inc(ring_used, 1)
            for m in range(NM):
                b = unit(11 + m)
                pe.wait_ge(sem("qkd_ready"), 2 * (m + 1))
                for i in range(SUB):
                    mm = turn(b[i // 4][:, (i % 4) * P:(i % 4 + 1) * P],
                              qkd[:, m, 2 * i:2 * i + 2, :].rearrange("p a b -> p (a b)"))
                mm.then_inc(sem("qkd_turned"), 1)
            def scores(s):
                if s >= 2:
                    pe.wait_ge(sem("scored"), s - 1)
                b = bank[s % 2]
                for m in range(NM):
                    if s < SUB:
                        lo = DD * (s % 2)
                        q = dqkT[lo:lo + DD, s // 2, m * P:(m + 1) * P]
                        k = dqkT[lo:lo + DD, SUB // 2 + s // 2, 0:(m + 1) * P]
                    else:
                        q = qkaT[0:QK_A, s - SUB, m * P:(m + 1) * P]
                        k = qkaT[0:QK_A, HA + s - SUB, 0:(m + 1) * P]
                    mm = pe.matmul(b[:, m * P:(2 * m + 1) * P], q, k, start=(m == 0), stop=True, skip_group_check=True)
                mm.then_inc(sem("scores"), 1)

            def probs_turn(s):
                if s == 0:
                    pe.wait_ge(sem("unit_copied"), 2 * 14)
                pe.wait_ge(sem("exped"), 2 * (s + 1))
                if s >= 2:
                    pe.wait_ge(sem("probsT_copied"), s - 1)
                for i in range(3):
                    mm = turn(bank[2 + s % 2][:, i * P:(i + 1) * P], probs[:, s % 2, i * P:(i + 1) * P])
                mm.then_inc(sem("probs_turned"), 1)

            def values(s):
                pe.wait_ge(sem("probsT_copied"), s + 1)
                if s >= 2:
                    pe.wait_ge(sem("headed"), s - 1)
                n = DV if s < SUB else VA
                b = bank[4 + s % 2]

                def v_of(m):
                    return dv[:, m, (s // 2) * DV:(s // 2 + 1) * DV] if s < SUB else va[:, m, s - SUB, :]

                pT = probsT[:, s % 2]
                pe.matmul(b[:, 0:n], pT[:, 0:P], v_of(0), start=True, stop=True, skip_group_check=True)
                pe.matmul(b[:, n:2 * n], pT[:, P:2 * P], v_of(0), start=True, stop=False, skip_group_check=True)
                pe.matmul(b[:, n:2 * n], pT[:, 2 * P:3 * P], v_of(1), start=False, stop=True, skip_group_check=True)\
                  .then_inc(sem("valued"), 1)

            def gate_part(s, m):
                g, q = s // 4, s % 4
                n = chunk_index("w_in", 0, O_GATE + g * HALF) + q // 2
                if q == 0 and m == 0 and g >= 1:
                    pe.wait_ge(sem("gates_copied"), 2 * g)
                split_part((bank[6], bank[7]), n, (2 * q, 2 * q + 1), (m,))

            HEADS = SUB + HA

            def o_b_turn(m):
                pe.wait_ge(sem("ob_ready"), m + 1)
                pe.wait_ge(sem("scored"), HEADS - 1 + m)
                for i in range(HD):
                    mm = turn(bank[m][:, i * P:(i + 1) * P], o_b[:, m, i, :])
                mm.then_inc(sem("o_turned"), 1)

            def step(s, first, last):
                if s < last:
                    if s > 0:
                        scores(s)
                    if s == SUB:
                        for half in range(2):
                            pe.wait_ge(sem(f"qkaT_copied{half}"), HA // 2)
                    if s == HEADS - 1:
                        o_b_turn(0)
                    gate_part(s, 0)
                if s > first:
                    probs_turn(s - 1)
                if s < last:
                    gate_part(s, 1)
                if s > first:
                    values(s - 1)

            n0 = chunk_index("w_in", 0, O_DV)
            split_part(unit(13), n0, range(KD // 2))
            pe.wait_ge(sem("unit_copied"), 2 * 13)
            scores(0)
            split_part(unit(13), n0 + 1, range(KD // 2, KD))
            for s in range(SUB + 1):
                step(s, 0, SUB)
            pe.wait_ge(sem("qka_ready"), 2 * NM)
            pe.wait_ge(sem("headed"), SUB)
            pe.wait_ge(sem("gates_copied"), 4)
            for p_, i in enumerate(QKA_ORDER):
                for a in range(2):
                    for m in range(NM):
                        mm = turn(bank[p_][0:QK_A, (2 * a + m) * P:(2 * a + m + 1) * P], qka[:, m, 2 * i + a, :])
                mm.then_inc(sem("qka_turned"), 1)
            for half in range(2):
                pe.wait_ge(sem(f"qkaT_copied{half}"), 1)
            for s in range(SUB, HEADS):
                step(s, SUB, HEADS)

            probs_turn(HEADS - 1)
            o_b_turn(1)
            values(HEADS - 1)
            pe.wait_ge(sem("gates_copied"), 8)
            for m in range(NM):
                pe.wait_ge(sem("featT_ready"), 5 + m)
                split_part((bank[6], bank[7]), chunk_index("w_bd", 0, 0), range(HD), (m,))
            pe.wait_ge(sem("headed"), HEADS)
            for m in range(NM):
                for i in range(HD):
                    mm = turn(bank[2 + m][:, i * P:(i + 1) * P],
                              o_a[:, m, 2 * i:2 * i + 2, :].rearrange("p a b -> p (a b)"))
                mm.then_inc(sem("o_turned"), 1)
            split_product((bank[4], bank[5]), (chunk_index("w_bd", 0, HALF),))
            pe.wait_ge(sem("featT_ready"), 8)
            def turn_half(src, h, done, ready):
                for m in range(NM):
                    pe.wait_ge(ready, 2 * h + m + 1)
                    for i in range(4):
                        k = 4 * h + i
                        mm = turn(bank[4 + 2 * h + m][:, i * P:(i + 1) * P], src[:, m, k * P:(k + 1) * P])
                    mm.then_inc(done, 1)

            split_product((bank[0], bank[1]), (chunk_index("w_ba", 0, 0),))
            split_part((bank[2], bank[3]), chunk_index("w_ba", 0, HALF), range(HD), (0,))
            turn_half(merged, 0, sem("merged_turned"), sem("merged_ready"))
            split_part((bank[2], bank[3]), chunk_index("w_ba", 0, HALF), range(HD), (1,))
            n = chunk_index("w_out", 0, 0)
            pe.wait_ge(sem("featT_ready"), 10)
            split_part((bank[0], bank[1]), n, range(KD // 2), (0,))
            turn_half(merged, 1, sem("merged_turned"), sem("merged_ready"))
            split_part((bank[0], bank[1]), n, range(KD // 2), (1,))
            pe.wait_ge(sem("featT_ready"), 12)
            split_product((bank[0], bank[1]), (n + 1,))
            split_product((bank[2], bank[3]), (n + 2, n + 3))

            def start_u(f, j):
                pe.wait_ge(sem("pick_ready"), j + 1)
                for g in range(2):
                    c0 = g * F + f * HALF
                    pe.matmul(bank[2 * f + g][:], pick.rearrange("p e s -> p (e s)"), b1_sb[:, c0:c0 + HALF],
                              start=True, stop=False, skip_group_check=True)

            for h in range(2):
                turn_half(t_sb, h, sem("t_turned"), sem("hg_ready"))
            pe.wait_ge(sem("small_landed"), 16 * SMALL)
            wr = v3(w_rt[:], KD)
            for i in range(2):
                pe.wait_ge(sem("tT_copied"), 2 * (i + 1))
                for q in range(4):
                    k = 4 * i + q
                    mm = pe.matmul(bank[0][q * E:(q + 1) * E, 0:SEQ], wr[:, k, :], tT[:, k, :],
                                   start=(i == 0), stop=(i == 1), skip_group_check=True)
            mm.then_inc(sem("partials"), 1)
            pe.wait_ge(sem("partial_copied"), 1)
            pe.wait_ge(sem("tables_ready"), TABLES)
            for m in range(NM):
                mm = pe.matmul(bank[1][:, m * E:(m + 1) * E], partial[:, m * P:(m + 1) * P], fold[:],
                               start=True, stop=True, skip_group_check=True)
            mm.then_inc(sem("logits"), 1)
            pe.wait_ge(sem("logits_read"), NM)
            pe.wait_ge(sem("bias_landed"), 32)
            start_u(0, 0)
            pe.wait_ge(sem("chosen"), NM)
            pe.matmul(bank[2][:, 0:E], before[:], chosen_v[:, 0], start=True, stop=True, skip_group_check=True)
            pe.matmul(bank[2][:, E:2 * E], ones[:], chosen_v[:, 0], start=True, stop=False, skip_group_check=True)
            pe.matmul(bank[2][:, E:2 * E], before[:], chosen_v[:, 1], start=False, stop=True, skip_group_check=True)\
              .then_inc(sem("places"), 1)

            def weights_turn():
                for m in range(NM):
                    mm = pe.matmul(bank[3][:, 0:E], ones[:], chosen_v[:, m], start=(m == 0), stop=(m == 1),
                                   skip_group_check=True)
                mm.then_inc(sem("counts"), 1)
                for m in range(NM):
                    mm = turn(bank[2][0:E, SEQ + m * P:SEQ + (m + 1) * P], weight_v[:, m, 0:E])
                mm.then_inc(sem("weights_turned"), 1)

            def gather():
                for k in range(KD):
                    for m in range(NM):
                        mm = pe.matmul(bank[6 + k // 4][:, (k % 4) * P:(k % 4 + 1) * P], t_sb[:, m, k * P:(k + 1) * P],
                                       onehot[:, m].rearrange("p e s -> p (e s)"),
                                       start=(m == 0), stop=(m == 1), skip_group_check=True)
                    if k % 4 == 3:
                        mm.then_inc(sem("gathered"), 1)

            def pair_arrive(i, cycle, c):
                if isinstance(cycle, int):
                    n = NHEAD + i * JOB_CHUNKS + c
                    pe.wait_ge(landed[slot_of(n)], 32 * lap_of(n))
                else:
                    n = NHEAD + CYCLE + i * JOB_CHUNKS + c
                    pe.wait_ge(landed[slot_of(n)], 32 * (CYCLE // WIDE) * cycle + 32 * (lap_of(n) - CYCLE // WIDE))
                return slot(n)

            def turn_act(half):
                for c in range(4):
                    mm = turn(bank[6 + half][:, c * P:(c + 1) * P], act_out[:, half, c * P:(c + 1) * P])
                mm.then_inc(sem(f"act_turned{half}"), 1)

            def pair(i, cycle, first=False, second=False):
                j = 2 * cycle + i
                for f in range(2):
                    if not (first and f == 0):
                        if not first:
                            pe.wait_ge(sem("acc_added"), 4 * j - 2 + 2 * f)
                        start_u(f, j)
                    for k in range(KD):
                        if f == 0 and k % 4 == 0:
                            pe.wait_ge(sem("xT_copied"), 2 * j + k // 4 + 1)
                        w = pair_arrive(i, cycle, f * KD + k).rearrange("p (e g n) -> p e g n", e=2, g=2)
                        for g, b in enumerate((bank[2 * f], bank[2 * f + 1])):
                            for e in range(2):
                                mm = pe.matmul(b[e * SLOTS:(e + 1) * SLOTS, :], xT[:, k, e * SLOTS:(e + 1) * SLOTS],
                                               w[:, e, g, :], start=False, stop=(k == KD - 1), skip_group_check=True)
                        mm.then_inc(ring_used, 1)
                        if f == 1 and k == 5:
                            pe.wait_ge(sem("act_ready0"), j + 1)
                            turn_act(0)
                for k in range(KD):
                    if k % 4 == 0:
                        pe.wait_ge(sem(f"aT_copied{k // 4}"), j + 1)
                    w = pair_arrive(i, cycle, 2 * KD + k).rearrange("p (e h n) -> p e h n", e=2, h=2)
                    for h in range(2):
                        for e in range(2):
                            mm = pe.matmul(bank[4 + h][e * SLOTS:(e + 1) * SLOTS, :],
                                           aT[k // 4][:, k % 4, e * SLOTS:(e + 1) * SLOTS], w[:, e, h, :],
                                           start=(k == 0), stop=(k == KD - 1), skip_group_check=True)
                        if k == KD - 1 and h == 0:
                            mm.then_inc(sem("y_half"), 1)
                    mm.then_inc(ring_used, 1)
                    if k == 2:
                        pe.wait_ge(sem("act_ready1"), j + 1)
                        turn_act(1)
                        pe.wait_ge(sem("gated_ready"), j + 1)
                        for m in range(NM):
                            mm = turn(bank[2][:, m * P:(m + 1) * P], gated[:, m].rearrange("p e s -> p (e s)"))
                        mm.then_inc(sem("gated_turned"), 1)
                        if first:
                            weights_turn()
                    if k == 3:
                        pe.wait_ge(sem("aT_copied1"), j + 1)
                        pe.wait_ge(sem("onehot_ready"), j + 2)
                        gather()
                pe.wait_ge(sem("gatedT_copied"), j + 1)
                if first:
                    pe.wait_ge(sem("weightT_copied"), 1)
                    pe.wait_ge(sem("counted"), 1)
                for h in range(2):
                    pe.wait_ge(sem(f"y_copied{h}"), j + 1)
                    for m in range(NM):
                        if second:
                            pe.matmul(bank[2 * h + m][:], weightT[:, m * P:(m + 1) * P], b2_sb[:, h * HALF:(h + 1) * HALF],
                                      start=True, stop=False, skip_group_check=True)
                        pe.matmul(bank[2 * h + m][:], gatedT[:, m * P:(m + 1) * P], y_sb[:, h * HALF:(h + 1) * HALF],
                                  start=not second, stop=True, skip_group_check=True).then_inc(sem("scattered"), 1)

            pe.wait_ge(sem("onehot_ready"), 1)
            pe.wait_ge(sem("t_scaled"), 2)
            gather()
            pair(0, 0, first=True)
            pair(1, 0, second=True)
            with pe.Fori(1, PAIRS // 2) as j:
                pair(0, j)
                pair(1, j)
            most = pe.value_load(fullest_i[0:1, 0:1], min_val=0, max_val=SEQ)
            with pe.Fori(1, ROUNDS) as r:
                with pe.If(most > r * SLOTS):
                    with pe.Fori(0, PAIRS // 2) as j:
                        pair(0, r * (PAIRS // 2) + j)
                        pair(1, r * (PAIRS // 2) + j)

        @block.scalar
        def _(act):
            act.dma_start(g_attn, gain(attn_norm, D)).then_inc(sem("gain_landed"), 16)
            act.wait_ge(sem("const_set"), 8)

            def x_square(m):
                act.wait_ge(sem(f"x_landed{m}"), 16)
                act.activation(qkd_r[:, m * D:(m + 1) * D], acc[:, m], ACT.Square, accum_out=ssq[:, m:m + 1])\
                   .then_inc(sem("x_squared"), 1)

            x_square(0)
            def split_hi(i):
                n = SPLIT[i]
                act.wait_ge(landed[slot_of(n)], 32 * lap_of(n))
                if i >= BUFFERS:
                    act.wait_ge(ring_used, SPLIT[i - BUFFERS] + 1)
                _, _, nk, _, cols = HEAD[n]
                act.copy(split_views(i)[0], slot(n, nk * cols)).then_inc(sem("hi_ready"), 1)

            for i in range(4):
                act.wait_ge(sem("xgT_turned"), i + 1)
                act.copy(featT[0][:, 4 * (i % 2):4 * (i % 2) + 4, (i // 2) * P:(i // 2 + 1) * P], v3(bank[i][:], 4))\
                   .then_inc(sem("featT_hi"), 1)
                if i == 1:
                    split_hi(0)
            split_hi(1)
            x_square(1)
            split_hi(2)
            act.wait_ge(sem("x_squared"), NM)
            act.activation(ssq[:, 0:NM], ssq[:, 0:NM], ACT.Sqrt, bias=eps[:], scale=1.0 / D).then_inc(sem("x_rooted"), 1)
            act.wait_ge(sem("x_inverted"), 1)

            def project_copy(u, m, dst, n):
                act.activation(dst, bank[2 * (u % 4) + m][:, 0:n], ACT.Copy, scale=rstd[:, m:m + 1])\
                   .then_inc(sem("unit_copied"), 1)

            act.wait_ge(sem("xgT_turned"), 4)
            for u, c0 in enumerate((O_Q, O_Q + Q_LORA // 2, O_KV)):
                split_hi(2 * u + 3)
                act.wait_ge(ring_used, chunk_index("w_in", 4, c0) + 1)
                for m in range(NM):
                    if u < 2:
                        project_copy(u, m, qlat[:, m, u * Q_LORA // 2:(u + 1) * Q_LORA // 2], Q_LORA // 2)
                    else:
                        project_copy(u, m, kvlat[:, m, :], KVW)
                split_hi(2 * u + 4)
            act.wait_ge(sem("unit_copied"), 6)
            for m in range(NM):
                act.activation(xn[:, m, 0:Q_LORA], qlat[:, m], ACT.Square, accum_out=ssq[:, 4 + m:5 + m])\
                   .then_inc(sem("lat_squared"), 1)
                act.activation(xn[:, m, Q_LORA:], kvlat[:, m, 0:KV_LORA], ACT.Square, accum_out=ssq[:, 6 + m:7 + m])\
                   .then_inc(sem("lat_squared"), 1)
            act.wait_ge(sem("lat_squared"), 4)
            act.activation(ssq[:, 4:6], ssq[:, 4:6], ACT.Sqrt, bias=eps[:], scale=1.0 / Q_LORA).then_inc(sem("lat_rooted"), 1)
            act.activation(ssq[:, 6:8], ssq[:, 6:8], ACT.Sqrt, bias=eps[:], scale=1.0 / KV_LORA).then_inc(sem("lat_rooted"), 1)
            split_hi(9)
            act.wait_ge(ring_used, chunk_index("w_in", 4, O_DQ) + 1)
            for m in range(NM):
                project_copy(3, m, qkd[:, m, 0:SUB, :].rearrange("p a b -> p (a b)"), WD)
            for m in range(NM):
                act.wait_ge(sem("lat_turned"), m + 1)
                for i in range(2):
                    act.copy(latT[:, 4 * i:4 * i + 4, m * P:(m + 1) * P], v3(bank[2 * ((4 + m) % 4) + i][:], 4))\
                       .then_inc(sem("unit_copied"), 1)
            split_hi(10)
            split_hi(11)
            act.wait_ge(ring_used, chunk_index("w_in", 4, O_DK) + 1)
            for m in range(NM):
                project_copy(6, m, qkd[:, m, SUB:, :].rearrange("p a b -> p (a b)"), WD)
            act.wait_ge(sem("unit_copied"), 14)
            for m in range(NM):
                act.activation(tok_r[:, m * D:(m + 1) * D], qkd[:, m].rearrange("p a b -> p (a b)"), ACT.Square)\
                   .then_inc(sem("qkd_squared"), 1)
            split_hi(12)
            for m in range(NM):
                act.wait_ge(sem("qkd_summed"), m + 1)
                r = slice(8 + 16 * m, 24 + 16 * m)
                act.activation(ssq[:, r], ssq[:, r], ACT.Sqrt, bias=eps[:], scale=1.0 / DD).then_inc(sem("qkd_rooted"), 1)
            act.wait_ge(ring_used, chunk_index("w_uq", 4, 0) + 1)
            for i in range(2):
                for m in range(NM):
                    act.copy(qka[:, m, 4 * i:4 * i + 4, :].rearrange("p a b -> p (a b)"),
                             bank[2 * ((7 + i) % 4) + m][:, 0:4 * QK_A]).then_inc(sem("unit_copied"), 1)
            act.wait_ge(ring_used, chunk_index("w_ukv", 0, 0) + 1)
            for i in range(2):
                for m in range(NM):
                    b = bank[2 * ((9 + i) % 4) + m][:].rearrange("p (h d) -> p h d", h=4)
                    act.copy(qka[:, m, HA + 4 * i:HA + 4 * i + 4, 0:NOPE], b[:, :, 0:NOPE]).then_inc(sem("k_copied"), 1)
                    act.copy(va[:, m, 4 * i:4 * i + 4, :], b[:, :, NOPE:]).then_inc(sem("unit_copied"), 1)
            for m in range(NM):
                act.copy(qka[:, m, HA:, NOPE:], kvlat[:, m, KV_LORA:].unsqueeze(1).broadcast_to([P, HA, ROPE_A]))\
                   .then_inc(sem("k_copied"), 1)
            for m in range(NM):
                act.wait_ge(sem("qkd_turned"), m + 1)
                for i in range(2):
                    act.copy(dqkT[:, 4 * i:4 * i + 4, m * P:(m + 1) * P], v3(bank[2 * ((11 + m) % 4) + i][:], 4))\
                       .then_inc(sem("unit_copied"), 1)
            act.wait_ge(sem("k_copied"), 6)
            act.wait_ge(sem("unit_copied"), 22)
            for m in range(NM):
                if m:
                    act.wait_ge(sem("qka_summed"), m)
                act.activation(squares, qka[:, m].rearrange("p a b -> p (a b)"), ACT.Square).then_inc(sem("qka_squared"), 1)
            act.wait_ge(sem("qka_summed"), NM)
            for m in range(NM):
                act.activation(rstd[:, 16 * m + 8:16 * m + 24], ssq[:, 16 * m + 8:16 * m + 24], ACT.Sqrt, bias=eps[:],
                               scale=1.0 / QK_A).then_inc(sem("qka_rooted"), 1)
            act.wait_ge(sem("lambda_summed"), 1)
            act.activation(lam[:, 2:4], lam[:, 0:2], ACT.Exp).then_inc(sem("lambda_exped"), 1)
            split_hi(13)
            def oT_copy(i):
                act.wait_ge(sem("o_turned"), i + 1)
                act.wait_ge(ring_used, chunk_index("w_bd", 0, 0))
                k = 4 * (i // 2)
                act.copy(featT[0][:, k:k + 4, (i % 2) * P:(i % 2 + 1) * P], v3(bank[i][:], 4)).then_inc(sem("featT_hi"), 1)

            def exps(s):
                act.wait_ge(sem("maxed"), 2 * (s + 1))
                if s >= 2:
                    act.wait_ge(sem("probs_turned"), s - 1)
                for m in range(NM):
                    c = slice(0, P) if m == 0 else slice(P, 3 * P)
                    act.activation(probs[:, s % 2, c], scored[:, s % 2, c], ACT.Exp, bias=nmax[:, 2 * s + m:2 * s + m + 1],
                                   accum_out=sums[:, 2 * s + m:2 * s + m + 1]).then_inc(sem("exped"), 1)

            def probsT_copy(s):
                act.wait_ge(sem("probs_turned"), s + 1)
                if s >= 2:
                    act.wait_ge(sem("valued"), s - 1)
                act.copy(probsT[:, s % 2], bank[2 + s % 2][:, 0:3 * P]).then_inc(sem("probsT_copied"), 1)

            def gates_copy(s):
                if s % 4 == 3:
                    g = s // 4
                    act.wait_ge(ring_used, chunk_index("w_in", 4, O_GATE + g * HALF) + 1)
                    for m in range(NM):
                        act.activation(gates[:, m, g * HALF:(g + 1) * HALF], bank[6 + m][:], ACT.Copy,
                                       scale=rstd[:, m:m + 1]).then_inc(sem("gates_copied"), 1)

            act.wait_ge(sem("lat_ready"), 4)
            for lo, hi in ((0, SUB), (SUB, SUB + HA)):
                if lo:
                    for p_ in range(0, HA, 2):
                        i = QKA_ORDER[p_]
                        act.wait_ge(sem("qka_turned"), p_ + 1)
                        act.copy(qkaT[0:QK_A, 2 * i:2 * i + 2, :], v3(bank[p_][0:QK_A, :], 2)).then_inc(sem("qkaT_copied0"), 1)
                for s in range(lo, hi + 1):
                    if s < hi:
                        exps(s)
                    if s == 0:
                        act.wait_ge(ring_used, chunk_index("w_in", 4, O_DV) + 1)
                        for m in range(NM):
                            project_copy(13, m, dv[:, m], WD)
                    if s - 1 >= lo:
                        probsT_copy(s - 1)
                    if s >= SUB + HA - 1 and lo:
                        oT_copy(s - (SUB + HA - 1))
                    if s < hi:
                        gates_copy(s)
                        if s % 2 == 0:
                            split_hi(14 + s // 2)
                    if s == SUB + 1:
                        for m in range(NM):
                            act.wait_ge(sem("ob_diffed"), m + 1)
                            act.activation(tok_r[:, m * WD:(m + 1) * WD], o_b[:, m].rearrange("p a b -> p (a b)"),
                                           ACT.Square).then_inc(sem("ob_squared"), 1)
                    if s == SUB + 3:
                        act.wait_ge(sem("ob_summed"), NM)
                        act.activation(ssq[:, 40:40 + 2 * HD], ssq[:, 40:40 + 2 * HD], ACT.Sqrt, bias=eps[:],
                                       scale=1.0 / DV).then_inc(sem("ob_rooted"), 1)
            act.wait_ge(sem("scores"), SUB + HA)
            act.dma_start(b1_sb, b1).then_inc(sem("bias_landed"), 16)
            act.dma_start(b2_sb, b2).then_inc(sem("bias_landed"), 16)
            act.wait_ge(sem("valued"), SUB + HA)
            act.dma_start(g_ffn, gain(ffn_norm, D)).then_inc(sem("ffn_gain_landed"), 16)
            split_hi(22)
            act.wait_ge(sem("gates_copied"), 8)
            for m in range(NM):
                act.activation(gates[:, m], gates[:, m], ACT.Sigmoid).then_inc(sem("gates_ready"), 1)
            oT_copy(2)
            oT_copy(3)
            split_hi(23)
            split_hi(24)
            split_hi(25)
            for i in range(4):
                h, m = i // 2, i % 2
                act.wait_ge(sem("merged_turned"), i + 1)
                act.copy(featT[0][:, 4 * h:4 * h + 4, m * P:(m + 1) * P], v3(bank[4 + i][:], 4))\
                   .then_inc(sem("featT_hi"), 1)
            act.wait_ge(sem("merged_ready"), 2 * NM)
            for c in ONCE[2:]:
                load_expert_chunk(act, NHEAD + c, c, 0)
            split_hi(26)
            split_hi(27)
            def tT_copy(i):
                h, m = i // 2, i % 2
                act.wait_ge(sem("t_turned"), i + 1)
                act.copy(tT[:, 4 * h:4 * h + 4, m * P:(m + 1) * P], v3(bank[4 + i][:], 4)).then_inc(sem("tT_copied"), 1)

            for h in range(2):
                if h:
                    tT_copy(0)
                    tT_copy(1)
                for m in range(NM):
                    act.wait_ge(sem("h_ready"), 2 * h + m + 1)
                    if h:
                        act.wait_ge(sem("h_squared"), m + 1)
                    act.activation(soft_r[:, D + m * HALF:D + (m + 1) * HALF], acc[:, m, h * HALF:(h + 1) * HALF],
                                   ACT.Square, accum_out=ssq[:, 50 + 2 * h + m:51 + 2 * h + m]).then_inc(sem("h_squared"), 1)
            tT_copy(2)
            tT_copy(3)
            act.wait_ge(sem("h_summed"), 1)
            act.activation(ssq[:, 54:56], ssq[:, 54:56], ACT.Sqrt, bias=eps[:], scale=1.0 / D).then_inc(sem("h_rooted"), 1)
            act.wait_ge(sem("h_inverted"), 1)
            for m in range(NM):
                act.activation(t_sb[:, m], t_sb[:, m], ACT.Copy, scale=rstd[:, 54 + m:55 + m]).then_inc(sem("t_scaled"), 1)
            act.wait_ge(sem("hg_ready"), 4)
            act.wait_ge(sem("h_squared"), 4)
            load_expert_chunk(act, NHEAD + ONCE[1], ONCE[1], 0)

            def xT_copy(j):
                for i in range(2):
                    act.wait_ge(sem("gathered"), 2 * j + i + 1)
                    act.copy(xT[:, 4 * i:4 * i + 4, :], v3(bank[6 + i][:], 4)).then_inc(sem("xT_copied"), 1)

            xT_copy(0)
            for m in range(NM):
                act.wait_ge(sem("top_negated"), m + 1)
                act.activation(expd_v[:, m], logit_v[:, m, 0:E], ACT.Exp, bias=negtop[:, m:m + 1]).then_inc(sem("router_exped"), 1)

            def pair(j, first=False):
                for f in range(2):
                    act.wait_ge(sem(f"glu_ready{f}"), j + 1)
                    act.activation(sig[:, f], glu[:, f], ACT.Sigmoid, scale=ALPHA).then_inc(sem(f"sig_ready{f}"), 1)
                    act.wait_ge(sem(f"act_turned{f}"), j + 1)
                    act.wait_ge(ring_used, JOB_CHUNKS * j + NHEAD)
                    act.copy(aT[f], v3(bank[6 + f][:], 4)).then_inc(sem(f"aT_copied{f}"), 1)
                act.wait_ge(sem("gated_turned"), j + 1)
                if not first:
                    act.wait_ge(sem("scattered"), 4 * j)
                else:
                    act.wait_ge(sem("weights_turned"), 1)
                act.copy(gatedT, bank[2][:, 0:SEQ]).then_inc(sem("gatedT_copied"), 1)
                if first:
                    act.copy(weightT[:], bank[2][0:E, SEQ:]).then_inc(sem("weightT_copied"), 1)
                xT_copy(j + 1)
                act.wait_ge(sem("y_half"), j + 1)
                act.copy(y_sb[:, 0:HALF], bank[4][:]).then_inc(sem("y_copied0"), 1)

            pair(0, first=True)
            with act.Fori(1, PAIRS) as j:
                pair(j)
            act.wait_ge(sem("counted"), 1)
            most = act.value_load(fullest_i[0:1, 0:1], min_val=0, max_val=SEQ)
            with act.Fori(1, ROUNDS) as r:
                with act.If(most > r * SLOTS):
                    with act.Fori(0, PAIRS) as p_:
                        pair(r * PAIRS + p_)

        @block.vector
        def _(dve):
            chain = [0]

            def link(ins):
                chain[0] += 1
                ins.then_inc(sem("dve_chain"), 1)
                dve.wait_ge(sem("dve_chain"), chain[0])

            tt, ts, stt = dve.tensor_tensor, dve.tensor_scalar, dve.scalar_tensor_tensor

            dve.memset(logit_v[:, :, E:], -SENTINEL).then_inc(sem("sentinels"), 1)
            dve.wait_ge(sem("gain_landed"), 16)
            for m in range(NM):
                dve.wait_ge(sem(f"x_landed{m}"), 16)
                tt(xn[:, m], acc[:, m], g_attn, ALU.mult).then_inc(sem("xg_ready"), 1)
            def split_lo(i, halves=(0, 1)):
                n = SPLIT[i]
                _, _, nk, _, cols = HEAD[n]
                hi, lo = split_views(i)
                dve.wait_ge(sem("hi_ready"), i + 1)
                for a in halves:
                    c = slice(a * nk * cols // 2, (a + 1) * nk * cols // 2)
                    tt(lo[:, c], slot(n, nk * cols)[:, c], hi[:, c], ALU.subtract).then_inc(sem("lo_ready"), 1)

            def turned_lo(i, k, m, b, before):
                dve.wait_ge(sem("featT_hi"), before + i + 1)
                c = slice(m * P, (m + 1) * P)
                tt(featT[1][:, k:k + 4, c], v3(bank[b][:], 4), featT[0][:, k:k + 4, c], ALU.subtract)\
                    .then_inc(sem("featT_ready"), 1)

            for i in range(4):
                turned_lo(i, 4 * (i % 2), i // 2, i, 0)
                if i == 1:
                    split_lo(0)
            for i in range(1, 9):
                if i == 3:
                    dve.wait_ge(sem("x_rooted"), 1)
                    dve.reciprocal(rstd[:, 0:NM], ssq[:, 0:NM]).then_inc(sem("x_inverted"), 1)
                split_lo(i)
            dve.wait_ge(sem("small_landed"), 16 * SMALL)
            link(tt(scratch_m[:, 0:2 * DD], lam_in[:, 0:2 * DD], lam_in[:, 2 * DD:], ALU.mult))
            dve.tensor_reduce(lam[:, 0:2], v3(scratch_m[:, 0:2 * DD], 2), AX.X, ALU.add).then_inc(sem("lambda_summed"), 1)
            dve.wait_ge(sem("lat_rooted"), 2)
            dve.wait_ge(sem("lat_gain_landed"), 32)
            link(dve.reciprocal(rstd[:, 4:8], ssq[:, 4:8]))
            for m in range(NM):
                stt(qlat[:, m], qlat[:, m], rstd[:, 4 + m:5 + m], g_qlat, ALU.mult, ALU.mult).then_inc(sem("lat_ready"), 1)
                stt(kvlat[:, m, 0:KV_LORA], kvlat[:, m, 0:KV_LORA], rstd[:, 6 + m:7 + m], g_kvlat, ALU.mult, ALU.mult)\
                    .then_inc(sem("lat_ready"), 1)

            for i in range(9, 12):
                split_lo(i)
            for m in range(NM):
                dve.wait_ge(sem("qkd_squared"), m + 1)
                dve.tensor_reduce(ssq[:, 8 + 16 * m:24 + 16 * m], v3(tok_r[:, m * D:(m + 1) * D], 2 * SUB), AX.X, ALU.add)\
                   .then_inc(sem("qkd_summed"), 1)
            for m in range(NM):
                dve.wait_ge(sem("qkd_rooted"), m + 1)
                dve.wait_ge(sem("qkd_summed"), NM)
                r = rstd[:, 8 + 16 * m:24 + 16 * m]
                link(dve.reciprocal(r, ssq[:, 8 + 16 * m:24 + 16 * m]))
                norm_rotate(dve, "qkd", qkd, m, SUB, DD, r, g_qkd, DD, ROPE_A, gate_r)
            split_lo(12)
            for m in range(NM):
                dve.wait_ge(sem("qka_squared"), m + 1)
                dve.tensor_reduce(ssq[:, 8 + 16 * m:24 + 16 * m], v3(squares, 2 * HA), AX.X, ALU.add)\
                   .then_inc(sem("qka_summed"), 1)

            def scale_mask(s):
                dve.wait_ge(sem("scores"), s + 1)
                if s >= 2:
                    dve.wait_ge(sem("exped"), 2 * (s - 1))
                scale = DD ** -0.5 if s < SUB else QK_A ** -0.5
                stt(scored[:, s % 2], bank[s % 2][:, 0:3 * P], scale, mask[:], ALU.mult, ALU.add).then_inc(sem("scored"), 1)
                dve.wait_ge(sem("scored"), s + 1)
                for m in range(NM):
                    c = slice(0, P) if m == 0 else slice(P, 3 * P)
                    dve.tensor_reduce(nmax[:, 2 * s + m:2 * s + m + 1], scored[:, s % 2, c], AX.X, ALU.max, negate=True)\
                       .then_inc(sem("maxed"), 1)

            def head_out(s):
                dve.wait_ge(sem("exped"), 2 * (s + 1))
                link(dve.reciprocal(rsum[:, 2 * s:2 * s + 2], sums[:, 2 * s:2 * s + 2]))
                dve.wait_ge(sem("valued"), s + 1)
                n = DV if s < SUB else VA
                dst = o_raw[:, :, s, :] if s < SUB else o_a[:, :, s - SUB, :]
                tt(dst, v3(bank[4 + s % 2][:, 0:2 * n], 2), rsum[:, 2 * s:2 * s + 2].unsqueeze(2).broadcast_to([P, NM, n]),
                   ALU.mult).then_inc(sem("headed"), 1)

            dve.wait_ge(sem("tables_ready"), TABLES)
            for s in range(SUB + 1):
                if s < SUB:
                    scale_mask(s)
                if s == 0:
                    split_lo(13)
                if s >= 1:
                    split_lo(14 + (s - 1) // 2, ((s - 1) % 2,))
                if s >= 1:
                    head_out(s - 1)
                if s < NM:
                    dve.wait_ge(sem("qka_rooted"), s + 1)
                    r = rstd[:, 8 + 16 * s:24 + 16 * s]
                    dve.reciprocal(r, r).then_inc(sem("qka_inverted"), 1)
            for p_ in range(1, HA, 2):
                i = QKA_ORDER[p_]
                dve.wait_ge(sem("qka_turned"), p_ + 1)
                dve.tensor_copy(qkaT[0:QK_A, 2 * i:2 * i + 2, :], v3(bank[p_][0:QK_A, :], 2)).then_inc(sem("qkaT_copied1"), 1)
            dve.wait_ge(sem("lambda_exped"), 1)
            link(tt(lam[:, 4:5], lam[:, 3:4], lam[:, 2:3], ALU.subtract))
            link(ts(lam[:, 5:6], lam[:, 4:5], -LAMBDA_INIT, None, ALU.add))
            ts(g_sub[:], g_sub[:], 1.0 - LAMBDA_INIT, None, ALU.mult).then_inc(sem("sub_gain_scaled"), 1)
            pairs = o_raw.rearrange("p m (h a) d -> p m h a d", a=2)

            def diff_piece(s):
                if s == SUB:
                    dve.wait_ge(sem("headed"), SUB)
                    dve.wait_ge(sem("qkd_turned"), NM)
                    for m in range(NM):
                        stt(o_b[:, m], pairs[:, m, :, 1], lam[:, 5:6], pairs[:, m, :, 0], ALU.mult, ALU.add)\
                            .then_inc(sem("ob_diffed"), 1)
                elif s == SUB + 2:
                    for m in range(NM):
                        dve.wait_ge(sem("ob_squared"), m + 1)
                        dve.tensor_reduce(ssq[:, 40 + HD * m:40 + HD * (m + 1)], v3(tok_r[:, m * WD:(m + 1) * WD], HD),
                                          AX.X, ALU.add).then_inc(sem("ob_summed"), 1)
                elif s == SUB + 4:
                    dve.wait_ge(sem("ob_rooted"), 1)
                    dve.reciprocal(rstd[:, 40:48], ssq[:, 40:48]).then_inc(sem("ob_inverted"), 1)

            for s in range(SUB, SUB + HA + 1):
                if s < SUB + HA:
                    scale_mask(s)
                if s >= SUB + 1:
                    split_lo(14 + (s - 1) // 2, ((s - 1) % 2,))
                    if s == SUB + HA:
                        for m in range(NM):
                            turned_lo(m, 0, m, m, 4)
                    head_out(s - 1)
                diff_piece(s)
            split_lo(22)
            def gate(name, h, g0, b0):
                dve.wait_ge(ring_used, chunk_index(name, 0, h * HALF) + 1)
                for m in range(NM):
                    g = gates[:, m, g0 + h * HALF:g0 + (h + 1) * HALF]
                    tt(g, bank[b0 + m][:], g, ALU.mult).then_inc(sem("branch_gated"), 1)

            for m in range(NM):
                turned_lo(2 + m, 4, m, 2 + m, 4)
            dve.wait_ge(sem("gates_ready"), NM)
            gate("w_bd", 0, D, 6)
            split_lo(23)
            gate("w_bd", 1, D, 4)
            split_lo(24)
            for h in range(2):
                gate("w_ba", h, 0, 2 * h)
                dve.wait_ge(sem("branch_gated"), 6 + 2 * h)
                for m in range(NM):
                    c = slice(h * HALF, (h + 1) * HALF)
                    tt(merged[:, m, c], gates[:, m, c], gates[:, m, D + c.start:D + c.stop], ALU.add)\
                        .then_inc(sem("merged_ready"), 1)
                if h == 1:
                    split_lo(25)
                for m in range(NM):
                    turned_lo(2 * h + m, 4 * h, m, 4 + 2 * h + m, 8)
            split_lo(26)
            split_lo(27)
            dve.wait_ge(sem("ffn_gain_landed"), 16)
            dve.wait_ge(sem("merged_turned"), 4)
            for h in range(2):
                dve.wait_ge(ring_used, chunk_index("w_out", 4, h * HALF) + 1)
                c = slice(h * HALF, (h + 1) * HALF)
                for m in range(NM):
                    tt(acc[:, m, c], bank[2 * h + m][:], acc[:, m, c], ALU.add).then_inc(sem("h_ready"), 1)
                for m in range(NM):
                    dve.wait_ge(sem("h_ready"), 2 * h + m + 1)
                    tt(t_sb[:, m, c], acc[:, m, c], g_ffn[:, c], ALU.mult).then_inc(sem("hg_ready"), 1)
            dve.wait_ge(sem("h_squared"), 4)
            tt(ssq[:, 54:56], ssq[:, 50:52], ssq[:, 52:54], ALU.add).then_inc(sem("h_summed"), 1)
            dve.wait_ge(sem("partials"), 1)
            dve.tensor_copy(partial[:], bank[0][:, 0:SEQ]).then_inc(sem("partial_copied"), 1)
            dve.wait_ge(sem("h_rooted"), 1)
            dve.reciprocal(rstd[:, 54:56], ssq[:, 54:56]).then_inc(sem("h_inverted"), 1)
            dve.wait_ge(sem("h_inverted"), 1)
            dve.wait_ge(sem("scores"), SUB + HA)
            dve.tensor_copy(pick, eye32[:, 0:2].unsqueeze(2).broadcast_to([E, 2, SLOTS])).then_inc(sem("pick_ready"), 1)
            dve.wait_ge(sem("logits"), 1)
            dve.wait_ge(sem("sentinels"), 1)
            t8 = [top[:, 8 * m:8 * m + 8] for m in range(NM)]
            for m in range(NM):
                stt(logit_v[:, m, 0:E], bank[1][:, m * E:(m + 1) * E], rstd[:, 54 + m:55 + m], b_rt[:],
                    ALU.mult, ALU.add).then_inc(sem("logits_read"), 1)
            for m in range(NM):
                dve.wait_ge(sem("logits_read"), m + 1)
                dve.max(t8[m], logit_v[:, m]).then_inc(sem("topped"), 1)
            for m in range(NM):
                dve.wait_ge(sem("topped"), m + 1)
                ts(negtop[:, m:m + 1], t8[m][:, 0:1], -1.0, None, ALU.mult).then_inc(sem("top_negated"), 1)
            for m in range(NM):
                dve.wait_ge(sem("top_negated"), m + 1)
                dve.memset(t8[m][:, TOP_K:8], -SENTINEL).then_inc(sem("top_cut"), 1)
            for m in range(NM):
                dve.wait_ge(sem("top_cut"), m + 1)
                dve.match_replace(marked_v[:, m], t8[m], logit_v[:, m], SENTINEL).then_inc(sem("matched"), 1)
            for m in range(NM):
                dve.wait_ge(sem("matched"), m + 1)
                ts(chosen_v[:, m], marked_v[:, m, 0:E], SENTINEL, None, ALU.is_ge).then_inc(sem("chosen"), 1)
            iota_b = iota[:].unsqueeze(1).broadcast_to([P, 2, SLOTS])

            def spread(ap, parts=P):
                return ap.unsqueeze(2).broadcast_to([parts, 2, SLOTS])

            dve.wait_ge(sem("places"), 1)
            for m in range(NM):
                stt(place_v[:, m, 0:E], bank[2][:, m * E:(m + 1) * E], FAR, chosen_v[:, m], ALU.add, ALU.mult)\
                    .then_inc(sem("placed"), 1)
            for m in range(NM):
                dve.wait_ge(sem("placed"), m + 1)
                ins = tt(onehot[:, m], iota_b, spread(place_v[:, m, 0:2]), ALU.is_equal)
            ins.then_inc(sem("onehot_ready"), 1)
            for m in range(NM):
                dve.wait_ge(sem("router_exped"), m + 1)
                link(tt(expd_v[:, m], expd_v[:, m], chosen_v[:, m], ALU.mult))
                link(dve.tensor_reduce(gsum[:, m:m + 1], expd_v[:, m], AX.X, ALU.add))
                link(dve.reciprocal(grec[:, m:m + 1], gsum[:, m:m + 1]))
                ts(weight_v[:, m, 0:E], expd_v[:, m], grec[:, m:m + 1], None, ALU.mult).then_inc(sem("weights_ready"), 1)

            def onehots(j):
                for m in range(NM):
                    ins = tt(onehot[:, m], iota_b, spread(place_v[:, m, bass.ds(2 * j, 2)]), ALU.is_equal)
                return ins

            def picks(j):
                return dve.tensor_copy(pick, spread(eye32[:, bass.ds(2 * j, 2)], E))

            def pair(j, first=False):
                dve.wait_ge(sem("onehot_ready"), j + 1)
                if first:
                    dve.wait_ge(sem("weights_ready"), NM)
                else:
                    dve.wait_ge(sem("gated_turned"), j)
                for m in range(NM):
                    ins = tt(gated[:, m], onehot[:, m], spread(weight_v[:, m, bass.ds(2 * j, 2)]), ALU.mult)
                ins.then_inc(sem("gated_ready"), 1)
                dve.wait_ge(sem("gathered"), 2 * j + 2)
                dve.wait_ge(sem("gated_ready"), j + 1)
                onehots(j + 1).then_inc(sem("onehot_ready"), 1)
                for f in range(2):
                    dve.wait_ge(ring_used, JOB_CHUNKS * j + NHEAD + KD * (f + 1))
                    if not first:
                        dve.wait_ge(sem(f"act_turned{f}"), j)
                    ts(glu[:, f], bank[2 * f][:], LIMIT, None, ALU.min).then_inc(sem(f"glu_ready{f}"), 1)
                    ts(lin[:, f], bank[2 * f + 1][:], LIMIT, -LIMIT, ALU.min, ALU.max).then_inc(sem(f"lin_ready{f}"), 1)
                    dve.wait_ge(sem(f"glu_ready{f}"), j + 1)
                    dve.wait_ge(sem(f"lin_ready{f}"), 2 * j + 1)
                    stt(lin[:, f], lin[:, f], 1.0, glu[:, f], ALU.add, ALU.mult).then_inc(sem(f"lin_ready{f}"), 1)
                    dve.wait_ge(sem(f"lin_ready{f}"), 2 * j + 2)
                    dve.wait_ge(sem(f"sig_ready{f}"), j + 1)
                    tt(act_out[:, f], lin[:, f], sig[:, f], ALU.mult).then_inc(sem(f"act_ready{f}"), 1)
                picks(j + 1).then_inc(sem("pick_ready"), 1)
                if first:
                    dve.wait_ge(sem("counts"), 1)
                    link(dve.tensor_reduce(fullest[:, 0:1], bank[3][:, 0:E], AX.X, ALU.max))
                    dve.tensor_copy(fullest_i[:], fullest[:, 0:1]).then_inc(sem("counted"), 1)
                dve.wait_ge(ring_used, JOB_CHUNKS * j + NHEAD + JOB_CHUNKS)
                dve.tensor_copy(y_sb[:, HALF:], bank[5][:]).then_inc(sem("y_copied1"), 1)
                for i in range(2 * NM):
                    h, m = i // 2, i % 2
                    dve.wait_ge(sem("scattered"), 4 * j + i + 1)
                    a = acc[:, m, h * HALF:(h + 1) * HALF]
                    tt(a, bank[i][:], a, ALU.add).then_inc(sem("acc_added"), 1)

            pair(0, first=True)
            dve.memset(place_v[:, :, ROUNDS * E:], 0.0).then_inc(sem("place_pad"), 1)
            for m in range(NM):
                for r in range(1, ROUNDS):
                    ts(place_v[:, m, r * E:(r + 1) * E], place_v[:, m, 0:E], -float(SLOTS * r), None, ALU.add)\
                        .then_inc(sem("placed"), 1)
                    dve.tensor_copy(weight_v[:, m, r * E:(r + 1) * E], weight_v[:, m, 0:E]).then_inc(sem("placed"), 1)
            dve.wait_ge(sem("placed"), NM + 2 * NM * (ROUNDS - 1))
            dve.wait_ge(sem("place_pad"), 1)
            with dve.Fori(1, PAIRS) as j:
                pair(j)
            dve.wait_ge(sem("acc_added"), 4 * PAIRS)
            most = dve.value_load(fullest_i[0:1, 0:1], min_val=0, max_val=SEQ)
            with dve.Fori(1, ROUNDS) as r:
                with dve.If(most > r * SLOTS):
                    dve.wait_ge(sem("stored"), 16 * 2 * NM + 16 * NM * (r - 1))
                    dve.sem_inc(sem("rounds_begun"), 1)
                    with dve.Fori(0, PAIRS) as p_:
                        pair(r * PAIRS + p_)
                    dve.wait_ge(sem("acc_added"), 4 * PAIRS * (r + 1))
                    dve.sem_inc(sem("rounds_added"), 1)


TABLES = 5
SMALL = 12


def rope_tables():
    cols = []
    for dim in (ROPE_A, DD):
        inv = (1.0 / (np.float32(10000.0) ** (np.arange(0, dim, 2, dtype=np.float32) / np.float32(dim)))).astype(np.float32)
        ang = np.arange(SEQ, dtype=np.float32)[:, None] * inv[None, :]
        cols += [np.cos(ang).astype(np.float32), np.sin(ang).astype(np.float32)]
    tabs = np.concatenate(cols, axis=1)
    return np.ascontiguousarray(tabs.reshape(NM, P, -1).transpose(1, 0, 2).reshape(P, -1))


_INS = ['x', 'attn_norm', 'w_in', 'mla_q_lat_norm', 'mla_kv_lat_norm', 'mla_w_uq', 'mla_w_ukv', 'mla_q_norm',
        'mla_k_norm', 'diff_q_norm', 'diff_k_norm', 'diff_lambda_q1', 'diff_lambda_k1', 'diff_lambda_q2',
        'diff_lambda_k2', 'diff_subln', 'w_branch_mla', 'w_branch_diff', 'w_out', 'ffn_norm', 'w_router',
        'b_router', 'w_mlp1', 'b_mlp1', 'w_mlp2', 'b_mlp2']


def kernel(**inputs):
    import concourse.bacc as _bacc
    from concourse.bass_utils import run_bass_kernel_spmd as _run

    nc = _bacc.Bacc("TRN2", target_bir_lowering=False, num_devices=1, dynamic_dma_scratch_size=1024)
    arrays, args = {}, []
    for name in _INS + ["rope"]:
        a = rope_tables() if name == "rope" else np.ascontiguousarray(inputs[name])[0]
        arrays[f"in_{name}"] = a
        args.append(nc.dram_tensor(f"in_{name}", a.shape, F32, kind="ExternalInput").ap())
    out = nc.dram_tensor("out_h", [SEQ, D], F32, kind="ExternalOutput").ap()
    build(nc, *args, out)
    r = _run(nc, [arrays], core_ids=[0])
    return r.results[0]["out_h"].reshape(1, SEQ, D)
```
